# Optimizing a Trainium2 kernel written in Bass

```python
import math
import jax, jax.numpy as jnp
from jax import lax
import numpy as np

D_MODEL = 2048
BATCH = 1
SEQ = 256
DEPTH = 1

MEM_LEN = 256
A_HEADS = 6
A_HEAD_DIM = 128
A_KV_RANK = 256
IDX_HEADS = 16
IDX_DIM = 64
TOPK_MAX = 256
Q_BLOCK = 128
B_HEADS = 12
B_KV_HEADS = 2
B_HEAD_DIM = 64
WINDOW = 128
BAND_BLOCK = 128
C_HEADS = 4
C_HEAD_DIM = 128
NUM_BUCKETS = 32
MAX_DISTANCE = 128
EPS = 1e-6

A_WIDTH = A_HEADS * A_HEAD_DIM
B_WIDTH = B_HEADS * B_HEAD_DIM
B_KV_WIDTH = B_KV_HEADS * B_HEAD_DIM
C_WIDTH = C_HEADS * C_HEAD_DIM
N_BRANCH = 3
IN_SIZES = (A_WIDTH, A_KV_RANK, IDX_HEADS * IDX_DIM, IDX_DIM, IDX_HEADS, A_WIDTH,
            B_WIDTH, B_KV_WIDTH, B_KV_WIDTH, B_WIDTH,
            C_WIDTH, C_WIDTH,
            N_BRANCH * D_MODEL)
IN_COLS = sum(IN_SIZES)


def rmsnorm(x, g):
    xf = x.astype(jnp.float32)
    y = xf * lax.rsqrt(jnp.mean(xf * xf, axis=-1, keepdims=True) + EPS)
    return (y * g.astype(jnp.float32)).astype(x.dtype)

def layernorm(x, g, b):
    xf = x.astype(jnp.float32)
    mu = jnp.mean(xf, axis=-1, keepdims=True)
    var = jnp.mean(jnp.square(xf - mu), axis=-1, keepdims=True)
    y = (xf - mu) * lax.rsqrt(var + EPS)
    return (y * g.astype(jnp.float32) + b.astype(jnp.float32)).astype(x.dtype)

def split_cols(y, sizes):
    cuts = np.cumsum(np.array(sizes))[:-1].tolist()
    return jnp.split(y, cuts, axis=-1)

def t5_bucket(dist):
    n = jnp.maximum(dist, 0)
    max_exact = NUM_BUCKETS // 2
    nf = jnp.maximum(n, 1).astype(jnp.float32)
    large = max_exact + (jnp.log(nf / max_exact) / math.log(MAX_DISTANCE / max_exact)
                         * (NUM_BUCKETS - max_exact)).astype(jnp.int32)
    large = jnp.minimum(large, NUM_BUCKETS - 1)
    return jnp.where(n < max_exact, n, large)

def dsa_attention(q, k, v, iq, ik, iw, bias_tab, topk):
    bsz, seq, nh, dh = q.shape
    nb = seq // Q_BLOCK
    key_pos = jnp.arange(seq, dtype=jnp.int32)

    def to_blocks(t):
        return jnp.moveaxis(t.reshape((bsz, nb, Q_BLOCK) + t.shape[2:]), 1, 0)

    def block_fn(args):
        qb, iqb, iwb, t0 = args
        tpos = t0 + jnp.arange(Q_BLOCK, dtype=jnp.int32)
        rel = jax.nn.relu(jnp.einsum('bthd,bsd->bths', iqb, ik))
        score = jnp.einsum('bths,bth->bts', rel, iwb).astype(jnp.float32)
        causal = key_pos[None, :] <= tpos[:, None]
        score = jnp.where(causal[None], score, -jnp.inf)
        _, idx = lax.top_k(score, topk)
        kg = jax.vmap(lambda kk, ii: kk[ii])(k, idx)
        vg = jax.vmap(lambda vv, ii: vv[ii])(v, idx)
        logits = jnp.einsum('bthd,btkhd->bthk', qb, kg).astype(jnp.float32) * (dh ** -0.5)
        dist = tpos[None, :, None] - idx
        bias = jnp.transpose(bias_tab[t5_bucket(dist)], (0, 1, 3, 2)).astype(jnp.float32)
        logits = jnp.where((dist >= 0)[:, :, None, :], logits + bias, -jnp.inf)
        p = jax.nn.softmax(logits, axis=-1).astype(vg.dtype)
        return jnp.einsum('bthk,btkhd->bthd', p, vg)

    t0s = jnp.arange(nb, dtype=jnp.int32) * Q_BLOCK
    out = lax.map(block_fn, (to_blocks(q), to_blocks(iq), to_blocks(iw), t0s))
    return jnp.moveaxis(out, 0, 1).reshape(bsz, seq, nh * dh)

def sliding_window_attention(q, k, v, sinks, bias_tab):
    bsz, seq, hq, dh = q.shape
    hkv = k.shape[2]
    g = hq // hkv
    blk = BAND_BLOCK
    nb = seq // blk
    qb = q.reshape(bsz, nb, blk, hkv, g, dh)

    def band(t):
        tb = t.reshape(bsz, nb, blk, hkv, dh)
        prev = jnp.concatenate([jnp.zeros_like(tb[:, :1]), tb[:, :-1]], axis=1)
        return jnp.concatenate([prev, tb], axis=2)

    kband, vband = band(k), band(v)
    logits = jnp.einsum('bnqhgd,bnkhd->bnhgqk', qb, kband).astype(jnp.float32) * (dh ** -0.5)
    qi = jnp.arange(blk, dtype=jnp.int32)[:, None]
    kj = jnp.arange(2 * blk, dtype=jnp.int32)[None, :]
    dist = blk + qi - kj
    bias = jnp.transpose(bias_tab[t5_bucket(dist)], (2, 0, 1)).reshape(hkv, g, blk, 2 * blk)
    key_pos = jnp.arange(nb, dtype=jnp.int32)[:, None, None] * blk + kj[None] - blk
    valid = (dist >= 0) & (dist < WINDOW) & (key_pos >= 0)
    logits = jnp.where(valid[None, :, None, None], logits + bias.astype(jnp.float32), -jnp.inf)
    sink = jnp.broadcast_to(sinks.astype(jnp.float32).reshape(hkv, g, 1, 1), logits.shape[:-1] + (1,))
    p = jax.nn.softmax(jnp.concatenate([logits, sink], axis=-1), axis=-1)[..., :-1]
    out = jnp.einsum('bnhgqk,bnkhd->bnqhgd', p.astype(v.dtype), vband)
    return out.reshape(bsz, seq, hq * dh)

def memory_attention(q, k, v):
    bsz, seq, nh, dh = q.shape
    logits = jnp.einsum('bthd,bmhd->bhtm', q, k).astype(jnp.float32) * (dh ** -0.5)
    p = jax.nn.softmax(logits, axis=-1).astype(v.dtype)
    return jnp.einsum('bhtm,bmhd->bthd', p, v).reshape(bsz, seq, nh * dh)

def first_inputs(seed: int = 0) -> dict:
    key = jax.random.key(seed)
    ks = jax.random.split(key, 24)
    f32 = jnp.float32

    def w(k, shape, fan_in):
        return jax.random.normal(k, shape, f32) * (fan_in ** -0.5)

    def gain(k, shape):
        return 1.0 + 0.05 * jax.random.normal(k, shape, f32)

    return {
        "x": jax.random.normal(ks[0], (BATCH, SEQ, D_MODEL), f32),
        "mem": jax.random.normal(ks[1], (BATCH, MEM_LEN, D_MODEL), f32),
        "norm_g": gain(ks[2], (DEPTH, D_MODEL)),
        "w_in": w(ks[3], (DEPTH, D_MODEL, IN_COLS), D_MODEL),
        "kv_norm_g": gain(ks[4], (DEPTH, A_KV_RANK)),
        "w_kv_up": w(ks[5], (DEPTH, A_KV_RANK, 2 * A_WIDTH), A_KV_RANK),
        "idx_k_ln_g": gain(ks[6], (DEPTH, IDX_DIM)),
        "idx_k_ln_b": 0.02 * jax.random.normal(ks[7], (DEPTH, IDX_DIM), f32),
        "q_norm_a": gain(ks[8], (DEPTH, A_HEAD_DIM)),
        "k_norm_a": gain(ks[9], (DEPTH, A_HEAD_DIM)),
        "q_norm_b": gain(ks[10], (DEPTH, B_HEAD_DIM)),
        "k_norm_b": gain(ks[11], (DEPTH, B_HEAD_DIM)),
        "sinks_b": 0.5 * jax.random.normal(ks[12], (DEPTH, B_HEADS), f32),
        "mem_norm_g": gain(ks[13], (DEPTH, D_MODEL)),
        "w_mem_kv": w(ks[14], (DEPTH, D_MODEL, 2 * C_WIDTH), D_MODEL),
        "q_norm_c": gain(ks[15], (DEPTH, C_HEAD_DIM)),
        "k_norm_c": gain(ks[16], (DEPTH, C_HEAD_DIM)),
        "w_up_a": w(ks[17], (DEPTH, A_WIDTH, D_MODEL), A_WIDTH),
        "w_up_b": w(ks[18], (DEPTH, B_WIDTH, D_MODEL), B_WIDTH),
        "w_up_c": w(ks[19], (DEPTH, C_WIDTH, D_MODEL), C_WIDTH),
        "gate_bias": 0.02 * jax.random.normal(ks[20], (DEPTH, N_BRANCH * D_MODEL), f32),
        "w_o": w(ks[21], (DEPTH, D_MODEL, D_MODEL), D_MODEL),
        "rel_bias": 0.5 * jax.random.normal(ks[22], (NUM_BUCKETS, A_HEADS + B_HEADS), f32),
    }

def first_block(x, mem, norm_g, w_in, kv_norm_g, w_kv_up, idx_k_ln_g, idx_k_ln_b,
              q_norm_a, k_norm_a, q_norm_b, k_norm_b, sinks_b, mem_norm_g, w_mem_kv,
              q_norm_c, k_norm_c, w_up_a, w_up_b, w_up_c, gate_bias, w_o, rel_bias):
    bsz, seq, _ = x.shape
    mlen = mem.shape[1]
    topk = min(TOPK_MAX, seq // 4)
    bias_a = rel_bias[:, :A_HEADS]
    bias_b = rel_bias[:, A_HEADS:]
    for l in range(DEPTH):
        h = rmsnorm(x, norm_g[l])
        (a_q, a_ckv, i_q, i_k, i_w, a_gate,
         b_q, b_k, b_v, b_gate,
         c_q, c_gate, mix_gate) = split_cols(h @ w_in[l], IN_SIZES)

        ckv = rmsnorm(a_ckv, kv_norm_g[l])
        a_k, a_v = jnp.split(ckv @ w_kv_up[l], 2, axis=-1)
        qa = rmsnorm(a_q.reshape(bsz, seq, A_HEADS, A_HEAD_DIM), q_norm_a[l])
        ka = rmsnorm(a_k.reshape(bsz, seq, A_HEADS, A_HEAD_DIM), k_norm_a[l])
        va = a_v.reshape(bsz, seq, A_HEADS, A_HEAD_DIM)
        iq = i_q.reshape(bsz, seq, IDX_HEADS, IDX_DIM)
        ik = layernorm(i_k, idx_k_ln_g[l], idx_k_ln_b[l])
        iw = i_w * (IDX_HEADS ** -0.5) * (IDX_DIM ** -0.5)
        oa = dsa_attention(qa, ka, va, iq, ik, iw, bias_a, topk) * jax.nn.silu(a_gate)

        qb = rmsnorm(b_q.reshape(bsz, seq, B_HEADS, B_HEAD_DIM), q_norm_b[l])
        kb = rmsnorm(b_k.reshape(bsz, seq, B_KV_HEADS, B_HEAD_DIM), k_norm_b[l])
        vb = b_v.reshape(bsz, seq, B_KV_HEADS, B_HEAD_DIM)
        ob = sliding_window_attention(qb, kb, vb, sinks_b[l], bias_b) * jax.nn.silu(b_gate)

        m_k, m_v = jnp.split(rmsnorm(mem, mem_norm_g[l]) @ w_mem_kv[l], 2, axis=-1)
        qc = rmsnorm(c_q.reshape(bsz, seq, C_HEADS, C_HEAD_DIM), q_norm_c[l])
        kc = rmsnorm(m_k.reshape(bsz, mlen, C_HEADS, C_HEAD_DIM), k_norm_c[l])
        vc = m_v.reshape(bsz, mlen, C_HEADS, C_HEAD_DIM)
        oc = memory_attention(qc, kc, vc) * jax.nn.silu(c_gate)

        g_a, g_b, g_c = jnp.split(jax.nn.sigmoid(mix_gate + gate_bias[l]), N_BRANCH, axis=-1)
        merged = g_a * (oa @ w_up_a[l]) + g_b * (ob @ w_up_b[l]) + g_c * (oc @ w_up_c[l])
        x = x + merged @ w_o[l]
    return x


N_META = 16
POOL_WIDTH = D_MODEL // 2
POOL_WINDOWS = (2, 4, 8, 16)
N_POOL_GROUPS = len(POOL_WINDOWS)
POOL_GROUP_DIM = POOL_WIDTH // N_POOL_GROUPS
CONV_WIDTH = D_MODEL // 2
CONV_KERNEL = 31
D_FF = 4 * D_MODEL
IN_COLS_2 = POOL_WIDTH + 2 * CONV_WIDTH + 2 * D_MODEL
RMS_EPS = 1e-6
LN_EPS = 1e-5


def rms_norm(x, g):
    xf = x.astype(jnp.float32)
    y = xf * lax.rsqrt(jnp.mean(xf * xf, axis=-1, keepdims=True) + RMS_EPS)
    return (y * g.astype(jnp.float32)).astype(x.dtype)

def layer_norm(x, g, b):
    xf = x.astype(jnp.float32)
    mu = jnp.mean(xf, axis=-1, keepdims=True)
    var = jnp.mean(jnp.square(xf - mu), axis=-1, keepdims=True)
    y = (xf - mu) * lax.rsqrt(var + LN_EPS)
    return (y * g.astype(jnp.float32) + b.astype(jnp.float32)).astype(x.dtype)

def causal_multiscale_pool(z, w_grp, scale):
    B, L, _ = z.shape
    zf = z.astype(jnp.float32).reshape(B, L, N_POOL_GROUPS, POOL_GROUP_DIM)
    cs = jnp.cumsum(zf, axis=1)
    pos = jnp.arange(L)
    means = []
    for g, w in enumerate(POOL_WINDOWS):
        csg = cs[:, :, g]
        lag = jnp.pad(csg[:, : L - w], ((0, 0), (w, 0), (0, 0)))
        cnt = jnp.minimum(pos + 1, w).astype(jnp.float32)[None, :, None]
        means.append((csg - lag) / cnt)
    pooled = jnp.stack(means, axis=2)
    d = (pooled - zf).astype(z.dtype)
    y = jnp.einsum('blgc,gcd->blgd', d, w_grp).reshape(B, L, POOL_WIDTH)
    return y * scale

def conformer_conv(v, gate, w_dw, b_dw, ln_g, ln_b):
    a = v * jax.nn.sigmoid(gate)
    c = lax.conv_general_dilated(
        a, w_dw[:, None, :], window_strides=(1,),
        padding=[(CONV_KERNEL - 1, 0)],
        dimension_numbers=('NWC', 'WIO', 'NWC'),
        feature_group_count=CONV_WIDTH) + b_dw
    return jax.nn.silu(layer_norm(c, ln_g, ln_b))

def second_inputs(seed: int = 0) -> dict:
    key = jax.random.key(seed)
    ks = jax.random.split(key, 24)
    f32 = jnp.float32
    n = lambda k, shape, s: jax.random.normal(k, shape, f32) * s
    gain = lambda k, shape: 1.0 + 0.05 * jax.random.normal(k, shape, f32)
    return {
        "x": jax.random.normal(ks[0], (BATCH, SEQ, D_MODEL), f32),
        "meta": n(ks[1], (N_META, D_MODEL), 1.0),
        "g_pre_mix": gain(ks[2], (DEPTH, D_MODEL)),
        "w_in": n(ks[3], (DEPTH, D_MODEL, IN_COLS_2), D_MODEL ** -0.5),
        "w_pool_grp": n(ks[4], (DEPTH, N_POOL_GROUPS, POOL_GROUP_DIM, POOL_GROUP_DIM), POOL_GROUP_DIM ** -0.5),
        "pool_scale": gain(ks[5], (DEPTH, POOL_WIDTH)),
        "w_pool_out": n(ks[6], (DEPTH, POOL_WIDTH, D_MODEL), POOL_WIDTH ** -0.5),
        "w_dw": n(ks[7], (DEPTH, CONV_KERNEL, CONV_WIDTH), CONV_KERNEL ** -0.5),
        "b_dw": n(ks[8], (DEPTH, CONV_WIDTH), 0.02),
        "conv_ln_g": gain(ks[9], (DEPTH, CONV_WIDTH)),
        "conv_ln_b": n(ks[10], (DEPTH, CONV_WIDTH), 0.02),
        "w_conv_out": n(ks[11], (DEPTH, CONV_WIDTH, D_MODEL), CONV_WIDTH ** -0.5),
        "w_o": n(ks[12], (DEPTH, D_MODEL, D_MODEL), D_MODEL ** -0.5),
        "g_post_mix": gain(ks[13], (DEPTH, D_MODEL)),
        "g_pre_mlp": gain(ks[14], (DEPTH, D_MODEL)),
        "w_up": n(ks[15], (DEPTH, D_MODEL, D_FF), D_MODEL ** -0.5),
        "w_down": n(ks[16], (DEPTH, D_FF, D_MODEL), D_FF ** -0.5),
        "g_post_mlp": gain(ks[17], (DEPTH, D_MODEL)),
    }

def second_block(x, meta, g_pre_mix, w_in, w_pool_grp, pool_scale, w_pool_out,
              w_dw, b_dw, conv_ln_g, conv_ln_b, w_conv_out, w_o, g_post_mix,
              g_pre_mlp, w_up, w_down, g_post_mlp):
    B = x.shape[0]
    meta_b = jnp.broadcast_to(meta[None].astype(x.dtype), (B, N_META, D_MODEL))
    h = jnp.concatenate([meta_b, x], axis=1)
    splits = np.cumsum([POOL_WIDTH, CONV_WIDTH, CONV_WIDTH, D_MODEL]).tolist()
    for l in range(DEPTH):
        u = rms_norm(h, g_pre_mix[l])
        proj = u @ w_in[l]
        z_pool, v_conv, g_conv, gate_a, gate_b = jnp.split(proj, splits, axis=-1)
        y_a = causal_multiscale_pool(z_pool, w_pool_grp[l], pool_scale[l]) @ w_pool_out[l]
        y_b = conformer_conv(v_conv, g_conv, w_dw[l], b_dw[l],
                             conv_ln_g[l], conv_ln_b[l]) @ w_conv_out[l]
        m = jax.nn.sigmoid(gate_a) * y_a + jax.nn.sigmoid(gate_b) * y_b
        h = h + rms_norm(m @ w_o[l], g_post_mix[l])
        u = rms_norm(h, g_pre_mlp[l])
        f = jnp.square(jax.nn.relu(u @ w_up[l])) @ w_down[l]
        h = h + rms_norm(f, g_post_mlp[l])
    return h[:, N_META:]


def setup_inputs(seed=0):
    out = dict(first_inputs(seed))
    for name, value in second_inputs(seed + 1).items():
        if name != "x":
            out[name + "_2"] = value
    return out


def reference(
    x, mem, norm_g, w_in, kv_norm_g, w_kv_up, idx_k_ln_g, idx_k_ln_b, q_norm_a, k_norm_a,
    q_norm_b, k_norm_b, sinks_b, mem_norm_g, w_mem_kv, q_norm_c, k_norm_c, w_up_a, w_up_b,
    w_up_c, gate_bias, w_o, rel_bias, meta_2, g_pre_mix_2, w_in_2, w_pool_grp_2, pool_scale_2,
    w_pool_out_2, w_dw_2, b_dw_2, conv_ln_g_2, conv_ln_b_2, w_conv_out_2, w_o_2, g_post_mix_2,
    g_pre_mlp_2, w_up_2, w_down_2, g_post_mlp_2,
):
    x = first_block(
        x, mem, norm_g, w_in, kv_norm_g, w_kv_up, idx_k_ln_g, idx_k_ln_b, q_norm_a, k_norm_a,
        q_norm_b, k_norm_b, sinks_b, mem_norm_g, w_mem_kv, q_norm_c, k_norm_c, w_up_a, w_up_b,
        w_up_c, gate_bias, w_o, rel_bias,
    )
    return second_block(
        x, meta_2, g_pre_mix_2, w_in_2, w_pool_grp_2, pool_scale_2, w_pool_out_2, w_dw_2,
        b_dw_2, conv_ln_g_2, conv_ln_b_2, w_conv_out_2, w_o_2, g_post_mix_2, g_pre_mlp_2,
        w_up_2, w_down_2, g_post_mlp_2,
    )


_drawn_inputs = setup_inputs


def setup_inputs(seed=0):
    import zlib

    import numpy as np

    out = dict(_drawn_inputs(seed))
    spreads = {}
    factors = {'norm_g': 2.907,
     'kv_norm_g': 8.0,
     'idx_k_ln_g': 4.277,
     'idx_k_ln_b': 7.786,
     'q_norm_a': 8.0,
     'k_norm_a': 8.0,
     'q_norm_b': 8.0,
     'k_norm_b': 8.0,
     'sinks_b': 200.0,
     'mem_norm_g': 8.0,
     'q_norm_c': 8.0,
     'k_norm_c': 8.0,
     'gate_bias': 8.0,
     'b_dw_2': 200.0,
     'conv_ln_b_2': 200.0,
     'meta_2': 6.211,
     'g_pre_mix_2': 8.0,
     'pool_scale_2': 8.0,
     'conv_ln_g_2': 64.0,
     'g_post_mix_2': 8.0,
     'g_pre_mlp_2': 8.0,
     'g_post_mlp_2': 8.0}
    for name, (base, spread) in spreads.items():
        noise = np.random.default_rng([zlib.crc32(name.encode()), seed]).standard_normal(out[name].shape)
        drawn = base * np.exp(spread * noise) if base else spread * noise
        out[name] = __import__('jax').numpy.asarray(drawn.astype(out[name].dtype))
    for name, factor in factors.items():
        out[name] = (out[name] * factor).astype(out[name].dtype)
    return out
```

```python
import math
from contextlib import ExitStack

import numpy as np
import concourse.bass as bass
from concourse import mybir

F32 = mybir.dt.float32
F32R = mybir.dt.float32r
ALU = mybir.AluOpType
ACT = mybir.ActivationFunctionType
AX = mybir.AxisListType.X

P = 128
D = 2048
KT = D // P
T = 256
META = 16
TM = T + META
A_HEADS, B_HEADS, C_HEADS = 6, 12, 4
IDX_HEADS, IDX_DIM, B_DIM = 16, 64, 64
TOPK = min(256, T // 4)
WINDOW = 128
BUCKETS, MAX_DISTANCE = 32, 128
KV_RANK = 256
A_W, B_W, C_W = 768, 768, 512
POOL_W = CONV_W = 1024
TAPS = 31
D_FF = 4 * D
EPS, LN_EPS = 1e-6, 1e-5
NEG = -1.0e30
TAKEN = -3.0e38

GROUP = 256
SLAB = 8
STAGES = 4
PAIRS = 2

A_CKV, I_Q, I_K = 768, 1024, 2048
A_GATE = 2128
MIX = 5712
E_AQ, E_CKV, E_IQ = 0, 6, 8
L_AGATE, L_BQ, L_BK, L_BV, L_BGATE, L_CQ, L_CGATE = 0, 6, 12, 13, 14, 20, 24

ROWS0 = [("gate_bias", 48), ("norm_g", 16), ("mem_norm_g", 16), ("g_pre_mix_2", 16), ("g_post_mix_2", 16), ("g_pre_mlp_2", 16)]
ROWS1 = [("g_post_mlp_2", 16), ("pool_scale_2", 8), ("b_dw_2", 8), ("conv_ln_g_2", 8), ("conv_ln_b_2", 8), ("kv_norm_g", 2),
         ("q_norm_a", 1), ("k_norm_a", 1), ("q_norm_c", 1), ("k_norm_c", 1)]
HALF_ROWS = ["q_norm_b", "k_norm_b", "idx_k_ln_g", "idx_k_ln_b"]
DW_ROWS = TAPS * (CONV_W // P)
COL, _at = {}, 0
for _name, _n in ROWS0 + ROWS1 + [(n, 1) for n in HALF_ROWS] + [("w_dw_2", DW_ROWS)]:
    COL[_name] = _at
    _at += _n
N0 = sum(n for _, n in ROWS0)
N1 = sum(n for _, n in ROWS1) + len(HALF_ROWS)
PARAM_GROUPS = [(0, N0), (N0, N1), (N0 + N1, DW_ROWS // 2), (N0 + N1 + DW_ROWS // 2, DW_ROWS // 2)]
PARAMS = _at

KB = 1024


def bucket_starts():
    n = np.arange(T, dtype=np.int32)
    exact = BUCKETS // 2
    nf = np.maximum(n, 1).astype(np.float32)
    large = exact + (np.log(nf / np.float32(exact)) / np.float32(math.log(MAX_DISTANCE / exact))
                     * np.float32(BUCKETS - exact)).astype(np.int32)
    b = np.where(n < exact, n, np.minimum(large, BUCKETS - 1))
    return [int(np.argmax(b == k)) for k in range(BUCKETS)] + [T]


class Chain:

    def __init__(self, eng, sem):
        self.eng, self.sem, self.n, self.term = eng, sem, 0, 0

    def __call__(self, ins):
        ins.then_inc(self.sem, 1)
        self.n += 1
        self.eng.wait_ge(self.sem, self.n + self.term)


def repeat(eng, count, unroll, body, chain=None, links=0):
    whole = count // unroll
    start = 0
    if whole >= 2:
        n0 = chain.n if chain else 0
        with eng.Fori(0, whole) as i:
            if chain:
                chain.term = i * links
            for u in range(unroll):
                body(i, u)
        if chain:
            assert chain.n - n0 == links, (chain.n - n0, links)
            chain.n, chain.term = n0 + whole * links, 0
        start = whole * unroll
    for s in range(start, count):
        body(s // unroll, s % unroll)


class Part:

    def __init__(self, w, col0, slabs, rhs, wide=False, cols=GROUP, stride=GROUP, row0=0):
        self.w, self.col0, self.slabs, self.rhs, self.wide, self.cols, self.stride, self.row0 = w, col0, slabs, rhs, wide, cols, stride, row0


class Job:

    def __init__(self, steps, parts, unroll, start_wait=None):
        self.steps, self.parts, self.unroll, self.start_wait = steps, parts, unroll, start_wait
        self.pieces = [(p, pn, sum(p.slabs[:q]), kt, q == len(p.slabs) - 1) for pn, p in enumerate(parts) for q, kt in enumerate(p.slabs)]
        self.S = len(self.pieces)

    def place(self, slab0, group0):
        self.slab0, self.group0 = slab0, group0
        return slab0 + self.steps * self.S, group0 + self.steps * len(self.parts)

    def slab(self, i, u, idx):
        n = self.slab0 + u * self.S + idx
        return n + i * (self.unroll * self.S), n

    def group(self, i, u, part):
        g = self.group0 + u * len(self.parts) + part
        last = self.slab0 + u * self.S + sum(len(p.slabs) for p in self.parts[:part + 1]) - 1
        return g + i * (self.unroll * len(self.parts)), g % 2, last + i * (self.unroll * self.S)


def build(nc, A, out):
    ctx = ExitStack()
    with ctx:
        ctx.enter_context(nc.sbuf_tensor("arena", [P, 53200], F32))
        BASE = 16512

        def at(name, kb, shape, dt=F32):
            return nc.alloc_sbuf_tensor_at(name, shape, dt, offset=BASE + int(kb * KB))

        def sem(name):
            return ctx.enter_context(nc.semaphore(name))

        stage = at("stage", 0, [P, STAGES, SLAB, GROUP])
        w_high = at("w_high", 32, [P, PAIRS, SLAB, GROUP], F32R)
        w_low = at("w_low", 48, [P, PAIRS, SLAB, GROUP], F32R)
        params = at("params", 64, [P, PARAMS])
        ident = at("ident", 66, [P, P])
        ones = at("ones", 66.5, [P, P])
        blocks = at("blocks", 67, [P, P])
        center = at("center", 67.5, [IDX_DIM, P])
        square = at("square", 68, [P, 2, 2 * TM])
        sumsq = at("sumsq", 72.25, [P, 2, TM])
        rstd = at("rstd", 74.5, [P, 2 * T])
        tmp = at("tmp", 76.5, [P, 2, 2 * TM])
        gate = at("gate", 80.75, [P, 2, 2 * TM])
        Z = 85
        hT = at("hT", Z, [P, KT, 2, T], F32R)
        late = at("late", Z + 32, [P, 28, T])
        mem_pair = at("mem_pair", Z + 32, [P, KT, 2, T], F32R)
        mkv = at("mkv", Z + 114, [P, 8, T])
        mem_in = at("mem_in", Z + 64, [P, 2, D])
        x_in = at("x_in", Z + 80, [P, 2, D])
        turned = at("turned", Z + 96, [P, KT, T])
        toep = at("toep", Z + 60, [P, A_HEADS + B_HEADS, T])
        early = at("early", Z + 78, [P, 16, T])
        flip = at("flip", Z + 113, [P, P])
        ikw = at("ikw", Z + 94, [P, T])
        akv = at("akv", Z + 95, [P, 12, T])
        ckv_pair = at("ckv_pair", Z + 107, [P, 2, 2, T], F32R)
        v_a = at("v_a", Z + 86, [P, 2, A_W])
        v_b = at("v_b", Z + 94, [P, 2, P])
        v_c = at("v_c", Z + 107, [P, 2, C_W])
        ptb = at("ptb", 76.5, [P, 2, 2 * T])
        lg = at("lg", 80.75, [P, 2, 2 * T])
        score = at("score", Z + 111, [P, 3 * P])
        work = at("work", Z + 112.5, [P, 3 * P])
        ikn = at("ikn", 72.25, [P, T])
        bk_swap = at("bk_swap", 73.25, [P, T])
        small = at("small", 65.71875, [P, 72])
        merged = at("merged", Z + 64, [P, KT, T])
        o_pair = at("o_pair", Z + 94, [P, 6, 2, T], F32R)
        merged_pair = at("merged_pair", Z + 32, [P, KT, 2, T], F32R)
        xT = at("xT", Z + 106, [P, KT, T])
        h1 = at("h1", Z, [P, KT, TM])
        uT = at("uT", Z + 17, [P, KT, 2, TM], F32R)
        m = at("m", Z + 52, [P, KT, T])
        d_pair = at("d_pair", Z + 68, [P, 8, 2, T], F32R)
        conv_pair = at("conv_pair", Z + 68, [P, 8, 2, T], F32R)
        z_pool = at("z_pool", Z + 84, [P, 8, TM])
        conv = at("conv", Z + 84, [P, 8, T])
        glu = at("glu", Z + 92.5, [P, 8, TAPS - 1 - META + TM])
        y_pair = at("y_pair", Z + 102, [P, 8, 2, T], F32R)
        window = at("window", Z + 118, [P, 2, 2 * TM])
        m_pair = at("m_pair", Z + 84, [P, KT, 2, T], F32R)
        mixed = at("mixed", Z + 52, [P, KT, T])
        u2 = at("u2", Z + 17, [P, KT, 2, T], F32R)
        f_pair = at("f_pair", Z + 84, [P, KT, 2, T], F32R)
        y = at("y", Z + 52, [P, KT, T])
        rows_out = at("rows_out", Z + 68, [P, 2, D])
        prow = at("prow", Z, [P, 4, P])
        meta_in = at("meta_in", Z + 17, [META, D])
        relb = at("relb", Z + 2, [BUCKETS, A_HEADS + B_HEADS])
        relT = at("relT", Z + 2.5, [A_HEADS + B_HEADS, BUCKETS])
        brow = at("brow", Z + 3, [A_HEADS + B_HEADS, 2 * T])
        zrow = at("zrow", Z + 5, [A_HEADS + B_HEADS, 2 * T])

        acc = ctx.enter_context(nc.psum_tensor("acc", [P, 4, 512], F32))
        aux = ctx.enter_context(nc.psum_tensor("aux", [P, 4, 512], F32))
        spill_x = nc.dram_tensor("spill_x", [P, KT, T], F32, kind="Internal").ap()
        NB = A_HEADS + B_HEADS
        bias_dram = nc.dram_tensor("bias_rows", [NB, 2 * T], F32, kind="Internal")

        iw = small[:, 0:32].rearrange("p (t h) -> p t h", t=2)
        negmax = small[:, 32:36].rearrange("p (b t) -> p b t", b=2)
        denom = small[:, 36:40].rearrange("p (b t) -> p b t", b=2)
        top8 = small[:, 40:56].rearrange("p (t e) -> p t e", t=2)
        sinks = small[:, 56:68]
        esink = small[:, 68:72].rearrange("p (b t) -> p b t", b=2)

        landed = [sem(f"landed{s}") for s in range(STAGES)]
        issued, high_done, split_done, used, acc_free = sem("issued"), sem("high_done"), sem("split_done"), sem("used"), sem("acc_free")
        act_link, dve_link, pool_link = sem("act_link"), sem("dve_link"), sem("pool_link")
        S = {}

        def s(name):
            if name not in S:
                S[name] = sem(name)
            return S[name]

        starts = bucket_starts()

        A = {n: (v[0] if v.shape[0] == 1 else v) for n, v in A.items()}

        def flat(v):
            return v.rearrange("p a t -> p (a t)")

        def gain_of(name):
            return COL[name]
        HEAD_NORMS = [(flat(early[:, E_CKV:E_CKV + 2, :]), 2 * T, ones, 1.0 / KV_RANK, True, ("folded_heads", 1), gain_of("kv_norm_g"))]
        HEAD_NORMS += [(flat(early[:, E_AQ + r:E_AQ + r + 2, :]), 2 * T, ones, 1.0 / P, False, ("folded_heads", 1), gain_of("q_norm_a")) for r in (0, 2, 4)]
        IK_NORM = len(HEAD_NORMS)
        HEAD_NORMS += [(ikn[:], T, blocks, 1.0 / IDX_DIM, False, ("ik_copied", 1), gain_of("idx_k_ln_g"))]
        HEAD_NORMS += [(flat(akv[:, r:r + 2, :]), 2 * T, ones, 1.0 / P, False, ("folded_heads", 3), gain_of("k_norm_a")) for r in (0, 2, 4)]
        HEAD_NORMS += [(flat(late[:, L_BQ + r:L_BQ + r + 2, :]), 2 * T, blocks, 1.0 / B_DIM, False, ("folded_heads", 4), gain_of("q_norm_b")) for r in (0, 2, 4)]
        HEAD_NORMS += [(late[:, L_BK, :], T, blocks, 1.0 / B_DIM, False, ("folded_heads", 4), gain_of("k_norm_b"))]
        HEAD_NORMS += [(flat(late[:, L_CQ + r:L_CQ + r + 2, :]), 2 * T, ones, 1.0 / P, False, ("folded_heads", 4), gain_of("q_norm_c")) for r in (0, 2)]
        HEAD_NORMS += [(flat(mkv[:, r:r + 2, :]), 2 * T, ones, 1.0 / P, False, ("folded_heads", 4), gain_of("k_norm_c")) for r in (0, 2)]
        WIDTHS = [T, T, TM, T, T, T, T]

        def head_cols(h, t):
            if h < A_HEADS + B_HEADS:
                return (0, P) if t == 0 else (P, 3 * P)
            return t * T, (t + 1) * T

        full = [8, 8]
        split3 = [6, 5, 5]

        def rhs_of(pair):
            return lambda k: (pair[:, k, :, :], pair[:, k, 0, :])

        def u_tokens(k):
            return uT[:, k, :, META:TM], uT[:, k, 0, META:TM]

        jobs = {}
        order = [
            ("mem_kv", Job(4, [Part(A["w_mem_kv"], 0, full, rhs_of(mem_pair))], 2, ("pair_ready", 8))),
            ("early", Job(8, [Part(A["w_in"], 0, full, rhs_of(hT))], 2, ("pair_ready", 16))),
            ("ikw", Job(1, [Part(A["w_in"], I_K, full, rhs_of(hT), cols=P)], 2)),
            ("kv_up", Job(6, [Part(A["w_kv_up"], 0, [2], rhs_of(ckv_pair))], 4, ("ckv_ready", 1))),
            ("late", Job(14, [Part(A["w_in"], A_GATE, full, rhs_of(hT))], 2)),
        ]
        for b, (w, width) in enumerate((("w_up_a", A_W), ("w_up_b", B_W), ("w_up_c", C_W))):
            order.append((w, Job(8, [Part(A["w_in"], MIX + b * D, split3, rhs_of(hT)),
                                     Part(A[w], 0, [width // P], rhs_of(o_pair))], 1, ("o_pair_ready", b + 1))))
        order += [
            ("w_o", Job(8, [Part(A["w_o"], 0, full, rhs_of(merged_pair))], 2, ("merged_ready", 8))),
            ("branches", Job(12, [Part(A["w_in_2"], 0, full, lambda k: (uT[:, k, 0, :], uT[:, k, 1, :]), wide=True)], 2, ("pair_ready", 24))),
            ("pool_grp", Job(4, [Part(A["w_pool_grp_2"], 0, [2], rhs_of(d_pair), stride=0)], 4, ("d_ready", 1))),
            ("pool_out", Job(8, [Part(A["w_in_2"], POOL_W + 2 * CONV_W, split3, u_tokens),
                                 Part(A["w_pool_out_2"], 0, [8], rhs_of(y_pair))], 1, ("y_pair_ready", 4))),
            ("conv_out", Job(8, [Part(A["w_in_2"], POOL_W + 2 * CONV_W + D, split3, u_tokens),
                                 Part(A["w_conv_out_2"], 0, [8], rhs_of(conv_pair))], 1, ("conv_ready", 1))),
            ("w_o_2", Job(8, [Part(A["w_o_2"], 0, full, rhs_of(m_pair))], 2, ("m_ready", 8))),
        ]
        for q in range(4):
            order.append((f"w_up{q}", Job(8, [Part(A["w_up_2"], q * D, full, rhs_of(u2))], 2, ("pair_ready", 32))))
            order.append((f"w_down{q}", Job(8, [Part(A["w_down_2"], 0, full, rhs_of(f_pair), row0=q * KT)], 2, ("f_ready", 8 * q + 8))))
        slab0 = group0 = 0
        for name, job in order:
            slab0, group0 = job.place(slab0, group0)
            jobs[name] = job
        names = [name for name, _ in order]

        stream_of_slabs = [(job, step, idx) for _, job in order for step in range(job.steps) for idx in range(job.S)]

        def load_slab(sp, job, i, u, idx):
            step = i * job.unroll + u
            n, n_static = job.slab(i, u, idx)
            p, _, k, kt, _ = job.pieces[idx]
            slot = n_static % STAGES
            sp.wait_ge(split_done, n + 1)
            sp.sem_inc(issued, 1)
            rows = slice((p.row0 + k) * P, (p.row0 + k + kt) * P)
            src = p.w[rows, bass.ds(p.col0 + step * p.stride, p.cols)] if p.stride else p.w[step, :, :]
            sp.dma_start(stage[:, slot, 0:kt, 0:p.cols], src.rearrange("(k p) n -> p k n", p=P)).then_inc(landed[slot], 16)

        def round_high(act, job, i, u, idx):
            n, n_static = job.slab(i, u, idx)
            p, _, k, kt, _ = job.pieces[idx]
            slot, pr = n_static % STAGES, n_static % PAIRS
            act.wait_ge(landed[slot], 16 * (n_static // STAGES + 1) + i * (16 * (job.unroll * job.S // STAGES)))
            act.wait_ge(used, n + 1)
            act.activation(w_high[:, pr, 0:kt, 0:p.cols], stage[:, slot, 0:kt, 0:p.cols], ACT.Copy).then_inc(high_done, 1)

        def subtract_low(dve, job, i, u, idx):
            n, n_static = job.slab(i, u, idx)
            p, _, k, kt, _ = job.pieces[idx]
            slot, pr = n_static % STAGES, n_static % PAIRS
            dve.wait_ge(high_done, n + 1)
            dve.tensor_tensor(w_low[:, pr, 0:kt, 0:p.cols], stage[:, slot, 0:kt, 0:p.cols],
                              w_high[:, pr, 0:kt, 0:p.cols].bitcast(F32), ALU.subtract).then_inc(split_done, 1)

        def stream(eng, split, name, body=None, chain=None, links=0, peel=False):
            job = jobs[name]
            tail = -(-PAIRS // job.S)

            def step(i, u, known):
                for idx, (_, part, _, _, last) in enumerate(job.pieces):
                    ahead = u * job.S + idx + PAIRS
                    if known:
                        n = job.slab0 + i * job.unroll * job.S + ahead
                        if n < len(stream_of_slabs):
                            j2, s2, idx2 = stream_of_slabs[n]
                            split(eng, j2, s2 // j2.unroll, s2 % j2.unroll, idx2)
                    else:
                        split(eng, job, i, ahead // job.S, ahead % job.S)
                    if last and body:
                        body(i, u, part)

            count = job.steps - tail
            looped = 0 if peel or count // job.unroll < 2 else count // job.unroll * job.unroll
            if looped:
                repeat(eng, looped, job.unroll, lambda i, u: step(i, u, False), chain, links * job.unroll)
            for n in range(looped, job.steps):
                step(n // job.unroll, n % job.unroll, True)

        def multiply(pe, job, i, u):
            for idx, (p, part, k0, kt, last) in enumerate(job.pieces):
                n, n_static = job.slab(i, u, idx)
                if k0 == 0:
                    g, bank, _ = job.group(i, u, part)
                    pe.wait_ge(acc_free, g + 1)
                pr = n_static % PAIRS
                pe.wait_ge(split_done, STAGES + n + 1)
                for j in range(p.cols // P):
                    bk = acc[:, 2 * bank + j, :]
                    for k in range(kt):
                        first, final = k0 + k == 0, last and k == kt - 1
                        high, low = (w[:, pr, k, j * P:(j + 1) * P] for w in (w_high, w_low))
                        if p.wide:
                            a, b = p.rhs(k0 + k)
                            pe.matmul(bk[:, 0:TM], high, b, start=first, stop=False)
                            pe.matmul(bk[:, 0:TM], low, a, start=False, stop=False)
                            mm = pe.matmul(bk[:, 0:TM], high, a, start=False, stop=final)
                            continue
                        both, a = p.rhs(k0 + k if p.stride else 2 * u + k)
                        if first:
                            pe.matmul(bk, high, both, start=True, stop=False, skip_group_check=True)
                            pe.matmul(bk[:, 0:T], low, a, start=False, stop=False, skip_group_check=True)
                        else:
                            pe.matmul(bk[:, 0:T], low, a, start=False, stop=False, skip_group_check=True)
                            mm = pe.matmul(bk, high, both, start=False, stop=final, skip_group_check=True)
                mm.then_inc(used, 1)

        def group_done(eng, job, i, u, part=0):
            g, bank, last = job.group(i, u, part)
            eng.wait_ge(used, PAIRS + last + 1)
            return acc[:, 2 * bank:2 * bank + 2, :], g

        def fold(dve, dst, banks):
            return dve.tensor_reduce(dst, banks.rearrange("p j (h t) -> p j t h", h=2), AX, ALU.add)

        block = ctx.enter_context(nc.Block())

        @block.sync
        def _(sp):
            def rows(name):
                v = A[name]
                return v.rearrange("(a n) -> a n", n=P)
            at_row = 0
            for group, members in enumerate((ROWS0, ROWS1)):
                at_row = 0
                for name, n in members:
                    sp.dma_start(prow[at_row:at_row + n, group, :], rows(name)).then_inc(s("params_in"), 16)
                    at_row += n
            for name in HALF_ROWS:
                for half in range(2):
                    sp.dma_start(prow[at_row:at_row + 1, 1, half * 64:half * 64 + 64], A[name].rearrange("(a n) -> a n", a=1)).then_inc(s("params_in"), 16)
                at_row += 1
            taps = A["w_dw_2"].rearrange("t (c n) -> (t c) n", n=P)
            for half in range(2):
                sp.dma_start(prow[0:DW_ROWS // 2, 2 + half, :], taps[half * DW_ROWS // 2:(half + 1) * DW_ROWS // 2, :]).then_inc(s("params_in"), 16)
            sp.dma_start(relb[:], A["rel_bias"]).then_inc(s("params_in"), 16)
            sp.dma_start(sinks, A["sinks_b"].partition_broadcast(P)).then_inc(s("sinks_in"), 16)
            sp.dma_start(mem_in[:], A["mem"].rearrange("(t p) d -> p t d", p=P)).then_inc(s("mem_in"), 16)
            sp.dma_start(x_in[:], A["x"].rearrange("(t p) d -> p t d", p=P)).then_inc(s("x_in"), 16)

            for name in names:
                job = jobs[name]
                repeat(sp, job.steps, job.unroll, lambda i, u: [load_slab(sp, job, i, u, idx) for idx in range(job.S)])
            for r in range(4):
                sp.wait_ge(s("rows_ready"), 2 * r + 2)
                for t in range(2):
                    sp.dma_start(out[0, t * P:(t + 1) * P, r * 512:(r + 1) * 512], rows_out[:, t, r * 512:(r + 1) * 512]).then_inc(s("stored"), 16)
            sp.wait_ge(s("stored"), 16 * 8)

        @block.gpsimd
        def _(pool):
            link = Chain(pool, pool_link)
            link(pool.memset(ones[:], 1.0))
            link(pool.memset(ident[:], 0.0))
            link(pool.affine_select(out=ident[:], in_=ident[:], compare_op=ALU.not_equal, fill=1.0, base=0,
                                    pattern=[[-1, P]], channel_multiplier=1))
            link(pool.memset(blocks[:], 0.0))
            link(pool.memset(blocks[0:64, 0:64], 1.0))
            link(pool.memset(blocks[64:128, 64:128], 1.0))
            link(pool.memset(zrow[:], 0.0))
            pool.sem_inc(s("consts"), 1)

            def gather_squares(count, first, width=2 * T, done=0):
                view = sumsq.rearrange("p a t -> p (a t)")[:, 0:width]
                for r in range(count):
                    q = first + r
                    pool.wait_ge(s("squared"), q + 1)
                    if r == 0:
                        pool.tensor_copy(view, square[:, q % 2, 0:width]).then_inc(s("gathered"), 1)
                    else:
                        pool.wait_ge(s("gathered"), q)
                        pool.tensor_tensor(view, view, square[:, q % 2, 0:width], ALU.add).then_inc(s("gathered"), 1)

            pool.wait_ge(s("bias_rows"), 1)
            pool.dma_start(bias_dram.ap(), brow[:]).then_inc(s("bias_out"), 16)
            gather_squares(8, 0)
            pool.wait_ge(s("stats"), 1)
            gather_squares(8, 8)
            pool.wait_ge(s("turned_pe"), 16)
            link(pool.memset(flip[:], 0.0))
            pool.affine_select(out=flip[:], in_=flip[:], compare_op=ALU.not_equal, fill=1.0, base=1 - P,
                               pattern=[[1, P]], channel_multiplier=1).then_inc(s("flip_made"), 1)
            pool.wait_ge(s("turned_done"), 16)
            pool.dma_start(spill_x, turned[:]).then_inc(s("x_out"), 16)
            pool.wait_ge(s("bias_out"), 16)
            pool.wait_ge(used, PAIRS + jobs["early"].slab0)
            pool.dma_start(toep[:], bass.AP(bias_dram, 0, [[1, P], [2 * T, NB], [1, T]])).then_inc(s("toep_in"), 16)
            pool.wait_ge(s("flip_copied"), NB // 2)
            pool.affine_select(out=toep[:], in_=toep[:], compare_op=ALU.is_ge, fill=NEG, base=P,
                               pattern=[[0, NB], [-1, T]], channel_multiplier=1).then_inc(s("toep_masked"), 1)
            pool.wait_ge(s("toep_masked"), 1)
            tb = toep[:, A_HEADS:NB, :]
            pool.affine_select(out=tb, in_=tb, compare_op=ALU.is_ge, fill=NEG, base=WINDOW - 1 - P,
                               pattern=[[0, B_HEADS], [1, T]], channel_multiplier=-1).then_inc(s("toep_masked"), 1)
            pool.wait_ge(s("scored"), 1)
            for t in range(2):
                v = score[:, t * P:t * P + P * (t + 1)]
                pool.affine_select(out=v, in_=v, compare_op=ALU.is_ge, fill=NEG, base=t * P,
                                   pattern=[[-1, P * (t + 1)]], channel_multiplier=1).then_inc(s("score_masked"), 1)
            pool.wait_ge(s("topk"), 1)
            pool.wait_ge(s("toep_masked"), 2)
            pool.wait_ge(s("head_normed"), 8)
            for h in range(A_HEADS):
                if h >= 2:
                    pool.wait_ge(s("logits"), h - 1)
                b = h % 2
                mk = square[:, b, 0:3 * P]
                pool.tensor_tensor(mk[:, 0:P], toep[:, h, P:T], work[:, 0:P], ALU.add).then_inc(s("bias_mask"), 1)
                pool.tensor_tensor(mk[:, P:3 * P], toep[:, h, :], work[:, P:3 * P], ALU.add).then_inc(s("bias_mask"), 1)

            pool.wait_ge(s("head_normed"), 12)
            pool.dma_start(bk_swap[0:64, :], late[64:128, L_BK, :]).then_inc(s("swapped"), 16)
            pool.dma_start(bk_swap[64:128, :], late[0:64, L_BK, :]).then_inc(s("swapped"), 16)
            pool.wait_ge(s("x_out"), 16)
            pool.wait_ge(s("pv_copied"), A_HEADS + B_HEADS + C_HEADS)
            pool.dma_start(xT[:], spill_x).then_inc(s("x_back"), 16)

            def gated(b, src, gates, tiles):
                for r in range(tiles // 2):
                    q = sum((3, 3, 2)[:b]) + r
                    pool.wait_ge(s("gate_sig"), q + 1)
                    v = gate[:, q % 2, 0:2 * T]
                    g2 = late[:, gates + 2 * r:gates + 2 * r + 2, :].rearrange("p a t -> p (a t)")
                    o2 = src[:, 2 * r:2 * r + 2, :].rearrange("p a t -> p (a t)")
                    link(pool.tensor_tensor(v, v, g2, ALU.mult))
                    pool.tensor_tensor(v, v, o2, ALU.mult).then_inc(s("gated"), 1)

            def merge(name, dst, steps0, add):
                job = jobs[name]

                def body(i, u):
                    n = steps0 + i
                    pool.wait_ge(s("sig_ready"), n + 1)
                    pool.wait_ge(s("up_ready"), n + 1)
                    d2 = dst[:, bass.ds(i * 2, 2), :].rearrange("p a t -> p (a t)")
                    if add:
                        link(pool.tensor_tensor(gate[:, 1, 0:2 * T], gate[:, 0, 0:2 * T], tmp[:, 1, 0:2 * T], ALU.mult))
                        pool.tensor_tensor(d2, d2, gate[:, 1, 0:2 * T], ALU.add).then_inc(s("merged_step"), 1)
                    else:
                        pool.tensor_tensor(d2, gate[:, 0, 0:2 * T], tmp[:, 1, 0:2 * T], ALU.mult).then_inc(s("merged_step"), 1)
                repeat(pool, job.steps, 1, body, link, 1 if add else 0)

            gated(0, early[:, E_AQ:E_AQ + 6, :], L_AGATE, 6)
            merge("w_up_a", merged, 0, False)
            gated(1, late[:, L_BQ:L_BQ + 6, :], L_BGATE, 6)
            merge("w_up_b", merged, 8, True)
            gated(2, late[:, L_CQ:L_CQ + 4, :], L_CGATE, 4)
            merge("w_up_c", merged, 16, True)

            def add_square(q, parity, first=False):
                pool.wait_ge(s("squared"), q + 1)
                sq = square[:, parity, 0:2 * T].rearrange("p (a t) -> p a t", a=2)
                if first:
                    pool.tensor_copy(sumsq[:, :, META:TM], sq).then_inc(s("gathered"), 1)
                else:
                    pool.wait_ge(s("gathered"), q)
                    pool.tensor_tensor(sumsq[:, :, META:TM], sumsq[:, :, META:TM], sq, ALU.add).then_inc(s("gathered"), 1)

            pool.wait_ge(s("merged_ready"), 8)
            pool.dma_start(meta_in[:], A["meta_2"]).then_inc(s("meta_in"), 16)
            pool.wait_ge(s("x_back"), 16)
            for g in range(8):
                pool.wait_ge(s("folded"), g + 1)
                pool.tensor_tensor(h1[:, 2 * g:2 * g + 2, META:TM], tmp[:, g % 2, 0:2 * T].rearrange("p (a t) -> p a t", a=2),
                                   xT[:, 2 * g:2 * g + 2, :], ALU.add).then_inc(s("residual"), 1)
                if g >= 1:
                    add_square(16 + g - 1, (g - 1) % 2, g == 1)
            add_square(23, 1)
            pool.wait_ge(s("branch"), 4)
            for g in range(4):
                pool.wait_ge(s("glu_sig"), g + 1)
                v = glu[:, 2 * g:2 * g + 2, TAPS - 1 - META:]
                pool.tensor_tensor(v, v, gate[:, g % 2, :].rearrange("p (a t) -> p a t", a=2), ALU.mult).then_inc(s("glu_done"), 1)
            merge("pool_out", m, 24, False)
            merge("conv_out", m, 32, True)
            for g in range(8):
                add_square(24 + g, g % 2, g == 0)
            pool.wait_ge(s("stats"), 4)
            for g in range(8):
                add_square(32 + g, g % 2, g == 0)

            def add_down(q):
                job = jobs[f"w_down{q}"]

                def body(i, u):
                    g = i * job.unroll + u
                    pool.wait_ge(s("down"), q * 8 + g + 1)
                    d2 = y[:, bass.ds(g * 2, 2), :].rearrange("p a t -> p (a t)")
                    pool.tensor_tensor(d2, d2, tmp[:, u, 0:2 * T], ALU.add).then_inc(s("down_added"), 1)
                repeat(pool, job.steps, job.unroll, body)

            pool.wait_ge(s("h2"), 16)
            pool.memset(y[:], 0.0).then_inc(s("y_zero"), 1)
            pool.wait_ge(s("y_zero"), 1)
            pool.sem_inc(s("down_added"), 1)
            for q in range(4):
                add_down(q)
            pool.wait_ge(s("stats"), 5)
            for g in range(8):
                add_square(40 + g, g % 2, g == 0)

        @block.scalar
        def _(act):
            def rounding(name, body=None, peel=False):
                stream(act, round_high, name, body, peel=peel)

            std = [0]

            def root():
                std[0] += 1
                act.wait_ge(s("variance"), std[0])
                act.activation(rstd[:, 0:WIDTHS[std[0] - 1]], rstd[:, 0:WIDTHS[std[0] - 1]], ACT.Sqrt).then_inc(s("root"), 1)

            def high_parts(pair, width, first, sl=slice(None)):
                for r in range(8):
                    act.wait_ge(s("scaled"), first + r + 1)
                    act.activation(pair[:, 2 * r:2 * r + 2, 0, :], tmp[:, r % 2, 0:2 * width].rearrange("p (a t) -> p a t", a=2),
                                   ACT.Copy).then_inc(s("pair_high"), 1)

            for e in range(16):
                act.wait_ge(s("turned_pe"), e + 1)
                if e == 8:
                    act.wait_ge(s("pair_ready"), 8)
                act.activation(turned[:, 2 * (e % 8):2 * (e % 8) + 2, :], aux[:, e % 4, :].rearrange("p (a t) -> p a t", a=2),
                               ACT.Copy).then_inc(s("turned_done"), 1)
                if e >= 2:
                    act.wait_ge(s("gathered"), e - 1)
                act.activation(square[:, e % 2, 0:2 * T], aux[:, e % 4, :], ACT.Square).then_inc(s("squared"), 1)
                if e == 7:
                    root()
                    high_parts(mem_pair, T, 0)
                    act.wait_ge(s("stats"), 1)
            root()
            high_parts(hT, T, 8)
            for n in range(PAIRS):
                round_high(act, jobs["mem_kv"], 0, 0, n)
            rounding("mem_kv")
            rounding("early")
            for r in range(NB // 2):
                act.wait_ge(s("flipped"), r + 1)
                act.activation(toep[:, 2 * r:2 * r + 2, :], aux[:, r % 4, :].rearrange("p (a t) -> p a t", a=2), ACT.Copy).then_inc(s("flip_copied"), 1)
            rounding("ikw")

            def head_norm(n):
                for r in range(n):
                    q = hn[0]
                    hn[0] += 1
                    src, width = HEAD_NORMS[q][0], HEAD_NORMS[q][1]
                    if q >= 1:
                        act.wait_ge(s("head_stats"), q)
                    act.wait_ge(s(HEAD_NORMS[q][5][0]), HEAD_NORMS[q][5][1])
                    act.activation(square[:, 0, 0:width], src, ACT.Square).then_inc(s("head_squared"), 1)
                    act.wait_ge(s("head_var"), q + 1)
                    act.activation(rstd[:, 0:width if not HEAD_NORMS[q][4] else T], rstd[:, 0:width if not HEAD_NORMS[q][4] else T], ACT.Sqrt).then_inc(s("head_root"), 1)
            hn = [0]
            head_norm(5)
            for h in range(IDX_HEADS):
                act.wait_ge(s("idx_products"), h + 1)
                if h >= 2:
                    act.wait_ge(s("idx_added"), 2 * (h - 1))
                act.activation(lg[:, h % 2, 0:3 * P], aux[:, h % 4, 0:3 * P], ACT.Relu).then_inc(s("idx_relu"), 1)
            rounding("kv_up")
            head_norm(3)

            def softmax_heads(first, last):
                def exps(h):
                    act.wait_ge(s("logits"), h + 1)
                    b = h % 2
                    for t in range(2):
                        lo, hi = head_cols(h, t)
                        act.activation(lg[:, b, lo:hi], lg[:, b, lo:hi], ACT.Exp, bias=negmax[:, b, t:t + 1],
                                       accum_out=denom[:, b, t:t + 1]).then_inc(s("exps"), 1)
                    if A_HEADS <= h < A_HEADS + B_HEADS:
                        for t in range(2):
                            act.activation(esink[:, b, t:t + 1], sinks[:, h - A_HEADS:h - A_HEADS + 1], ACT.Exp,
                                           bias=negmax[:, b, t:t + 1]).then_inc(s("sink_exps"), 1)

                def turned_probs(h):
                    act.wait_ge(s("probs_turned"), h + 1)
                    if h >= 2:
                        act.wait_ge(s("pv"), h - 1)
                    w = 3 * P if h < A_HEADS + B_HEADS else 4 * P
                    act.activation(ptb[:, h % 2, 0:w], aux[:, 2, 0:w], ACT.Copy).then_inc(s("probs_copied"), 1)

                exps(first)
                for h in range(first, last):
                    if h + 1 < last:
                        exps(h + 1)
                    turned_probs(h)

            softmax_heads(0, A_HEADS)
            rounding("late")
            head_norm(8)
            softmax_heads(A_HEADS, A_HEADS + B_HEADS + C_HEADS)

            def silu(b, gates, tiles):
                act.wait_ge(s("merged_step"), 8 * b)
                for r in range(tiles // 2):
                    q = sum((3, 3, 2)[:b]) + r
                    if q >= 2:
                        act.wait_ge(s("o_split"), q - 1)
                    g2 = late[:, gates + 2 * r:gates + 2 * r + 2, :]
                    act.activation(gate[:, q % 2, 0:2 * T].rearrange("p (a t) -> p a t", a=2), g2, ACT.Sigmoid).then_inc(s("gate_sig"), 1)

            def gate_groups(name, steps0, bias):
                def body(i, u, part):
                    if part == 1:
                        return
                    n = steps0 + i
                    act.wait_ge(s("gate_in"), n + 1)
                    act.wait_ge(s("merged_step"), n)
                    for j in range(2):
                        b = params[:, bass.ds(COL["gate_bias"] + bias + i * 2 + j, 1)] if bias is not None else 0.0
                        act.activation(gate[:, 0, j * T:(j + 1) * T], tmp[:, 0, j * T:(j + 1) * T], ACT.Sigmoid,
                                       bias=b).then_inc(s("sig_half") if j == 0 else s("sig_ready"), 1)
                rounding(name, body)

            silu(0, L_AGATE, 6)
            gate_groups("w_up_a", 0, 0)
            silu(1, L_BGATE, 6)
            gate_groups("w_up_b", 8, 16)
            silu(2, L_CGATE, 4)
            gate_groups("w_up_c", 16, 32)

            def square_of(v, parity, q):
                act.wait_ge(s("gathered"), q - 1)
                act.activation(square[:, parity, 0:2 * T].rearrange("p (a t) -> p a t", a=2), v, ACT.Square).then_inc(s("squared"), 1)

            def sq_residual(i, u, part):
                g = 2 * i + u
                act.wait_ge(s("residual"), 2 + g + 1)
                square_of(h1[:, bass.ds(2 * g, 2), META:TM], u, 16 + g)
            rounding("w_o", sq_residual)
            root()
            high_parts(uT, TM, 16)

            def glu_body(i, u, part):
                g = 2 * i + u
                if g < 8:
                    return
                banks, _ = group_done(act, jobs["branches"], i, u)
                if g >= 10:
                    act.wait_ge(s("glu_done"), g - 9)
                act.activation(gate[:, u, :].rearrange("p (a t) -> p a t", a=2), banks[:, :, 0:TM], ACT.Sigmoid).then_inc(s("glu_sig"), 1)
            rounding("branches", glu_body, peel=True)
            rounding("pool_grp")
            act.wait_ge(s("conv_centered"), 1)
            for r in range(4):
                if r:
                    act.wait_ge(s("gathered2"), r)
                act.activation(square[:, 0, 0:2 * T], conv[:, 2 * r:2 * r + 2, :].rearrange("p a t -> p (a t)"), ACT.Square).then_inc(s("conv_sq"), 1)
            root()
            for r in range(4):
                act.wait_ge(s("conv_scaled"), r + 1)
                act.activation(gate[:, 0, 0:2 * T], conv[:, 2 * r:2 * r + 2, :].rearrange("p a t -> p (a t)"), ACT.Sigmoid).then_inc(s("conv_sig"), 1)
                act.wait_ge(s("conv_used"), r + 1)
            gate_groups("pool_out", 24, None)
            gate_groups("conv_out", 32, None)

            def sq_mixed(i, u, part):
                g = 2 * i + u
                act.wait_ge(s("mixed"), g + 1)
                square_of(mixed[:, bass.ds(2 * g, 2), :], u, 24 + g)
            rounding("w_o_2", sq_mixed)
            root()
            for g in range(8):
                act.wait_ge(s("h2"), 2 * g + 2)
                square_of(h1[:, 2 * g:2 * g + 2, META:TM], g % 2, 32 + g)
            root()
            high_parts(u2, T, 24)
            for q in range(4):
                rounding(f"w_up{q}")
                rounding(f"w_down{q}")
            for g in range(8):
                act.wait_ge(s("down_added"), 33)
                square_of(y[:, 2 * g:2 * g + 2, :], g % 2, 40 + g)
            root()
            for e in range(8):
                act.wait_ge(s("out_turned"), e + 1)
                r, t = e // 2, e % 2
                act.activation(rows_out[:, t, r * 512:(r + 1) * 512], aux[:, e % 4, :], ACT.Copy).then_inc(s("rows_ready"), 1)

        @block.tensor
        def _(pe):
            def products(name):
                job = jobs[name]
                if job.start_wait:
                    pe.wait_ge(s(job.start_wait[0]), job.start_wait[1])
                repeat(pe, job.steps, job.unroll, lambda i, u: multiply(pe, job, i, u))

            def stat(width, gathered):
                pe.wait_ge(s("gathered"), gathered)
                v = sumsq.rearrange("p a t -> p (a t)")
                for a in range(2):
                    mm = pe.matmul(aux[:, 0, 0:width], ones[:], v[:, a * width:(a + 1) * width], start=(a == 0), stop=(a == 1))
                mm.then_inc(s("stats"), 1)

            def stat_wide(width, gathered, lo):
                pe.wait_ge(s("gathered"), gathered)
                for a in range(2):
                    mm = pe.matmul(aux[:, 0, 0:width], ones[:], sumsq[:, a, lo:TM], start=(a == 0), stop=(a == 1))
                mm.then_inc(s("stats"), 1)

            pe.sem_inc(used, PAIRS)
            pe.wait_ge(s("consts"), 1)
            pe.wait_ge(s("params_in"), 16 * (len(ROWS0) + len(ROWS1) + 2 * len(HALF_ROWS) + 3))
            for q, (c0, n) in enumerate(PARAM_GROUPS):
                pe.transpose(aux[:, q, 0:n], prow[0:n, q, :], ident[0:n, 0:n])
            pe.transpose(aux[0:NB, 1, P:P + BUCKETS], relb[:], ident[0:BUCKETS, 0:BUCKETS]).then_inc(s("params_turned"), 1)
            pe.wait_ge(s("params_copied"), 5)
            for e in range(16):
                src = mem_in if e < 8 else x_in
                if e == 0:
                    pe.wait_ge(s("mem_in"), 16)
                if e == 8:
                    stat(T, 8)
                    pe.wait_ge(s("variance"), 1)
                    pe.wait_ge(s("x_in"), 16)
                if e >= 4:
                    pe.wait_ge(s("squared"), e - 3)
                for k in range(2):
                    for t in range(2):
                        kt = 2 * (e % 8) + k
                        mm = pe.transpose(aux[:, e % 4, (2 * k + t) * P:(2 * k + t + 1) * P], src[:, t, kt * P:(kt + 1) * P], ident[:])
                mm.then_inc(s("turned_pe"), 1)
            stat(T, 16)
            products("mem_kv")
            products("early")
            pe.wait_ge(s("toep_in"), 16)
            pe.wait_ge(s("flip_made"), 1)
            for r in range(NB // 2):
                if r >= 4:
                    pe.wait_ge(s("flip_copied"), r - 3)
                pe.matmul(aux[:, r % 4, :], flip[:], toep[:, 2 * r:2 * r + 2, :], start=True, stop=True).then_inc(s("flipped"), 1)
            products("ikw")
            hn = [0]

            def head_norm(n):
                for r in range(n):
                    q = hn[0]
                    hn[0] += 1
                    src, width, mat, inv, both, _, _ = HEAD_NORMS[q]
                    if q == IK_NORM:
                        pe.wait_ge(s("folded_heads"), 2)
                        pe.wait_ge(s("center"), 2)
                        pe.wait_ge(s("head_var"), q)
                        pe.matmul(aux[:, 1, 0:T], center[:], ikw[0:IDX_DIM, :], start=True, stop=True).then_inc(s("ik_centered"), 1)
                        for t in range(2):
                            mm = pe.transpose(aux[:, 2, t * P:(t + 1) * P], ikw[:, t * P:(t + 1) * P], ident[:])
                        mm.then_inc(s("iw_turned"), 1)
                    pe.wait_ge(s("head_squared"), q + 1)
                    if q >= 1:
                        pe.wait_ge(s("head_var"), q)
                    if both:
                        for a in range(2):
                            mm = pe.matmul(aux[:, 0, 0:T], mat[:], square[:, 0, a * T:(a + 1) * T], start=(a == 0), stop=(a == 1))
                    else:
                        mm = pe.matmul(aux[:, 0, 0:width], mat[:], square[:, 0, 0:width], start=True, stop=True)
                    mm.then_inc(s("head_stats"), 1)
            pe.wait_ge(s("flip_copied"), NB // 2)
            head_norm(5)
            pe.wait_ge(s("ik_ready"), 1)
            for h in range(IDX_HEADS):
                if h >= 4:
                    pe.wait_ge(s("idx_relu"), h - 3)
                r = (h % 2) * 64
                q = early[r:r + 64, E_IQ + h // 2, :]
                pe.matmul(aux[:, h % 4, 0:P], q[:, 0:P], ikn[r:r + 64, 0:P], start=True, stop=True)
                pe.matmul(aux[:, h % 4, P:3 * P], q[:, P:T], ikn[r:r + 64, :], start=True, stop=True).then_inc(s("idx_products"), 1)
            products("kv_up")
            pe.wait_ge(s("idx_relu"), IDX_HEADS)
            head_norm(3)

            def values(src, dst_tiles, tiles, done0):
                for v in range(tiles):
                    n = done0 + v
                    if n >= 1:
                        pe.wait_ge(s("values_copied"), n)
                    for t in range(2):
                        mm = pe.transpose(aux[:, 3, t * P:(t + 1) * P], src[:, v, t * P:(t + 1) * P], ident[:])
                    mm.then_inc(s("values_turned"), 1)

            pe.wait_ge(s("folded_heads"), 3)
            pe.wait_ge(s("idx_relu"), IDX_HEADS)
            values(akv[:, 6:12, :], v_a, 6, 0)

            def softmax_heads(first, last):
                def logits(h):
                    if h - first >= 2:
                        pe.wait_ge(s("logits"), h - 1)
                    bank = aux[:, h % 2, :]
                    if h < A_HEADS:
                        q, k = early[:, E_AQ + h, :], akv[:, h, :]
                    elif h < A_HEADS + B_HEADS:
                        b = h - A_HEADS
                        r = (b % 2) * 64
                        kv = b // (B_HEADS // 2)
                        q = late[r:r + 64, L_BQ + b // 2, :]
                        k = late[r:r + 64, L_BK, :] if kv == b % 2 else bk_swap[r:r + 64, :]
                    else:
                        c = h - A_HEADS - B_HEADS
                        q, k = late[:, L_CQ + c, :], mkv[:, c, :]
                    for t in range(2):
                        lo, hi = head_cols(h, t)
                        mm = pe.matmul(bank[:, lo:hi], q[:, t * P:(t + 1) * P], k[:, 0:hi - lo], start=True, stop=True)
                    mm.then_inc(s("qk"), 1)

                def attend(h):
                    pe.wait_ge(s("probs"), h + 1)
                    if h >= 1:
                        pe.wait_ge(s("probs_copied"), h)
                    w = 3 if h < A_HEADS + B_HEADS else 4
                    for c in range(w):
                        mm = pe.transpose(aux[:, 2, c * P:(c + 1) * P], lg[:, h % 2, c * P:(c + 1) * P], ident[:])
                    mm.then_inc(s("probs_turned"), 1)
                    pe.wait_ge(s("probs_copied"), h + 1)
                    dst = aux[:, 3, 0:T]
                    if h >= 1:
                        pe.wait_ge(s("pv_copied"), h)
                    if h < A_HEADS:
                        v = lambda st: v_a[:, st, h * P:(h + 1) * P]
                    elif h < A_HEADS + B_HEADS:
                        b = h - A_HEADS
                        kv, r = b // (B_HEADS // 2), (b % 2) * 64
                        v = lambda st: v_b[:, st, kv * 64:kv * 64 + 64]
                        dst = aux[r:r + 64, 3, 0:T]
                    else:
                        c = h - A_HEADS - B_HEADS
                        v = lambda st: v_c[:, st, c * P:(c + 1) * P]
                    p = ptb[:, h % 2, :]
                    if w == 3:
                        pe.matmul(dst[:, 0:P], v(0), p[:, 0:P], start=True, stop=True)
                        pe.matmul(dst[:, P:T], v(0), p[:, P:2 * P], start=True, stop=False)
                        mm = pe.matmul(dst[:, P:T], v(1), p[:, 2 * P:3 * P], start=False, stop=True)
                    else:
                        for t in range(2):
                            for st in range(2):
                                lo = (2 * t + st) * P
                                mm = pe.matmul(dst[:, t * P:(t + 1) * P], v(st), p[:, lo:lo + P], start=(st == 0), stop=(st == 1))
                    mm.then_inc(s("pv"), 1)

                logits(first)
                for h in range(first, last):
                    if h + 1 < last:
                        logits(h + 1)
                    attend(h)

            pe.wait_ge(s("head_normed"), 8)
            pe.wait_ge(s("values_copied"), 6)
            softmax_heads(0, A_HEADS)
            products("late")
            pe.wait_ge(s("pv_copied"), A_HEADS)
            head_norm(8)
            pe.wait_ge(s("folded_heads"), 4)
            values(late[:, L_BV:L_BV + 1, :], v_b, 1, 6)
            values(mkv[:, 4:8, :], v_c, 4, 7)
            pe.wait_ge(s("head_normed"), 16)
            pe.wait_ge(s("values_copied"), 11)
            pe.wait_ge(s("swapped"), 32)
            softmax_heads(A_HEADS, A_HEADS + B_HEADS + C_HEADS)
            for name in ("w_up_a", "w_up_b", "w_up_c", "w_o"):
                products(name)
            pe.wait_ge(s("meta_in"), 16)
            pe.wait_ge(s("pv_copied"), 22)
            for k in range(KT):
                mm = pe.transpose(aux[:, 1, k * META:(k + 1) * META], meta_in[:, k * P:(k + 1) * P], ident[0:META, 0:META])
            mm.then_inc(s("meta_turned"), 1)
            pe.wait_ge(s("meta_sums"), 1)
            stat_wide(TM, 24, 0)
            products("branches")
            products("pool_grp")
            pe.wait_ge(s("conv_done"), 1)
            for k in range(8):
                mm = pe.matmul(aux[:, 1, 0:T], ones[:], conv[:, k, :], start=(k == 0), stop=(k == 7))
            mm.then_inc(s("conv_sum"), 1)
            for r in range(4):
                pe.wait_ge(s("conv_sq"), r + 1)
                for a in range(2):
                    mm = pe.matmul(aux[:, 0, 0:T], ones[:], square[:, 0, a * T:(a + 1) * T], start=(r == 0 and a == 0), stop=(r == 3 and a == 1))
                mm.then_inc(s("gathered2"), 1)
            for name in ("pool_out", "conv_out", "w_o_2"):
                products(name)
            stat_wide(T, 32, META)
            pe.wait_ge(s("variance"), 5)
            stat_wide(T, 40, META)
            for q in range(4):
                products(f"w_up{q}")
                products(f"w_down{q}")
            stat_wide(T, 48, META)
            pe.wait_ge(s("variance"), 7)
            for e in range(8):
                r, t = e // 2, e % 2
                pe.wait_ge(s("final"), 4 * r + 4)
                if e >= 4:
                    pe.wait_ge(s("rows_ready"), e - 3)
                for k in range(4):
                    mm = pe.transpose(aux[:, e % 4, k * P:(k + 1) * P], y[:, 4 * r + k, t * P:(t + 1) * P], ident[:])
                mm.then_inc(s("out_turned"), 1)

        @block.vector
        def _(dve):
            link = Chain(dve, dve_link)

            def column(name, k=0):
                return params[:, COL[name] + k:COL[name] + k + 1]

            dve.sem_inc(split_done, STAGES)
            dve.sem_inc(acc_free, 2)
            dve.wait_ge(s("params_turned"), 1)
            for q, (c0, n) in enumerate(PARAM_GROUPS):
                dve.tensor_copy(params[:, c0:c0 + n], aux[:, q, 0:n]).then_inc(s("params_copied"), 1)
            link(dve.tensor_copy(relT[:], aux[0:NB, 1, P:P + BUCKETS]))
            dve.sem_inc(s("params_copied"), 1)
            dve.wait_ge(s("params_copied"), 5)
            dve.wait_ge(s("consts"), 1)
            for b in range(BUCKETS):
                lo = T - starts[b + 1]
                hi = T - starts[b] if b else 2 * T
                mm = dve.tensor_scalar(brow[:, lo:hi], zrow[:, lo:hi], relT[:, b:b + 1], None, ALU.add)
            mm.then_inc(s("bias_rows"), 1)
            link(dve.tensor_scalar(center[:, 0:64], ident[0:64, 0:64], 1.0 / IDX_DIM, None, ALU.subtract))
            dve.sem_inc(s("center"), 1)
            dve.tensor_scalar(center[:, 64:128], ident[0:64, 0:64], 1.0 / IDX_DIM, None, ALU.subtract).then_inc(s("center"), 1)

            stat_n = [0]

            def inverse_std(width, inv_d, eps, src=None):
                q = stat_n[0]
                stat_n[0] += 1
                if src is None:
                    dve.wait_ge(s("stats"), src_stats[0] + 1)
                    src_stats[0] += 1
                    src = aux[:, 0, 0:width]
                r = rstd[:, 0:width]
                dve.tensor_scalar(r, src, inv_d, eps, ALU.mult, ALU.add).then_inc(s("variance"), 1)
                dve.wait_ge(s("root"), q + 1)
                link(dve.reciprocal(r, r))
            src_stats = [0]

            def normalize(src, pair, width, gain, first):
                def low(r):
                    dve.wait_ge(s("pair_high"), first + r + 1)
                    dve.tensor_tensor(pair[:, 2 * r:2 * r + 2, 1, :], tmp[:, r % 2, 0:2 * width].rearrange("p (a t) -> p a t", a=2),
                                      pair[:, 2 * r:2 * r + 2, 0, :].bitcast(F32), ALU.subtract).then_inc(s("pair_ready"), 1)
                for r in range(8):
                    dve.wait_ge(s("pair_ready"), first + max(r - 1, 0))
                    for a in range(2):
                        k = 2 * r + a
                        ins = dve.scalar_tensor_tensor(out=tmp[:, r % 2, a * width:(a + 1) * width], in0=src(k), scalar=column(gain, k),
                                                       in1=rstd[:, 0:width], op0=ALU.mult, op1=ALU.mult)
                        if a == 0:
                            ins.then_inc(s("scaled_half"), 1)
                        else:
                            dve.wait_ge(s("scaled_half"), first + r + 1)
                            ins.then_inc(s("scaled"), 1)
                    if r >= 1:
                        low(r - 1)
                low(7)

            inverse_std(T, 1.0 / D, EPS)
            normalize(lambda k: turned[:, k, :], mem_pair, T, "mem_norm_g", 0)
            inverse_std(T, 1.0 / D, EPS)
            dve.wait_ge(s("bias_out"), 16)
            normalize(lambda k: turned[:, k, :], hT, T, "norm_g", 8)

            def splitting(name, body, links=0, peel=False):
                stream(dve, subtract_low, name, body, link, links, peel)

            def fold_into(name, dst, tile0=0, done=None):
                job = jobs[name]

                def body(i, u, part):
                    banks, _ = group_done(dve, job, i, u)
                    g = i * job.unroll + u
                    ins = fold(dve, dst[:, bass.ds(tile0 + g * 2, 2), :], banks)
                    ins.then_inc(acc_free, 1)
                return body

            for n in range(PAIRS):
                subtract_low(dve, jobs["mem_kv"], 0, 0, n)
            splitting("mem_kv", fold_into("mem_kv", mkv))
            dve.wait_ge(s("x_out"), 16)
            splitting("early", fold_into("early", early))

            def signal(name):
                dve.drain().then_inc(s(name), 1)

            signal("folded_heads")

            def ikw_body(i, u, part):
                banks, _ = group_done(dve, jobs["ikw"], i, u)
                dve.tensor_reduce(ikw[:], banks[:, 0, :].rearrange("p (h t) -> p t h", h=2), AX, ALU.add).then_inc(acc_free, 1)
            splitting("ikw", ikw_body)
            signal("folded_heads")
            hn = [0]

            def head_norm(n):
                for r in range(n):
                    q = hn[0]
                    hn[0] += 1
                    src, width, mat, inv, both, _, gain = HEAD_NORMS[q]
                    if q == IK_NORM:
                        dve.wait_ge(s("ik_centered"), 1)
                        link(dve.tensor_copy(ikn[:], aux[:, 1, 0:T]))
                        dve.sem_inc(s("ik_copied"), 1)
                        dve.wait_ge(s("iw_turned"), 1)
                        dve.tensor_scalar(iw, aux[:, 2, 0:T].rearrange("p (t c) -> p t c", t=2)[:, :, 64:80],
                                          IDX_HEADS ** -0.5 * IDX_DIM ** -0.5, None, ALU.mult).then_inc(s("iw_ready"), 1)
                    w = T if both else width
                    dve.wait_ge(s("head_stats"), q + 1)
                    if q:
                        dve.wait_ge(s("head_normed"), q)
                    dve.tensor_scalar(rstd[:, 0:w], aux[:, 0, 0:w], inv, EPS, ALU.mult, ALU.add).then_inc(s("head_var"), 1)
                    dve.wait_ge(s("head_root"), q + 1)
                    link(dve.reciprocal(rstd[:, 0:w], rstd[:, 0:w]))
                    if both:
                        for a in range(2):
                            link(dve.scalar_tensor_tensor(out=tmp[:, 0, a * T:(a + 1) * T], in0=src[:, a * T:(a + 1) * T], scalar=params[:, gain + a:gain + a + 1],
                                                          in1=rstd[:, 0:T], op0=ALU.mult, op1=ALU.mult))
                        v = tmp[:, 0, 0:2 * T].rearrange("p (a t) -> p a t", a=2)
                        link(dve.tensor_copy(ckv_pair[:, :, 0, :], v))
                        link(dve.tensor_tensor(ckv_pair[:, :, 1, :], v, ckv_pair[:, :, 0, :].bitcast(F32), ALU.subtract))
                        dve.sem_inc(s("ckv_ready"), 1)
                        dve.sem_inc(s("head_normed"), 1)
                        continue
                    ins = dve.scalar_tensor_tensor(out=src, in0=src, scalar=params[:, gain:gain + 1], in1=rstd[:, 0:w], op0=ALU.mult, op1=ALU.mult)
                    if q == IK_NORM:
                        link(ins)
                        dve.wait_ge(s("iw_ready"), 1)
                        ins = dve.tensor_scalar(ikn[:], ikn[:], column("idx_k_ln_b"), None, ALU.add)
                        ins.then_inc(s("ik_ready"), 1)
                        dve.wait_ge(s("ik_ready"), 1)
                        dve.sem_inc(s("head_normed"), 1)
                        continue
                    ins.then_inc(s("head_normed"), 1)
            head_norm(5)
            dve.memset(score[:], 0.0).then_inc(s("score_zero"), 1)
            dve.wait_ge(s("score_zero"), 1)
            for h in range(IDX_HEADS):
                dve.wait_ge(s("idx_relu"), h + 1)
                if h:
                    dve.wait_ge(s("idx_added"), 2 * h)
                for t in range(2):
                    lo, hi = head_cols(0, t)
                    dve.scalar_tensor_tensor(out=score[:, lo:hi], in0=lg[:, h % 2, lo:hi], scalar=iw[:, t, h:h + 1], in1=score[:, lo:hi],
                                             op0=ALU.mult, op1=ALU.add).then_inc(s("idx_added"), 1)
            dve.wait_ge(s("idx_added"), 2 * IDX_HEADS)
            dve.sem_inc(s("scored"), 1)
            dve.wait_ge(s("score_masked"), 2)
            for r in range(TOPK // 8):
                for t in range(2):
                    lo, hi = head_cols(0, t)
                    src = score if r == 0 else work
                    link(dve.max(top8[:, t, :], src[:, lo:hi]))
                    link(dve.match_replace(work[:, lo:hi], top8[:, t, :], src[:, lo:hi], TAKEN))
            dve.tensor_scalar(work[:], work[:], TAKEN / 2, NEG, ALU.is_gt, ALU.mult).then_inc(s("topk"), 1)
            splitting("kv_up", fold_into("kv_up", akv))
            signal("folded_heads")
            head_norm(3)

            def copy_values(dst, tiles, done0):
                for v in range(tiles):
                    dve.wait_ge(s("values_turned"), done0 + v + 1)
                    dve.tensor_copy(dst[:, :, v * P:(v + 1) * P], aux[:, 3, 0:T].rearrange("p (t c) -> p t c", t=2)).then_inc(s("values_copied"), 1)
            copy_values(v_a, 6, 0)

            def softmax_heads(first, last):
                def logits(h):
                    b = h % 2
                    dve.wait_ge(s("qk"), h + 1)
                    if h - first >= 2:
                        dve.wait_ge(s("probs_turned"), h - 1)
                    w = 3 * P if h < A_HEADS + B_HEADS else 4 * P
                    scale = (B_DIM if A_HEADS <= h < A_HEADS + B_HEADS else P) ** -0.5
                    if h < A_HEADS:
                        dve.wait_ge(s("bias_mask"), 2 * h + 2)
                        link(dve.scalar_tensor_tensor(out=lg[:, b, 0:w], in0=aux[:, b, 0:w], scalar=scale, in1=square[:, b, 0:w], op0=ALU.mult, op1=ALU.add))
                    elif h < A_HEADS + B_HEADS:
                        for t in range(2):
                            lo, hi = head_cols(h, t)
                            link(dve.scalar_tensor_tensor(out=lg[:, b, lo:hi], in0=aux[:, b, lo:hi], scalar=scale,
                                                          in1=toep[:, h, T - (hi - lo):T], op0=ALU.mult, op1=ALU.add))
                    else:
                        link(dve.tensor_scalar(lg[:, b, 0:w], aux[:, b, 0:w], scale, None, ALU.mult))
                    for t in range(2):
                        lo, hi = head_cols(h, t)
                        link(dve.tensor_reduce(negmax[:, b, t:t + 1], lg[:, b, lo:hi], AX, ALU.max))
                    if A_HEADS <= h < A_HEADS + B_HEADS:
                        link(dve.tensor_scalar(negmax[:, b, :], negmax[:, b, :], sinks[:, h - A_HEADS:h - A_HEADS + 1], None, ALU.max))
                    link(dve.tensor_scalar(negmax[:, b, :], negmax[:, b, :], -1.0, None, ALU.mult))
                    dve.sem_inc(s("logits"), 1)

                def scale_probs(h):
                    b = h % 2
                    dve.wait_ge(s("exps"), 2 * h + 2)
                    if A_HEADS <= h < A_HEADS + B_HEADS:
                        dve.wait_ge(s("sink_exps"), 2 * (h - A_HEADS) + 2)
                    if A_HEADS <= h < A_HEADS + B_HEADS:
                        link(dve.tensor_tensor(denom[:, b, :], denom[:, b, :], esink[:, b, :], ALU.add))
                    link(dve.reciprocal(denom[:, b, :], denom[:, b, :]))
                    for t in range(2):
                        lo, hi = head_cols(h, t)
                        link(dve.tensor_scalar(lg[:, b, lo:hi], lg[:, b, lo:hi], denom[:, b, t:t + 1], None, ALU.mult))
                    dve.sem_inc(s("probs"), 1)

                def copy_out(h):
                    dve.wait_ge(s("pv"), h + 1)
                    if h < A_HEADS:
                        dst, src = early[:, E_AQ + h, :], aux[:, 3, 0:T]
                    elif h < A_HEADS + B_HEADS:
                        bb = h - A_HEADS
                        r = (bb % 2) * 64
                        dst, src = late[r:r + 64, L_BQ + bb // 2, :], aux[r:r + 64, 3, 0:T]
                    else:
                        dst, src = late[:, L_CQ + h - A_HEADS - B_HEADS, :], aux[:, 3, 0:T]
                    dve.tensor_copy(dst, src).then_inc(s("pv_copied"), 1)

                logits(first)
                for h in range(first, last):
                    if h + 1 < last:
                        logits(h + 1)
                    scale_probs(h)
                    copy_out(h)

            dve.wait_ge(s("sinks_in"), 16)
            softmax_heads(0, A_HEADS)
            splitting("late", fold_into("late", late))
            signal("folded_heads")
            head_norm(8)
            copy_values(v_b, 1, 6)
            copy_values(v_c, 4, 7)
            softmax_heads(A_HEADS, A_HEADS + B_HEADS + C_HEADS)

            def split_branch(b, tiles):
                for r in range(tiles // 2):
                    q = sum((3, 3, 2)[:b]) + r
                    dve.wait_ge(s("gated"), q + 1)
                    v = gate[:, q % 2, 0:2 * T].rearrange("p (a t) -> p a t", a=2)
                    link(dve.tensor_copy(o_pair[:, 2 * r:2 * r + 2, 0, :], v))
                    dve.tensor_tensor(o_pair[:, 2 * r:2 * r + 2, 1, :], v, o_pair[:, 2 * r:2 * r + 2, 0, :].bitcast(F32), ALU.subtract).then_inc(s("o_split"), 1)
                dve.wait_ge(s("o_split"), sum((3, 3, 2)[:b + 1]))
                dve.sem_inc(s("o_pair_ready"), 1)

            def gated_product(name, steps0, dst=None, pair=None, ready=None):
                job = jobs[name]

                def body(i, u, part):
                    n = steps0 + i
                    banks, _ = group_done(dve, job, i, u, part)
                    if part == 0:
                        dve.wait_ge(s("merged_step"), n)
                    done = s("gate_in") if part == 0 else s("up_ready")
                    fold(dve, tmp[:, part, 0:2 * T].rearrange("p (a t) -> p a t", a=2), banks).then_inc(done, 1)
                    dve.wait_ge(done, n + 1)
                    dve.sem_inc(acc_free, 1)
                    if part == 1 and pair is not None:
                        dve.wait_ge(s("merged_step"), n + 1)
                        hi, lo = pair[:, bass.ds(i * 2, 2), 0, :], pair[:, bass.ds(i * 2, 2), 1, :]
                        v = dst[:, bass.ds(i * 2, 2), :]
                        dve.tensor_copy(hi, v).then_inc(s("pair_step"), 1)
                        dve.wait_ge(s("pair_step"), i + 1 + (0 if ready == "merged_ready" else 8))
                        dve.tensor_tensor(lo, v, hi.bitcast(F32), ALU.subtract).then_inc(s(ready), 1)
                splitting(name, body)

            split_branch(0, 6)
            gated_product("w_up_a", 0)
            split_branch(1, 6)
            gated_product("w_up_b", 8)
            split_branch(2, 4)
            gated_product("w_up_c", 16, merged, merged_pair, "merged_ready")

            dve.sem_inc(s("residual"), 2)

            def wo_body(i, u, part):
                banks, _ = group_done(dve, jobs["w_o"], i, u)
                g = 2 * i + u
                dve.wait_ge(s("residual"), g + 1)
                fold(dve, tmp[:, u, 0:2 * T].rearrange("p (a t) -> p a t", a=2), banks).then_inc(s("folded"), 1)
                dve.wait_ge(s("folded"), g + 1)
                dve.sem_inc(acc_free, 1)
            splitting("w_o", wo_body)
            dve.wait_ge(s("meta_turned"), 1)
            link(dve.tensor_copy(h1[:, :, 0:META], aux[:, 1, 0:KT * META].rearrange("p (k t) -> p k t", k=KT)))
            sqm = tmp[:, 0, 0:KT * META]
            dve.wait_ge(s("residual"), 2 + 8)
            link(dve.tensor_tensor(sqm.rearrange("p (k t) -> p k t", k=KT), h1[:, :, 0:META], h1[:, :, 0:META], ALU.mult))
            link(dve.memset(sumsq[:, 1, 0:META], 0.0))
            dve.tensor_reduce(sumsq[:, 0, 0:META], sqm.rearrange("p (k t) -> p t k", k=KT), AX, ALU.add).then_inc(s("meta_sums"), 1)
            inverse_std(TM, 1.0 / D, EPS)
            normalize(lambda k: h1[:, k, :], uT, TM, "g_pre_mix_2", 16)

            link(dve.memset(glu[:, :, 0:TAPS - 1 - META], 0.0))

            def branch_body(i, u, part):
                g = 2 * i + u
                banks, _ = group_done(dve, jobs["branches"], i, u)
                if g < 4:
                    link(dve.tensor_copy(z_pool[:, 2 * g:2 * g + 2, :], banks[:, :, 0:TM]))
                elif g < 8:
                    link(dve.tensor_copy(glu[:, 2 * (g - 4):2 * (g - 4) + 2, TAPS - 1 - META:], banks[:, :, 0:TM]))
                    dve.sem_inc(s("branch"), 1)
                else:
                    dve.wait_ge(s("glu_sig"), g - 7)
                dve.sem_inc(acc_free, 1)
            splitting("branches", branch_body, peel=True)
            for g in range(4):
                src = z_pool[:, 2 * g:2 * g + 2, :]
                reach = 1
                for r in range(g + 1):
                    dst = window[:, r % 2, :].rearrange("p (a t) -> p a t", a=2)
                    link(dve.tensor_tensor(dst[:, :, 2 * reach - 1:TM], src[:, :, 2 * reach - 1:TM], src[:, :, reach - 1:TM - reach], ALU.add))
                    src = dst
                    reach *= 2
                v = tmp[:, 0, 0:2 * T].rearrange("p (a t) -> p a t", a=2)
                link(dve.scalar_tensor_tensor(out=v, in0=src[:, :, META:TM], scalar=1.0 / reach, in1=z_pool[:, 2 * g:2 * g + 2, META:TM],
                                              op0=ALU.mult, op1=ALU.subtract))
                link(dve.tensor_copy(d_pair[:, 2 * g:2 * g + 2, 0, :], v))
                link(dve.tensor_tensor(d_pair[:, 2 * g:2 * g + 2, 1, :], v, d_pair[:, 2 * g:2 * g + 2, 0, :].bitcast(F32), ALU.subtract))
            dve.sem_inc(s("d_ready"), 1)
            def grp_body(i, u, part):
                banks, _ = group_done(dve, jobs["pool_grp"], i, u)
                g = 4 * i + u
                v = tmp[:, 0, 0:2 * T].rearrange("p (a t) -> p a t", a=2)
                link(fold(dve, v, banks))
                dve.sem_inc(acc_free, 1)
                for a in range(2):
                    link(dve.tensor_scalar(v[:, a, :], v[:, a, :], column("pool_scale_2", 2 * g + a), None, ALU.mult))
                link(dve.tensor_copy(y_pair[:, 2 * g:2 * g + 2, 0, :], v))
                dve.tensor_tensor(y_pair[:, 2 * g:2 * g + 2, 1, :], v, y_pair[:, 2 * g:2 * g + 2, 0, :].bitcast(F32), ALU.subtract).then_inc(s("y_pair_ready"), 1)
                dve.wait_ge(s("y_pair_ready"), g + 1)
            splitting("pool_grp", grp_body)
            dve.wait_ge(s("glu_done"), 4)
            for k in range(8):
                dve.tensor_scalar(conv[:, k, :], glu[:, k, 0:T], column("w_dw_2", k), column("b_dw_2", k), ALU.mult, ALU.add).then_inc(s("conv_taps"), 1)

            with dve.Fori(1, TAPS) as tap:
                for k in range(8):
                    if k == 0:
                        dve.wait_ge(s("conv_taps"), 8 * tap)
                    dve.scalar_tensor_tensor(out=conv[:, k, :], in0=glu[:, k, bass.ds(tap, T)], scalar=params[:, bass.ds(COL["w_dw_2"] + k + 8 * tap, 1)],
                                             in1=conv[:, k, :], op0=ALU.mult, op1=ALU.add).then_inc(s("conv_taps"), 1)
            dve.wait_ge(s("conv_taps"), 8 * TAPS)
            dve.sem_inc(s("conv_done"), 1)

            dve.wait_ge(s("conv_sum"), 1)
            link(dve.tensor_scalar(rstd[:, T:2 * T], aux[:, 1, 0:T], 1.0 / CONV_W, None, ALU.mult))
            for k in range(8):
                ins = dve.tensor_tensor(conv[:, k, :], conv[:, k, :], rstd[:, T:2 * T], ALU.subtract)
                link(ins)
            dve.sem_inc(s("conv_centered"), 1)
            dve.wait_ge(s("gathered2"), 4)
            inverse_std(T, 1.0 / CONV_W, LN_EPS, src=aux[:, 0, 0:T])
            for r in range(4):
                for a in range(2):
                    k = 2 * r + a
                    link(dve.scalar_tensor_tensor(out=conv[:, k, :], in0=conv[:, k, :], scalar=column("conv_ln_g_2", k), in1=rstd[:, 0:T], op0=ALU.mult, op1=ALU.mult))
                    link(dve.tensor_scalar(conv[:, k, :], conv[:, k, :], column("conv_ln_b_2", k), None, ALU.add))
                dve.sem_inc(s("conv_scaled"), 1)
                dve.wait_ge(s("conv_sig"), r + 1)
                v = conv[:, 2 * r:2 * r + 2, :]
                link(dve.tensor_tensor(v, v, gate[:, 0, 0:2 * T].rearrange("p (a t) -> p a t", a=2), ALU.mult))
                dve.sem_inc(s("conv_used"), 1)
            for r in range(4):
                v = conv[:, 2 * r:2 * r + 2, :]
                link(dve.tensor_copy(conv_pair[:, 2 * r:2 * r + 2, 0, :], v))
                link(dve.tensor_tensor(conv_pair[:, 2 * r:2 * r + 2, 1, :], v, conv_pair[:, 2 * r:2 * r + 2, 0, :].bitcast(F32), ALU.subtract))
            dve.sem_inc(s("conv_ready"), 1)
            gated_product("pool_out", 24)
            gated_product("conv_out", 32, m, m_pair, "m_ready")

            def mixed_body(i, u, part):
                banks, _ = group_done(dve, jobs["w_o_2"], i, u)
                g = 2 * i + u
                fold(dve, mixed[:, bass.ds(2 * g, 2), :], banks).then_inc(s("mixed"), 1)
                dve.wait_ge(s("mixed"), g + 1)
                dve.sem_inc(acc_free, 1)
            splitting("w_o_2", mixed_body)
            inverse_std(T, 1.0 / D, EPS)
            for k in range(KT):
                v = tmp[:, k % 2, 0:T]
                link(dve.scalar_tensor_tensor(out=v, in0=mixed[:, k, :], scalar=column("g_post_mix_2", k), in1=rstd[:, 0:T], op0=ALU.mult, op1=ALU.mult))
                dve.tensor_tensor(h1[:, k, META:TM], h1[:, k, META:TM], v, ALU.add).then_inc(s("h2"), 1)
            inverse_std(T, 1.0 / D, EPS)
            dve.wait_ge(s("h2"), 16)
            normalize(lambda k: h1[:, k, META:TM], u2, T, "g_pre_mlp_2", 24)

            def up_body(q):
                job = jobs[f"w_up{q}"]

                def body(i, u, part):
                    banks, _ = group_done(dve, job, i, u)
                    g = i * job.unroll + u
                    v = tmp[:, u, 0:2 * T].rearrange("p (a t) -> p a t", a=2)
                    link(fold(dve, v, banks))
                    dve.sem_inc(acc_free, 1)
                    f = tmp[:, u, 0:2 * T]
                    link(dve.scalar_tensor_tensor(out=f, in0=f, scalar=0.0, in1=f, op0=ALU.max, op1=ALU.mult))
                    hi, lo = f_pair[:, bass.ds(g * 2, 2), 0, :], f_pair[:, bass.ds(g * 2, 2), 1, :]
                    link(dve.tensor_copy(hi, v))
                    dve.tensor_tensor(lo, v, hi.bitcast(F32), ALU.subtract).then_inc(s("f_ready"), 1)
                return body

            def down_body(q):
                job = jobs[f"w_down{q}"]

                def body(i, u, part):
                    banks, _ = group_done(dve, job, i, u)
                    g = i * job.unroll + u
                    dve.wait_ge(s("down_added"), 8 * q + g)
                    fold(dve, tmp[:, u, 0:2 * T].rearrange("p (a t) -> p a t", a=2), banks).then_inc(s("down"), 1)
                    dve.wait_ge(s("down"), 8 * q + g + 1)
                    dve.sem_inc(acc_free, 1)
                return body
            for q in range(4):
                splitting(f"w_up{q}", up_body(q), 3)
                splitting(f"w_down{q}", down_body(q))
                dve.wait_ge(s("down_added"), 1 + 8 * q + 8)
            inverse_std(T, 1.0 / D, EPS)
            for k in range(KT):
                v = tmp[:, k % 2, 0:T]
                link(dve.scalar_tensor_tensor(out=v, in0=y[:, k, :], scalar=column("g_post_mlp_2", k), in1=rstd[:, 0:T], op0=ALU.mult, op1=ALU.mult))
                dve.tensor_tensor(y[:, k, :], h1[:, k, META:TM], v, ALU.add).then_inc(s("final"), 1)


_NAMES = ["x", "mem", "norm_g", "w_in", "kv_norm_g", "w_kv_up", "idx_k_ln_g", "idx_k_ln_b", "q_norm_a", "k_norm_a",
          "q_norm_b", "k_norm_b", "sinks_b", "mem_norm_g", "w_mem_kv", "q_norm_c", "k_norm_c", "w_up_a", "w_up_b",
          "w_up_c", "gate_bias", "w_o", "rel_bias", "meta_2", "g_pre_mix_2", "w_in_2", "w_pool_grp_2", "pool_scale_2",
          "w_pool_out_2", "w_dw_2", "b_dw_2", "conv_ln_g_2", "conv_ln_b_2", "w_conv_out_2", "w_o_2", "g_post_mix_2",
          "g_pre_mlp_2", "w_up_2", "w_down_2", "g_post_mlp_2"]


def kernel(**inputs):
    import concourse.bacc as bacc
    from concourse.bass_utils import run_bass_kernel_spmd

    nc = bacc.Bacc("TRN2", target_bir_lowering=False, num_devices=1)
    arrays, views = {}, {}
    for name in _NAMES:
        a = np.ascontiguousarray(inputs[name])
        arrays[f"in_{name}"] = a
        views[name] = nc.dram_tensor(f"in_{name}", a.shape, mybir.dt.from_np(a.dtype), kind="ExternalInput").ap()
    out = nc.dram_tensor("out", (1, T, D), F32, kind="ExternalOutput").ap()
    build(nc, views, out)
    return run_bass_kernel_spmd(nc, [arrays], core_ids=[0]).results[0]["out"]
```

```python
import math
from contextlib import ExitStack

import numpy as np
import concourse.bass as bass
from concourse import mybir

F32 = mybir.dt.float32
F32R = mybir.dt.float32r
ALU = mybir.AluOpType
ACT = mybir.ActivationFunctionType
AX = mybir.AxisListType.X

P = 128
D = 2048
KT = D // P
T = 256
META = 16
TM = T + META
A_HEADS, B_HEADS, C_HEADS = 6, 12, 4
IDX_HEADS, IDX_DIM, B_DIM = 16, 64, 64
TOPK = min(256, T // 4)
WINDOW = 128
BUCKETS, MAX_DISTANCE = 32, 128
KV_RANK = 256
A_W, B_W, C_W = 768, 768, 512
POOL_W = CONV_W = 1024
TAPS = 31
D_FF = 4 * D
EPS, LN_EPS = 1e-6, 1e-5
NEG = -1.0e30
TAKEN = -3.0e38

GROUP = 256
SLAB = 4
STAGES = 8
PAIRS = 4

A_CKV, I_Q, I_K = 768, 1024, 2048
A_GATE = 2128
MIX = 5712
E_AQ, E_CKV, E_IQ = 0, 6, 8
L_AGATE, L_BQ, L_BK, L_BV, L_BGATE, L_CQ, L_CGATE = 0, 6, 12, 13, 14, 20, 24

ROWS0 = [("gate_bias", 48), ("norm_g", 16), ("mem_norm_g", 16), ("g_pre_mix_2", 16), ("g_post_mix_2", 16), ("g_pre_mlp_2", 16)]
ROWS1 = [("g_post_mlp_2", 16), ("pool_scale_2", 8), ("b_dw_2", 8), ("conv_ln_g_2", 8), ("conv_ln_b_2", 8), ("kv_norm_g", 2),
         ("q_norm_a", 1), ("k_norm_a", 1), ("q_norm_c", 1), ("k_norm_c", 1)]
HALF_ROWS = ["q_norm_b", "k_norm_b", "idx_k_ln_g", "idx_k_ln_b"]
DW_ROWS = TAPS * (CONV_W // P)
COL, _at = {}, 0
for _name, _n in ROWS0 + ROWS1 + [(n, 1) for n in HALF_ROWS] + [("w_dw_2", DW_ROWS)]:
    COL[_name] = _at
    _at += _n
N0 = sum(n for _, n in ROWS0)
N1 = sum(n for _, n in ROWS1) + len(HALF_ROWS)
PARAM_GROUPS = [(0, N0), (N0, N1), (N0 + N1, DW_ROWS // 2), (N0 + N1 + DW_ROWS // 2, DW_ROWS // 2)]
PARAMS = _at

DVE_TILES = 6
POOL_ORDER = (3, 2, 1, 0)

KB = 1024


def bucket_starts():
    n = np.arange(T, dtype=np.int32)
    exact = BUCKETS // 2
    nf = np.maximum(n, 1).astype(np.float32)
    large = exact + (np.log(nf / np.float32(exact)) / np.float32(math.log(MAX_DISTANCE / exact))
                     * np.float32(BUCKETS - exact)).astype(np.int32)
    b = np.where(n < exact, n, np.minimum(large, BUCKETS - 1))
    return [int(np.argmax(b == k)) for k in range(BUCKETS)] + [T]


class Chain:

    def __init__(self, eng, sem):
        self.eng, self.sem, self.n, self.term = eng, sem, 0, 0

    def __call__(self, ins):
        ins.then_inc(self.sem, 1)
        self.n += 1
        self.eng.wait_ge(self.sem, self.n + self.term)


def repeat(eng, count, unroll, body, chain=None, links=0):
    whole = count // unroll
    start = 0
    if whole >= 2:
        n0 = chain.n if chain else 0
        with eng.Fori(0, whole) as i:
            if chain:
                chain.term = i * links
            for u in range(unroll):
                body(i, u)
        if chain:
            assert chain.n - n0 == links, (chain.n - n0, links)
            chain.n, chain.term = n0 + whole * links, 0
        start = whole * unroll
    for s in range(start, count):
        body(s // unroll, s % unroll)


class Part:

    def __init__(self, w, col0, slabs, rhs, ready=None, wide=False, cols=GROUP, stride=GROUP, row0=0):
        self.w, self.col0, self.slabs, self.rhs, self.wide, self.cols, self.stride, self.row0 = w, col0, slabs, rhs, wide, cols, stride, row0
        self.ready = ready


class Job:

    def __init__(self, steps, parts, unroll):
        self.steps, self.parts, self.unroll = steps, parts, unroll
        self.pieces = [(p, pn, sum(p.slabs[:q]), kt, q == len(p.slabs) - 1) for pn, p in enumerate(parts) for q, kt in enumerate(p.slabs)]
        self.S = len(self.pieces)

    def place(self, slab0, group0):
        self.slab0, self.group0 = slab0, group0
        return slab0 + self.steps * self.S, group0 + self.steps * len(self.parts)

    def slab(self, i, u, idx):
        n = self.slab0 + u * self.S + idx
        return n + i * (self.unroll * self.S), n

    def group(self, i, u, part):
        g = self.group0 + u * len(self.parts) + part
        last = self.slab0 + u * self.S + sum(len(p.slabs) for p in self.parts[:part + 1]) - 1
        return g + i * (self.unroll * len(self.parts)), g % 2, last + i * (self.unroll * self.S)


def build(nc, A, out):
    ctx = ExitStack()
    with ctx:
        ctx.enter_context(nc.sbuf_tensor("arena", [P, 53200], F32))
        BASE = 16512

        def at(name, kb, shape, dt=F32):
            return nc.alloc_sbuf_tensor_at(name, shape, dt, offset=BASE + int(kb * KB))

        def sem(name):
            return ctx.enter_context(nc.semaphore(name))

        stage = at("stage", 0, [P, STAGES, SLAB, GROUP])
        w_high = at("w_high", 32, [P, PAIRS, SLAB, GROUP], F32R)
        w_low = at("w_low", 48, [P, PAIRS, SLAB, GROUP], F32R)
        params = at("params", 64, [P, PARAMS])
        ident = at("ident", 66, [P, P])
        ones = at("ones", 66.5, [P, P])
        blocks = at("blocks", 67, [P, P])
        center = at("center", 67.5, [IDX_DIM, P])
        square = at("square", 68, [P, 2, 2 * TM])
        sumsq = at("sumsq", 72.25, [P, 2, TM])
        rstd = at("rstd", 74.5, [P, 2 * T])
        tmp = at("tmp", 76.5, [P, 2, 2 * TM])
        gate = at("gate", 80.75, [P, 2, 2 * TM])
        Z = 85
        hT = at("hT", Z, [P, KT, 2, T], F32R)
        late = at("late", Z + 32, [P, 28, T])
        mem_pair = at("mem_pair", Z + 32, [P, KT, 2, T], F32R)
        mkv = at("mkv", Z + 114, [P, 8, T])
        mem_in = at("mem_in", Z + 64, [P, 2, D])
        x_in = at("x_in", Z + 80, [P, 2, D])
        turned = at("turned", Z + 96, [P, KT, T])
        toep = at("toep", Z + 60, [P, A_HEADS + B_HEADS, T])
        early = at("early", Z + 78, [P, 16, T])
        flip = at("flip", Z + 113, [P, P])
        ikw = at("ikw", Z + 94, [P, T])
        akv = at("akv", Z + 95, [P, 12, T])
        ckv_pair = at("ckv_pair", Z + 107, [P, 2, 2, T], F32R)
        v_a = at("v_a", Z + 86, [P, 2, A_W])
        v_b = at("v_b", Z + 111, [P, 2, P])
        v_c = at("v_c", Z + 107, [P, 2, C_W])
        ptb = at("ptb", 76.5, [P, 2, 2 * T])
        lg = at("lg", 80.75, [P, 2, 2 * T])
        ptb_bc = at("ptb_bc", Z + 60, [P, 2, 2 * T])
        lg_bc = at("lg_bc", Z + 118, [P, 2, 2 * T])
        bias_mask = [at("bias_mask0", Z + 84, [P, 3 * P]), at("bias_mask1", Z + 92, [P, 3 * P])]
        score = at("score", Z + 111, [P, 3 * P])
        work = at("work", Z + 112.5, [P, 3 * P])
        ikn = at("ikn", 72.25, [P, T])
        bk_swap = at("bk_swap", 73.25, [P, T])
        small = at("small", 65.71875, [P, 72])
        merged = at("merged", Z + 78, [P, KT, T])
        o_pair = at("o_pair", Z + 94, [P, 6, 2, T], F32R)
        merged_pair = at("merged_pair", Z + 32, [P, KT, 2, T], F32R)
        xT = at("xT", Z + 106, [P, KT, T])
        h1 = at("h1", Z, [P, KT, TM])
        uT = at("uT", Z + 17, [P, KT, 2, TM], F32R)
        m = at("m", Z + 52, [P, KT, T])
        d_pair = at("d_pair", Z + 68, [P, 8, 2, T], F32R)
        y_pair = at("y_pair", Z + 68, [P, 8, 2, T], F32R)
        glu = at("glu", Z + 84, [P, 8, TAPS - 1 - META + TM])
        conv = at("conv", Z + 93, [P, 8, T])
        z_pool = at("z_pool", Z + 101.25, [P, 8, TM])
        window = at("window", Z + 109.75, [P, 2, 2 * TM])
        product = at("product", Z + 118, [P, 2, T])
        conv_pair = at("conv_pair", Z + 101.25, [P, 8, 2, T], F32R)
        m_pair = at("m_pair", Z + 68, [P, KT, 2, T], F32R)
        mixed = at("mixed", Z + 52, [P, KT, T])
        u2 = at("u2", Z + 17, [P, KT, 2, T], F32R)
        f_pair = at("f_pair", Z + 84, [P, KT, 2, T], F32R)
        y = at("y", Z + 52, [P, KT, T])
        rows_out = at("rows_out", Z + 68, [P, 2, D])
        prow = at("prow", Z, [P, 4, P])
        meta_in = at("meta_in", Z + 17, [META, D])
        relb = at("relb", Z + 2, [BUCKETS, A_HEADS + B_HEADS])
        relT = at("relT", Z + 2.5, [A_HEADS + B_HEADS, BUCKETS])
        brow = at("brow", Z + 3, [A_HEADS + B_HEADS, 2 * T])
        zrow = at("zrow", Z + 5, [A_HEADS + B_HEADS, 2 * T])

        acc = ctx.enter_context(nc.psum_tensor("acc", [P, 4, 512], F32))
        aux = ctx.enter_context(nc.psum_tensor("aux", [P, 4, 512], F32))
        spill_x = nc.dram_tensor("spill_x", [P, KT, T], F32, kind="Internal").ap()
        NB = A_HEADS + B_HEADS
        bias_dram = nc.dram_tensor("bias_rows", [NB, 2 * T], F32, kind="Internal")

        iw = small[:, 0:32].rearrange("p (t h) -> p t h", t=2)
        negmax = small[:, 32:36].rearrange("p (b t) -> p b t", b=2)
        denom = small[:, 36:40].rearrange("p (b t) -> p b t", b=2)
        top8 = small[:, 40:56].rearrange("p (t e) -> p t e", t=2)
        sinks = small[:, 56:68]
        esink = small[:, 68:72].rearrange("p (b t) -> p b t", b=2)

        landed = [sem(f"landed{s}") for s in range(STAGES)]
        issued, high_done, split_done, used, acc_free = sem("issued"), sem("high_done"), sem("split_done"), sem("used"), sem("acc_free")
        act_link, dve_link, pool_link = sem("act_link"), sem("dve_link"), sem("pool_link")
        S = {}

        def s(name):
            if name not in S:
                S[name] = sem(name)
            return S[name]

        starts = bucket_starts()

        A = {n: (v[0] if v.shape[0] == 1 else v) for n, v in A.items()}

        def column(name, k=0):
            return params[:, COL[name] + k:COL[name] + k + 1]
        def tiles_of(src, first, n):
            return src[:, first:first + n, :].rearrange("p a t -> p (a t)")

        def norm(src, first, n, mat, inv, group, gain, both=False):
            return (tiles_of(src, first, n), n * T, mat, inv, both, group, COL[gain])

        HEAD_NORMS = [(ikn[:], T, blocks, 1.0 / IDX_DIM, False, ("ikw", 0), COL["idx_k_ln_g"])]
        HEAD_NORMS += [norm(mkv, r, 2, ones, 1.0 / P, ("mem_kv", 3), "k_norm_c") for r in (0, 2)]
        HEAD_NORMS += [norm(early, E_AQ + r, 2, ones, 1.0 / P, ("early", r // 2), "q_norm_a") for r in (0, 2, 4)]
        HEAD_NORMS += [norm(early, E_CKV, 2, ones, 1.0 / KV_RANK, ("early", 3), "kv_norm_g", True)]
        HEAD_NORMS += [norm(akv, r, 2, ones, 1.0 / P, ("kv_up", r // 2), "k_norm_a") for r in (0, 2, 4)]
        HEAD_NORMS += [norm(late, L_BQ + r, 2, blocks, 1.0 / B_DIM, ("late", (L_BQ + r) // 2), "q_norm_b") for r in (0, 2, 4)]
        HEAD_NORMS += [norm(late, L_BK, 1, blocks, 1.0 / B_DIM, ("late", L_BK // 2), "k_norm_b")]
        HEAD_NORMS += [norm(late, L_CQ + r, 2, ones, 1.0 / P, ("late", (L_CQ + r) // 2), "q_norm_c") for r in (0, 2)]
        NORM_AT = {"early": {1: 0, 3: 1, 5: 2, 8: 3, 10: 4, 12: 5, 16: 6},
                   "late": {2: 7, 4: 8, 6: 9, 40: 10, 42: 11, 44: 12, 46: 13, 50: 14, 52: 15}}
        NORMS_A, NORMS_ALL = 10, 16
        FLIP_AT = 7
        INDEX_AT = {"early": {21: 0, 22: 2, 25: 4, 26: 6, 29: 8, 30: 10}, "late": {0: 12, 1: 14}}
        TOPK_AT = 3
        VALUES_AT = {3 + v: v for v in range(6)}
        VALUES_AT.update({41: 6, 43: 7, 44: 8, 47: 9, 48: 10})
        HEADS = [("A", h) for h in range(A_HEADS)] + [("C", h) for h in range(C_HEADS)] + [("B", h) for h in range(B_HEADS)]
        HEAD_AT = {"late": {12 + 4 * h: h for h in range(6)},
                   "w_up_a": {4 * h: 6 + h for h in range(11)},
                   "w_up_c": {6 + 4 * h: 17 + h for h in range(5)}}
        SILU_AT = 48

        def stages(table, n, lag):
            return table.get(n - lag)

        WIDTHS = [T, T, TM, T, T, T, T]

        def head_cols(kind, t):
            if kind == "C":
                return t * T, (t + 1) * T
            return (0, P) if t == 0 else (P, 3 * P)

        def logits_of(n):
            a, b = (lg, ptb) if HEADS[n][0] == "A" else (lg_bc, ptb_bc)
            width = 4 * P if HEADS[n][0] == "C" else 3 * P
            return a[:, n % 2, 0:width], b[:, n % 2, 0:width], width

        LN_SLAB = 38

        full = [4, 4, 4, 4]

        def rhs_of(pair):
            return lambda k: (pair[:, k, :, :], pair[:, k, 0, :])

        def u_tokens(k):
            return uT[:, k, :, META:TM], uT[:, k, 0, META:TM]

        jobs = {}
        order = [
            ("mem_kv", Job(4, [Part(A["w_mem_kv"], 0, full, rhs_of(mem_pair), ("pair_ready", 0))], 2)),
            ("ikw", Job(1, [Part(A["w_in"], I_K, full, rhs_of(hT), ("pair_ready", 8), cols=P)], 2)),
            ("early", Job(8, [Part(A["w_in"], 0, full, rhs_of(hT))], 2)),
            ("kv_up", Job(6, [Part(A["w_kv_up"], 0, [2], rhs_of(ckv_pair), ("ckv_ready", 0))], 8)),
            ("late", Job(14, [Part(A["w_in"], A_GATE, full, rhs_of(hT))], 2)),
        ]
        for w, b, slabs, before in (("w_up_a", 0, [3, 3], 0), ("w_up_c", 2, [2, 2], 3), ("w_up_b", 1, [3, 3], 5)):
            order.append((w, Job(8, [Part(A["w_in"], MIX + b * D, full, rhs_of(hT)),
                                     Part(A[w], 0, slabs, rhs_of(o_pair), ("o_split", before))], 4)))
        order += [
            ("w_o", Job(8, [Part(A["w_o"], 0, full, rhs_of(merged_pair), ("merged_ready", 0))], 2)),
        ]
        for name, col0, stride in (("values", POOL_W, GROUP), ("gates", POOL_W + CONV_W, GROUP), ("pools", POOL_W - GROUP, -GROUP)):
            order.append((name, Job(4, [Part(A["w_in_2"], col0, full, lambda k: (uT[:, k, 0, :], uT[:, k, 1, :]), ("pair_ready", 16),
                                             wide=True, stride=stride)], 2)))
        order += [
            ("pool_grp", Job(4, [Part(A["w_pool_grp_2"], 0, [2], rhs_of(d_pair), ("d_ready", 0), stride=0)], 8)),
            ("pool_out", Job(8, [Part(A["w_in_2"], POOL_W + 2 * CONV_W, full, u_tokens),
                                 Part(A["w_pool_out_2"], 0, [4, 4], rhs_of(y_pair), ("y_pair_ready", 0))], 4)),
            ("conv_out", Job(8, [Part(A["w_in_2"], POOL_W + 2 * CONV_W + D, full, u_tokens),
                                 Part(A["w_conv_out_2"], 0, [4, 4], rhs_of(conv_pair), ("conv_ready", 0))], 4)),
            ("w_o_2", Job(8, [Part(A["w_o_2"], 0, full, rhs_of(m_pair), ("m_ready", 0))], 2)),
        ]
        for q in range(4):
            order.append((f"w_up{q}", Job(8, [Part(A["w_up_2"], q * D, full, rhs_of(u2), ("pair_ready", 24))], 2)))
            order.append((f"w_down{q}", Job(8, [Part(A["w_down_2"], 0, full, rhs_of(f_pair), ("f_ready", 8 * q), row0=q * KT)], 2)))
        slab0 = group0 = 0
        for name, job in order:
            slab0, group0 = job.place(slab0, group0)
            jobs[name] = job
        names = [name for name, _ in order]

        stream_of_slabs = [(job, step, idx) for _, job in order for step in range(job.steps) for idx in range(job.S)]

        def load_slab(sp, job, i, u, idx):
            step = i * job.unroll + u
            n, n_static = job.slab(i, u, idx)
            p, _, k, kt, _ = job.pieces[idx]
            slot = n_static % STAGES
            sp.wait_ge(split_done, n + 1)
            sp.sem_inc(issued, 1)
            rows = slice((p.row0 + k) * P, (p.row0 + k + kt) * P)
            src = p.w[rows, bass.ds(p.col0 + step * p.stride, p.cols)] if p.stride else p.w[POOL_ORDER[step], :, :]
            sp.dma_start(stage[:, slot, 0:kt, 0:p.cols], src.rearrange("(k p) n -> p k n", p=P)).then_inc(landed[slot], 16)

        def round_high(act, job, i, u, idx):
            n, n_static = job.slab(i, u, idx)
            p, _, k, kt, _ = job.pieces[idx]
            slot, pr = n_static % STAGES, n_static % PAIRS
            act.wait_ge(landed[slot], 16 * (n_static // STAGES + 1) + i * (16 * (job.unroll * job.S // STAGES)))
            act.wait_ge(used, n + 1)
            act.activation(w_high[:, pr, 0:kt, 0:p.cols], stage[:, slot, 0:kt, 0:p.cols], ACT.Copy).then_inc(high_done, 1)

        def subtract_low(dve, job, i, u, idx):
            n, n_static = job.slab(i, u, idx)
            p, _, k, kt, _ = job.pieces[idx]
            slot, pr = n_static % STAGES, n_static % PAIRS
            dve.wait_ge(high_done, n + 1)
            dve.tensor_tensor(w_low[:, pr, 0:kt, 0:p.cols], stage[:, slot, 0:kt, 0:p.cols],
                              w_high[:, pr, 0:kt, 0:p.cols].bitcast(F32), ALU.subtract).then_inc(split_done, 1)

        def stream(eng, split, name, body=None, chain=None, links=0, beside=None):
            job = jobs[name]
            tail = -(-PAIRS // job.S)

            def step(i, u, known):
                for idx, (_, part, _, _, last) in enumerate(job.pieces):
                    ahead = u * job.S + idx + PAIRS
                    if known:
                        n = job.slab0 + i * job.unroll * job.S + ahead
                        if n < len(stream_of_slabs):
                            j2, s2, idx2 = stream_of_slabs[n]
                            split(eng, j2, s2 // j2.unroll, s2 % j2.unroll, idx2)
                    else:
                        split(eng, job, i, ahead // job.S, ahead % job.S)
                    if last and body:
                        body(i, u, part)
                    if beside:
                        beside((i * job.unroll + u) * job.S + idx)

            count = job.steps - tail
            looped = 0 if beside or count // job.unroll < 2 else count // job.unroll * job.unroll
            if looped:
                repeat(eng, looped, job.unroll, lambda i, u: step(i, u, False), chain, links * job.unroll)
            for n in range(looped, job.steps):
                step(n // job.unroll, n % job.unroll, True)

        def multiply(pe, job, i, u, beside=None):
            for idx, (p, part, k0, kt, last) in enumerate(job.pieces):
                n, n_static = job.slab(i, u, idx)
                if k0 == 0:
                    g, bank, _ = job.group(i, u, part)
                    pe.wait_ge(acc_free, g + 1)
                pr = n_static % PAIRS
                if p.ready:
                    name, before = p.ready
                    pe.wait_ge(s(name), before + ((0 if p.stride else 2 * u) + k0 + kt + 1) // 2)
                pe.wait_ge(split_done, STAGES + n + 1)
                for j in range(p.cols // P):
                    bk = acc[:, 2 * bank + j, :]
                    for k in range(kt):
                        first, final = k0 + k == 0, last and k == kt - 1
                        high, low = (w[:, pr, k, j * P:(j + 1) * P] for w in (w_high, w_low))
                        if p.wide:
                            a, b = p.rhs(k0 + k)
                            pe.matmul(bk[:, 0:TM], high, b, start=first, stop=False)
                            pe.matmul(bk[:, 0:TM], low, a, start=False, stop=False)
                            mm = pe.matmul(bk[:, 0:TM], high, a, start=False, stop=final)
                            continue
                        both, a = p.rhs(k0 + k if p.stride else 2 * POOL_ORDER[u] + k)
                        if first:
                            pe.matmul(bk, high, both, start=True, stop=False, skip_group_check=True)
                            pe.matmul(bk[:, 0:T], low, a, start=False, stop=False, skip_group_check=True)
                        else:
                            pe.matmul(bk[:, 0:T], low, a, start=False, stop=False, skip_group_check=True)
                            mm = pe.matmul(bk, high, both, start=False, stop=final, skip_group_check=True)
                mm.then_inc(used, 1)
                if beside:
                    beside((i * job.unroll + u) * job.S + idx)

        def group_done(eng, job, i, u, part=0):
            g, bank, last = job.group(i, u, part)
            eng.wait_ge(used, PAIRS + last + 1)
            return acc[:, 2 * bank:2 * bank + 2, :], g

        def folded(name, group):
            return 2 + jobs[name].group0 + group + 1

        def fold(dve, dst, banks):
            return dve.tensor_reduce(dst, banks.rearrange("p j (h t) -> p j t h", h=2), AX, ALU.add)

        block = ctx.enter_context(nc.Block())

        @block.sync
        def _(sp):
            def rows(name):
                v = A[name]
                return v.rearrange("(a n) -> a n", n=P)
            at_row = 0
            for group, members in enumerate((ROWS0, ROWS1)):
                at_row = 0
                for name, n in members:
                    sp.dma_start(prow[at_row:at_row + n, group, :], rows(name)).then_inc(s("params_in"), 16)
                    at_row += n
            for name in HALF_ROWS:
                for half in range(2):
                    sp.dma_start(prow[at_row:at_row + 1, 1, half * 64:half * 64 + 64], A[name].rearrange("(a n) -> a n", a=1)).then_inc(s("params_in"), 16)
                at_row += 1
            taps = A["w_dw_2"].rearrange("t (c n) -> (t c) n", n=P)
            for half in range(2):
                sp.dma_start(prow[0:DW_ROWS // 2, 2 + half, :], taps[half * DW_ROWS // 2:(half + 1) * DW_ROWS // 2, :]).then_inc(s("params_in"), 16)
            sp.dma_start(relb[:], A["rel_bias"]).then_inc(s("params_in"), 16)
            sp.dma_start(sinks, A["sinks_b"].partition_broadcast(P)).then_inc(s("sinks_in"), 16)
            sp.dma_start(mem_in[:], A["mem"].rearrange("(t p) d -> p t d", p=P)).then_inc(s("mem_in"), 16)
            sp.dma_start(x_in[:], A["x"].rearrange("(t p) d -> p t d", p=P)).then_inc(s("x_in"), 16)

            for name in names:
                job = jobs[name]
                repeat(sp, job.steps, job.unroll, lambda i, u: [load_slab(sp, job, i, u, idx) for idx in range(job.S)])
            for r in range(4):
                sp.wait_ge(s("rows_ready"), 2 * r + 2)
                for t in range(2):
                    sp.dma_start(out[0, t * P:(t + 1) * P, r * 512:(r + 1) * 512], rows_out[:, t, r * 512:(r + 1) * 512]).then_inc(s("stored"), 16)
            sp.wait_ge(s("stored"), 16 * 8)

        @block.gpsimd
        def _(pool):
            link = Chain(pool, pool_link)
            link(pool.memset(ones[:], 1.0))
            link(pool.memset(ident[:], 0.0))
            link(pool.affine_select(out=ident[:], in_=ident[:], compare_op=ALU.not_equal, fill=1.0, base=0,
                                    pattern=[[-1, P]], channel_multiplier=1))
            link(pool.memset(blocks[:], 0.0))
            link(pool.memset(blocks[0:64, 0:64], 1.0))
            link(pool.memset(blocks[64:128, 64:128], 1.0))
            link(pool.memset(zrow[:], 0.0))
            pool.sem_inc(s("consts"), 1)

            def gather_squares(count, first, width=2 * T, done=0):
                view = sumsq.rearrange("p a t -> p (a t)")[:, 0:width]
                for r in range(count):
                    q = first + r
                    pool.wait_ge(s("squared"), q + 1)
                    if r == 0:
                        pool.tensor_copy(view, square[:, q % 2, 0:width]).then_inc(s("gathered"), 1)
                    else:
                        pool.wait_ge(s("gathered"), q)
                        pool.tensor_tensor(view, view, square[:, q % 2, 0:width], ALU.add).then_inc(s("gathered"), 1)

            pool.wait_ge(s("bias_rows"), 1)
            pool.dma_start(bias_dram.ap(), brow[:]).then_inc(s("bias_out"), 16)
            gather_squares(8, 0)
            pool.wait_ge(s("stats"), 1)
            gather_squares(8, 8)
            pool.wait_ge(s("turned_pe"), 16)
            link(pool.memset(flip[:], 0.0))
            pool.affine_select(out=flip[:], in_=flip[:], compare_op=ALU.not_equal, fill=1.0, base=1 - P,
                               pattern=[[1, P]], channel_multiplier=1).then_inc(s("flip_made"), 1)
            pool.wait_ge(s("turned_done"), 16)
            pool.dma_start(spill_x, turned[:]).then_inc(s("x_out"), 16)
            pool.wait_ge(s("bias_out"), 16)
            pool.wait_ge(used, PAIRS + jobs["ikw"].slab0)
            pool.dma_start(toep[:], bass.AP(bias_dram, 0, [[1, P], [2 * T, NB], [1, T]])).then_inc(s("toep_in"), 16)
            pool.wait_ge(s("flip_copied"), NB // 2)
            pool.affine_select(out=toep[:], in_=toep[:], compare_op=ALU.is_ge, fill=NEG, base=P,
                               pattern=[[0, NB], [-1, T]], channel_multiplier=1).then_inc(s("toep_masked"), 1)
            pool.wait_ge(s("toep_masked"), 1)
            tb = toep[:, A_HEADS:NB, :]
            pool.affine_select(out=tb, in_=tb, compare_op=ALU.is_ge, fill=NEG, base=WINDOW - 1 - P,
                               pattern=[[0, B_HEADS], [1, T]], channel_multiplier=-1).then_inc(s("toep_masked"), 1)
            pool.wait_ge(s("scored"), 1)
            for t in range(2):
                v = score[:, t * P:t * P + P * (t + 1)]
                pool.affine_select(out=v, in_=v, compare_op=ALU.is_ge, fill=NEG, base=t * P,
                                   pattern=[[-1, P * (t + 1)]], channel_multiplier=1).then_inc(s("score_masked"), 1)
            pool.wait_ge(s("topk"), 1)
            pool.wait_ge(s("toep_masked"), 2)
            for h in range(A_HEADS):
                if h >= 2:
                    pool.wait_ge(s("logits"), h - 1)
                mk = bias_mask[h % 2]
                pool.tensor_tensor(mk[:, 0:P], toep[:, h, P:T], work[:, 0:P], ALU.add).then_inc(s("masked"), 1)
                pool.tensor_tensor(mk[:, P:3 * P], toep[:, h, :], work[:, P:3 * P], ALU.add).then_inc(s("masked"), 1)

            pool.wait_ge(s("head_normed"), 14)
            pool.dma_start(bk_swap[0:64, :], late[64:128, L_BK, :]).then_inc(s("swapped"), 16)
            pool.dma_start(bk_swap[64:128, :], late[0:64, L_BK, :]).then_inc(s("swapped"), 16)

            def gated(first, src, gates, tiles):
                for r in range(tiles // 2):
                    q = first + r
                    pool.wait_ge(s("gate_sig"), q + 1)
                    v = gate[:, q % 2, 0:2 * T]
                    g2 = late[:, gates + 2 * r:gates + 2 * r + 2, :].rearrange("p a t -> p (a t)")
                    o2 = src[:, 2 * r:2 * r + 2, :].rearrange("p a t -> p (a t)")
                    link(pool.tensor_tensor(v, v, g2, ALU.mult))
                    pool.tensor_tensor(v, v, o2, ALU.mult).then_inc(s("gated"), 1)

            def merge(name, dst, steps0, add, beside=None):
                job = jobs[name]

                def body(i, u):
                    n = steps0 + i
                    pool.wait_ge(s("sig_ready"), n + 1)
                    pool.wait_ge(s("up_ready"), n + 1)
                    d2 = dst[:, bass.ds(i * 2, 2), :].rearrange("p a t -> p (a t)")
                    if add:
                        link(pool.tensor_tensor(gate[:, 1, 0:2 * T], gate[:, 0, 0:2 * T], tmp[:, 1, 0:2 * T], ALU.mult))
                        pool.tensor_tensor(d2, d2, gate[:, 1, 0:2 * T], ALU.add).then_inc(s("merged_step"), 1)
                    else:
                        pool.tensor_tensor(d2, gate[:, 0, 0:2 * T], tmp[:, 1, 0:2 * T], ALU.mult).then_inc(s("merged_step"), 1)
                    if beside:
                        beside(i)
                if beside:
                    for i in range(job.steps):
                        body(i, 0)
                else:
                    repeat(pool, job.steps, 1, body, link, 1 if add else 0)

            gated(0, early[:, E_AQ:E_AQ + 6, :], L_AGATE, 6)
            merge("w_up_a", merged, 0, False)
            gated(3, late[:, L_CQ:L_CQ + 4, :], L_CGATE, 4)
            merge("w_up_c", merged, 8, True)
            pool.wait_ge(s("x_out"), 16)
            pool.wait_ge(s("pv_copied"), len(HEADS))
            pool.dma_start(xT[:], spill_x).then_inc(s("x_back"), 16)
            gated(5, late[:, L_BQ:L_BQ + 6, :], L_BGATE, 6)
            merge("w_up_b", merged, 16, True)

            def add_square(q, parity, first=False):
                pool.wait_ge(s("squared"), q + 1)
                sq = square[:, parity, 0:2 * T].rearrange("p (a t) -> p a t", a=2)
                if first:
                    pool.tensor_copy(sumsq[:, :, META:TM], sq).then_inc(s("gathered"), 1)
                else:
                    pool.wait_ge(s("gathered"), q)
                    pool.tensor_tensor(sumsq[:, :, META:TM], sumsq[:, :, META:TM], sq, ALU.add).then_inc(s("gathered"), 1)

            pool.wait_ge(s("merged_ready"), 8)
            pool.dma_start(meta_in[:], A["meta_2"]).then_inc(s("meta_in"), 16)
            pool.wait_ge(s("x_back"), 16)
            for g in range(8):
                pool.wait_ge(s("folded"), g + 1)
                pool.tensor_tensor(h1[:, 2 * g:2 * g + 2, META:TM], tmp[:, g % 2, 0:2 * T].rearrange("p (a t) -> p a t", a=2),
                                   xT[:, 2 * g:2 * g + 2, :], ALU.add).then_inc(s("residual"), 1)
                if g >= 1:
                    add_square(16 + g - 1, (g - 1) % 2, g == 1)
            add_square(23, 1)
            pool.wait_ge(s("values_moved"), 4)
            for g in range(4):
                pool.wait_ge(s("glu_sig"), g + 1)
                v = glu[:, 2 * g:2 * g + 2, TAPS - 1 - META:]
                pool.tensor_tensor(v, v, gate[:, g % 2, :].rearrange("p (a t) -> p a t", a=2), ALU.mult).then_inc(s("glu_done"), 1)
            pool.wait_ge(s("glu_done"), 4)

            taps_done = [0]
            mine = range(DVE_TILES, 8)

            def conv_taps(count):
                for _ in range(count):
                    n = taps_done[0]
                    if n == len(mine) * TAPS:
                        return
                    taps_done[0] += 1
                    tap, k = n // len(mine), mine[n % len(mine)]
                    w = column("w_dw_2", 8 * tap + k)
                    if tap == 0:
                        ins = pool.tensor_scalar(conv[:, k, :], glu[:, k, 0:T], w, column("b_dw_2", k), ALU.mult, ALU.add)
                    else:
                        link(pool.tensor_scalar(product[:, n % 2, :], glu[:, k, tap:tap + T], w, None, ALU.mult))
                        pool.wait_ge(s("pool_taps"), n - len(mine) + 1)
                        ins = pool.tensor_tensor(conv[:, k, :], conv[:, k, :], product[:, n % 2, :], ALU.add)
                    ins.then_inc(s("pool_taps"), 1)

            for q, g in enumerate(POOL_ORDER):
                pool.wait_ge(s("pooled"), q + 1)
                src = z_pool[:, 2 * g:2 * g + 2, :]
                reach = 1
                for r in range(g + 1):
                    dst = window[:, r % 2, :].rearrange("p (a t) -> p a t", a=2)
                    link(pool.tensor_tensor(dst[:, :, 2 * reach - 1:TM], src[:, :, 2 * reach - 1:TM], src[:, :, reach - 1:TM - reach], ALU.add))
                    src = dst
                    reach *= 2
                v = window[:, (g + 1) % 2, 0:2 * T].rearrange("p (a t) -> p a t", a=2)
                link(pool.tensor_scalar(v, src[:, :, META:TM], 1.0 / reach, None, ALU.mult))
                link(pool.tensor_tensor(v, v, z_pool[:, 2 * g:2 * g + 2, META:TM], ALU.subtract))
                link(pool.tensor_copy(d_pair[:, 2 * g:2 * g + 2, 0, :], v))
                link(pool.tensor_tensor(d_pair[:, 2 * g:2 * g + 2, 1, :], v, d_pair[:, 2 * g:2 * g + 2, 0, :].bitcast(F32), ALU.subtract))
                pool.sem_inc(s("d_ready"), 1)
                conv_taps(4 if q < 3 else 20)
            merge("pool_out", m, 24, False, lambda n: conv_taps(5))
            conv_taps(8 * TAPS)
            merge("conv_out", m, 32, True)
            for g in range(8):
                add_square(24 + g, g % 2, g == 0)
            pool.wait_ge(s("stats"), 4)
            for g in range(8):
                add_square(32 + g, g % 2, g == 0)

            def add_down(q):
                job = jobs[f"w_down{q}"]

                def body(i, u):
                    g = i * job.unroll + u
                    pool.wait_ge(s("down"), q * 8 + g + 1)
                    d2 = y[:, bass.ds(g * 2, 2), :].rearrange("p a t -> p (a t)")
                    pool.tensor_tensor(d2, d2, tmp[:, u, 0:2 * T], ALU.add).then_inc(s("down_added"), 1)
                repeat(pool, job.steps, job.unroll, body)

            pool.wait_ge(s("h2"), 16)
            pool.memset(y[:], 0.0).then_inc(s("y_zero"), 1)
            pool.wait_ge(s("y_zero"), 1)
            pool.sem_inc(s("down_added"), 1)
            for q in range(4):
                add_down(q)
            pool.wait_ge(s("stats"), 5)
            for g in range(8):
                add_square(40 + g, g % 2, g == 0)

        @block.scalar
        def _(act):
            def rounding(name, body=None, beside=None):
                stream(act, round_high, name, body, beside=beside)

            std = [0]

            def root():
                std[0] += 1
                act.wait_ge(s("variance"), std[0])
                act.activation(rstd[:, 0:WIDTHS[std[0] - 1]], rstd[:, 0:WIDTHS[std[0] - 1]], ACT.Sqrt).then_inc(s("root"), 1)

            def high_parts(pair, width, first, sl=slice(None)):
                for r in range(8):
                    act.wait_ge(s("scaled"), first + r + 1)
                    act.activation(pair[:, 2 * r:2 * r + 2, 0, :], tmp[:, r % 2, 0:2 * width].rearrange("p (a t) -> p a t", a=2),
                                   ACT.Copy).then_inc(s("pair_high"), 1)

            for e in range(16):
                act.wait_ge(s("turned_pe"), e + 1)
                if e == 8:
                    act.wait_ge(s("pair_ready"), 8)
                act.activation(turned[:, 2 * (e % 8):2 * (e % 8) + 2, :], aux[:, e % 4, :].rearrange("p (a t) -> p a t", a=2),
                               ACT.Copy).then_inc(s("turned_done"), 1)
                if e >= 2:
                    act.wait_ge(s("gathered"), e - 1)
                act.activation(square[:, e % 2, 0:2 * T], aux[:, e % 4, :], ACT.Square).then_inc(s("squared"), 1)
                if e == 7:
                    root()
                    high_parts(mem_pair, T, 0)
                    act.wait_ge(s("stats"), 1)
            root()
            high_parts(hT, T, 8)
            for n in range(PAIRS):
                round_high(act, jobs["mem_kv"], 0, 0, n)
            rounding("mem_kv")
            rounding("ikw")

            def norm_steps(name, n):
                q = stages(NORM_AT[name], n, 0)
                if q is not None:
                    src, width, _, _, _, (job, group), _ = HEAD_NORMS[q]
                    if q == 0:
                        act.wait_ge(s("ik_copied"), 1)
                    act.wait_ge(acc_free, folded(job, group))
                    if q >= 1:
                        act.wait_ge(s("head_stats"), q)
                    act.activation(square[:, 0, 0:width], src, ACT.Square).then_inc(s("head_squared"), 1)
                q = stages(NORM_AT[name], n, 2)
                if q is not None:
                    w = T if HEAD_NORMS[q][4] else HEAD_NORMS[q][1]
                    act.wait_ge(s("head_var"), q + 1)
                    act.activation(rstd[:, 0:w], rstd[:, 0:w], ACT.Sqrt).then_inc(s("head_root"), 1)

            def index_steps(name, n):
                first = stages(INDEX_AT[name], n, 0)
                for h in () if first is None else (first, first + 1):
                    act.wait_ge(s("idx_products"), h + 1)
                    if h >= 2:
                        act.wait_ge(s("idx_added"), 2 * (h - 1))
                    act.activation(lg[:, h % 2, 0:3 * P], aux[:, 2 + h % 2, 0:3 * P], ACT.Relu).then_inc(s("idx_relu"), 1)

            def head_steps(name, n):
                h = stages(HEAD_AT[name], n, 1)
                if h is not None:
                    kind, c = HEADS[h]
                    l, _, _ = logits_of(h)
                    b = h % 2
                    act.wait_ge(s("logits"), h + 1)
                    for t in range(2):
                        lo, hi = head_cols(kind, t)
                        act.activation(l[:, lo:hi], l[:, lo:hi], ACT.Exp, bias=negmax[:, b, t:t + 1],
                                       accum_out=denom[:, b, t:t + 1]).then_inc(s("exps"), 1)
                    if kind == "B":
                        for t in range(2):
                            act.activation(esink[:, b, t:t + 1], sinks[:, c:c + 1], ACT.Exp, bias=negmax[:, b, t:t + 1]).then_inc(s("sink_exps"), 1)
                h = stages(HEAD_AT[name], n, 3)
                if h is not None:
                    _, turned_p, w = logits_of(h)
                    act.wait_ge(s("probs_turned"), h + 1)
                    if h >= 2:
                        act.wait_ge(s("pv"), h - 1)
                    act.activation(turned_p, aux[:, 2, 0:w], ACT.Copy).then_inc(s("probs_copied"), 1)

            def beside_early(n):
                norm_steps("early", n)
                if 0 <= n - FLIP_AT < NB // 2:
                    r = n - FLIP_AT
                    act.wait_ge(s("flipped"), r + 1)
                    act.activation(toep[:, 2 * r:2 * r + 2, :], aux[:, 2 + r % 2, :].rearrange("p (a t) -> p a t", a=2), ACT.Copy).then_inc(s("flip_copied"), 1)
                index_steps("early", n)

            def silu_step(q, gates, r):
                if q >= 2:
                    act.wait_ge(s("o_split"), q - 1)
                g2 = late[:, gates + 2 * r:gates + 2 * r + 2, :]
                act.activation(gate[:, q % 2, 0:2 * T].rearrange("p (a t) -> p a t", a=2), g2, ACT.Sigmoid).then_inc(s("gate_sig"), 1)

            def beside_late(n):
                index_steps("late", n)
                norm_steps("late", n)
                head_steps("late", n)
                if 0 <= n - SILU_AT < 3:
                    if n == SILU_AT:
                        act.wait_ge(s("probs_turned"), A_HEADS)
                    silu_step(n - SILU_AT, L_AGATE, n - SILU_AT)

            rounding("early", beside=beside_early)
            rounding("kv_up")
            rounding("late", beside=beside_late)

            def silu(first, steps, gates, tiles):
                act.wait_ge(s("merged_step"), steps)
                for r in range(tiles // 2):
                    silu_step(first + r, gates, r)

            def gate_groups(name, steps0, bias, beside=None):
                def body(i, u, part):
                    if part == 1:
                        return
                    i = i * jobs[name].unroll + u
                    n = steps0 + i
                    act.wait_ge(s("gate_in"), n + 1)
                    act.wait_ge(s("merged_step"), n)
                    for j in range(2):
                        b = params[:, bass.ds(COL["gate_bias"] + bias + i * 2 + j, 1)] if bias is not None else 0.0
                        act.activation(gate[:, 0, j * T:(j + 1) * T], tmp[:, 0, j * T:(j + 1) * T], ACT.Sigmoid,
                                       bias=b).then_inc(s("sig_half") if j == 0 else s("sig_ready"), 1)
                rounding(name, body, beside)

            gate_groups("w_up_a", 0, 0, lambda n: head_steps("w_up_a", n))
            silu(3, 8, L_CGATE, 4)
            gate_groups("w_up_c", 8, 32, lambda n: head_steps("w_up_c", n))
            silu(5, 16, L_BGATE, 6)
            gate_groups("w_up_b", 16, 16)

            def square_of(v, parity, q):
                act.wait_ge(s("gathered"), q - 1)
                act.activation(square[:, parity, 0:2 * T].rearrange("p (a t) -> p a t", a=2), v, ACT.Square).then_inc(s("squared"), 1)

            def sq_residual(i, u, part):
                g = 2 * i + u
                act.wait_ge(s("residual"), 2 + g + 1)
                square_of(h1[:, bass.ds(2 * g, 2), META:TM], u, 16 + g)
            rounding("w_o", sq_residual)
            root()
            high_parts(uT, TM, 16)

            rounding("values")

            def glu_body(i, u, part):
                g = 2 * i + u
                banks, _ = group_done(act, jobs["gates"], i, u)
                if g >= 2:
                    act.wait_ge(s("glu_done"), g - 1)
                act.activation(gate[:, g % 2, :].rearrange("p (a t) -> p a t", a=2), banks[:, :, 0:TM], ACT.Sigmoid).then_inc(s("glu_sig"), 1)
            rounding("gates", glu_body)
            rounding("pools")
            rounding("pool_grp")

            def layer_norm_steps(n):
                r = n - LN_SLAB - 2
                if 0 <= r < 4:
                    act.wait_ge(s("conv_centered"), r + 1)
                    if r >= 2:
                        act.wait_ge(s("conv_squares"), r - 1)
                    act.activation(square[:, r % 2, 0:2 * T], conv[:, 2 * r:2 * r + 2, :].rearrange("p a t -> p (a t)"), ACT.Square).then_inc(s("conv_sq"), 1)
                if r == 4:
                    root()
                if r == 5:
                    for q in range(4):
                        act.wait_ge(s("conv_scaled"), q + 1)
                        for k in (2 * q, 2 * q + 1):
                            act.activation(square[:, q % 2, (k % 2) * T:(k % 2 + 1) * T], conv[:, k, :], ACT.Sigmoid,
                                           bias=column("conv_ln_b_2", k), scale=column("conv_ln_g_2", k)).then_inc(s("conv_sig"), 1)
                            act.wait_ge(s("conv_sig"), k + 1)
                            act.activation(conv[:, k, :], conv[:, k, :], ACT.Identity,
                                           bias=column("conv_ln_b_2", k), scale=column("conv_ln_g_2", k)).then_inc(s("conv_affine"), 1)
                        if q >= 1:
                            conv_high(q - 1)
                    conv_high(3)

            def conv_high(q):
                act.wait_ge(s("conv_used"), q + 1)
                act.activation(conv_pair[:, 2 * q:2 * q + 2, 0, :], conv[:, 2 * q:2 * q + 2, :], ACT.Copy).then_inc(s("conv_high"), 1)

            gate_groups("pool_out", 24, None, layer_norm_steps)
            gate_groups("conv_out", 32, None)

            def sq_mixed(i, u, part):
                g = 2 * i + u
                act.wait_ge(s("mixed"), g + 1)
                square_of(mixed[:, bass.ds(2 * g, 2), :], u, 24 + g)
            rounding("w_o_2", sq_mixed)
            root()
            for g in range(8):
                act.wait_ge(s("h2"), 2 * g + 2)
                square_of(h1[:, 2 * g:2 * g + 2, META:TM], g % 2, 32 + g)
            root()
            high_parts(u2, T, 24)
            for q in range(4):
                rounding(f"w_up{q}")
                rounding(f"w_down{q}")
            for g in range(8):
                act.wait_ge(s("down_added"), 33)
                square_of(y[:, 2 * g:2 * g + 2, :], g % 2, 40 + g)
            root()
            for e in range(8):
                act.wait_ge(s("out_turned"), e + 1)
                r, t = e // 2, e % 2
                act.activation(rows_out[:, t, r * 512:(r + 1) * 512], aux[:, e % 4, :], ACT.Copy).then_inc(s("rows_ready"), 1)

        @block.tensor
        def _(pe):
            def products(name, beside=None):
                job = jobs[name]
                if beside:
                    for step in range(job.steps):
                        multiply(pe, job, step // job.unroll, step % job.unroll, beside)
                    return
                repeat(pe, job.steps, job.unroll, lambda i, u: multiply(pe, job, i, u))

            def stat(width, gathered):
                pe.wait_ge(s("gathered"), gathered)
                v = sumsq.rearrange("p a t -> p (a t)")
                for a in range(2):
                    mm = pe.matmul(aux[:, 0, 0:width], ones[:], v[:, a * width:(a + 1) * width], start=(a == 0), stop=(a == 1))
                mm.then_inc(s("stats"), 1)

            def stat_wide(width, gathered, lo):
                pe.wait_ge(s("gathered"), gathered)
                for a in range(2):
                    mm = pe.matmul(aux[:, 0, 0:width], ones[:], sumsq[:, a, lo:TM], start=(a == 0), stop=(a == 1))
                mm.then_inc(s("stats"), 1)

            pe.sem_inc(used, PAIRS)
            pe.wait_ge(s("consts"), 1)
            pe.wait_ge(s("params_in"), 16 * (len(ROWS0) + len(ROWS1) + 2 * len(HALF_ROWS) + 3))
            for q, (c0, n) in enumerate(PARAM_GROUPS):
                pe.transpose(aux[:, q, 0:n], prow[0:n, q, :], ident[0:n, 0:n])
            pe.transpose(aux[0:NB, 1, P:P + BUCKETS], relb[:], ident[0:BUCKETS, 0:BUCKETS]).then_inc(s("params_turned"), 1)
            pe.wait_ge(s("params_copied"), 5)
            for e in range(16):
                src = mem_in if e < 8 else x_in
                if e == 0:
                    pe.wait_ge(s("mem_in"), 16)
                if e == 8:
                    stat(T, 8)
                    pe.wait_ge(s("variance"), 1)
                    pe.wait_ge(s("x_in"), 16)
                if e >= 4:
                    pe.wait_ge(s("squared"), e - 3)
                for k in range(2):
                    for t in range(2):
                        kt = 2 * (e % 8) + k
                        mm = pe.transpose(aux[:, e % 4, (2 * k + t) * P:(2 * k + t + 1) * P], src[:, t, kt * P:(kt + 1) * P], ident[:])
                mm.then_inc(s("turned_pe"), 1)
            stat(T, 16)
            products("mem_kv")
            products("ikw")

            def norm_steps(name, n):
                q = stages(NORM_AT[name], n, 1)
                if q is None:
                    return
                _, width, mat, _, both, _, _ = HEAD_NORMS[q]
                pe.wait_ge(s("head_squared"), q + 1)
                if q >= 1:
                    pe.wait_ge(s("head_var"), q)
                if both:
                    for a in range(2):
                        mm = pe.matmul(aux[:, 1, 0:T], mat[:], square[:, 0, a * T:(a + 1) * T], start=(a == 0), stop=(a == 1))
                else:
                    mm = pe.matmul(aux[:, 1, 0:width], mat[:], square[:, 0, 0:width], start=True, stop=True)
                mm.then_inc(s("head_stats"), 1)

            def index_steps(name, n):
                first = stages(INDEX_AT[name], n, 0)
                for h in () if first is None else (first, first + 1):
                    pe.wait_ge(s("ik_ready"), 1)
                    pe.wait_ge(acc_free, folded("early", E_IQ // 2 + h // 4))
                    if h >= 2:
                        pe.wait_ge(s("idx_relu"), h - 1)
                    r = (h % 2) * 64
                    q = early[r:r + 64, E_IQ + h // 2, :]
                    pe.matmul(aux[:, 2 + h % 2, 0:P], q[:, 0:P], ikn[r:r + 64, 0:P], start=True, stop=True)
                    pe.matmul(aux[:, 2 + h % 2, P:3 * P], q[:, P:T], ikn[r:r + 64, :], start=True, stop=True).then_inc(s("idx_products"), 1)

            def beside_early(n):
                if n == 0:
                    pe.wait_ge(acc_free, folded("ikw", 0))
                    pe.wait_ge(s("center"), 2)
                    pe.matmul(aux[:, 1, 0:T], center[:], ikw[0:IDX_DIM, :], start=True, stop=True).then_inc(s("ik_centered"), 1)
                    for t in range(2):
                        mm = pe.transpose(aux[:, 2, t * P:(t + 1) * P], ikw[:, t * P:(t + 1) * P], ident[:])
                    mm.then_inc(s("iw_turned"), 1)
                norm_steps("early", n)
                if 0 <= n - FLIP_AT < NB // 2:
                    r = n - FLIP_AT
                    if r == 0:
                        pe.wait_ge(s("toep_in"), 16)
                        pe.wait_ge(s("flip_made"), 1)
                        pe.wait_ge(s("iw_ready"), 1)
                    if r >= 2:
                        pe.wait_ge(s("flip_copied"), r - 1)
                    pe.matmul(aux[:, 2 + r % 2, :], flip[:], toep[:, 2 * r:2 * r + 2, :], start=True, stop=True).then_inc(s("flipped"), 1)
                if n == FLIP_AT + NB // 2:
                    pe.wait_ge(s("flip_copied"), NB // 2)
                index_steps("early", n)

            def value_steps(n):
                v = VALUES_AT.get(n)
                if v is None:
                    return
                if v < 6:
                    src = akv[:, 6 + v, :]
                    pe.wait_ge(acc_free, folded("kv_up", 3 + v // 2))
                    pe.wait_ge(s("idx_relu"), IDX_HEADS)
                elif v == 6:
                    src = late[:, L_BV, :]
                    pe.wait_ge(acc_free, folded("late", L_BV // 2))
                    pe.wait_ge(s("pv_copied"), A_HEADS)
                else:
                    src = mkv[:, 4 + v - 7, :]
                if v >= 1:
                    pe.wait_ge(s("values_copied"), v)
                for t in range(2):
                    mm = pe.transpose(aux[:, 3, t * P:(t + 1) * P], src[:, t * P:(t + 1) * P], ident[:])
                mm.then_inc(s("values_turned"), 1)

            def head_logits(h):
                kind, c = HEADS[h]
                pe.wait_ge(s("head_normed"), NORMS_A if kind == "A" else NORMS_ALL)
                if h >= 1:
                    pe.wait_ge(s("logits"), h)
                if kind == "A":
                    q, k = early[:, E_AQ + c, :], akv[:, c, :]
                elif kind == "C":
                    q, k = late[:, L_CQ + c, :], mkv[:, c, :]
                else:
                    pe.wait_ge(s("swapped"), 32)
                    r = (c % 2) * 64
                    q = late[r:r + 64, L_BQ + c // 2, :]
                    k = late[r:r + 64, L_BK, :] if c // (B_HEADS // 2) == c % 2 else bk_swap[r:r + 64, :]
                for t in range(2):
                    lo, hi = head_cols(kind, t)
                    mm = pe.matmul(aux[:, 0, lo:hi], q[:, t * P:(t + 1) * P], k[:, 0:hi - lo], start=True, stop=True)
                mm.then_inc(s("qk"), 1)

            def turn_probs(h):
                l, _, w = logits_of(h)
                pe.wait_ge(s("probs"), h + 1)
                if h >= 1:
                    pe.wait_ge(s("probs_copied"), h)
                for c in range(w // P):
                    mm = pe.transpose(aux[:, 2, c * P:(c + 1) * P], l[:, c * P:(c + 1) * P], ident[:])
                mm.then_inc(s("probs_turned"), 1)

            def weigh_values(h):
                kind, c = HEADS[h]
                _, p, _ = logits_of(h)
                pe.wait_ge(s("probs_copied"), h + 1)
                pe.wait_ge(s("values_copied"), 6 if kind == "A" else 11)
                if h >= 1:
                    pe.wait_ge(s("pv_copied"), h)
                dst = aux[:, 3, 0:T]
                if kind == "A":
                    v, lo, hi = v_a, c * P, (c + 1) * P
                elif kind == "C":
                    v, lo, hi = v_c, c * P, (c + 1) * P
                else:
                    v, lo, r = v_b, c // (B_HEADS // 2) * 64, (c % 2) * 64
                    hi = lo + 64
                    dst = aux[r:r + 64, 3, 0:T]
                if kind == "C":
                    for t in range(2):
                        for st in range(2):
                            at = (2 * t + st) * P
                            mm = pe.matmul(dst[:, t * P:(t + 1) * P], v[:, st, lo:hi], p[:, at:at + P], start=(st == 0), stop=(st == 1))
                else:
                    pe.matmul(dst[:, 0:P], v[:, 0, lo:hi], p[:, 0:P], start=True, stop=True)
                    pe.matmul(dst[:, P:T], v[:, 0, lo:hi], p[:, P:2 * P], start=True, stop=False)
                    mm = pe.matmul(dst[:, P:T], v[:, 1, lo:hi], p[:, 2 * P:3 * P], start=False, stop=True)
                mm.then_inc(s("pv"), 1)

            def head_steps(name, n):
                for lag, stage in ((5, weigh_values), (3, turn_probs), (0, head_logits)):
                    h = stages(HEAD_AT[name], n, lag)
                    if h is not None:
                        stage(h)

            def beside_late(n):
                index_steps("late", n)
                norm_steps("late", n)
                value_steps(n)
                head_steps("late", n)

            products("early", beside_early)
            products("kv_up")
            products("late", beside_late)
            products("w_up_a", lambda n: head_steps("w_up_a", n))
            products("w_up_c", lambda n: head_steps("w_up_c", n))
            for name in ("w_up_b", "w_o"):
                products(name)
            pe.wait_ge(s("meta_in"), 16)
            pe.wait_ge(s("pv_copied"), len(HEADS))
            for k in range(KT):
                mm = pe.transpose(aux[:, 1, k * META:(k + 1) * META], meta_in[:, k * P:(k + 1) * P], ident[0:META, 0:META])
            mm.then_inc(s("meta_turned"), 1)
            pe.wait_ge(s("meta_sums"), 1)
            stat_wide(TM, 24, 0)
            for name in ("values", "gates", "pools", "pool_grp"):
                products(name)

            def layer_norm_sums(n):
                if n == LN_SLAB:
                    pe.wait_ge(s("conv_done"), 1)
                    pe.wait_ge(s("pool_taps"), (8 - DVE_TILES) * TAPS)
                    for k in range(8):
                        mm = pe.matmul(aux[:, 1, 0:T], ones[:], conv[:, k, :], start=(k == 0), stop=(k == 7))
                    mm.then_inc(s("conv_sum"), 1)
                r = n - LN_SLAB - 3
                if 0 <= r < 4:
                    pe.wait_ge(s("conv_sq"), r + 1)
                    for a in range(2):
                        mm = pe.matmul(aux[:, 0, 0:T], ones[:], square[:, r % 2, a * T:(a + 1) * T], start=(r == 0 and a == 0), stop=(r == 3 and a == 1))
                    mm.then_inc(s("conv_squares"), 1)
            products("pool_out", layer_norm_sums)
            for name in ("conv_out", "w_o_2"):
                products(name)
            stat_wide(T, 32, META)
            pe.wait_ge(s("variance"), 5)
            stat_wide(T, 40, META)
            for q in range(4):
                products(f"w_up{q}")
                products(f"w_down{q}")
            stat_wide(T, 48, META)
            pe.wait_ge(s("variance"), 7)
            for e in range(8):
                r, t = e // 2, e % 2
                pe.wait_ge(s("final"), 4 * r + 4)
                if e >= 4:
                    pe.wait_ge(s("rows_ready"), e - 3)
                for k in range(4):
                    mm = pe.transpose(aux[:, e % 4, k * P:(k + 1) * P], y[:, 4 * r + k, t * P:(t + 1) * P], ident[:])
                mm.then_inc(s("out_turned"), 1)

        @block.vector
        def _(dve):
            link = Chain(dve, dve_link)

            dve.sem_inc(split_done, STAGES)
            dve.sem_inc(acc_free, 2)
            dve.wait_ge(s("params_turned"), 1)
            for q, (c0, n) in enumerate(PARAM_GROUPS):
                dve.tensor_copy(params[:, c0:c0 + n], aux[:, q, 0:n]).then_inc(s("params_copied"), 1)
            link(dve.tensor_copy(relT[:], aux[0:NB, 1, P:P + BUCKETS]))
            dve.sem_inc(s("params_copied"), 1)
            dve.wait_ge(s("params_copied"), 5)
            dve.wait_ge(s("consts"), 1)
            for b in range(BUCKETS):
                lo = T - starts[b + 1]
                hi = T - starts[b] if b else 2 * T
                mm = dve.tensor_scalar(brow[:, lo:hi], zrow[:, lo:hi], relT[:, b:b + 1], None, ALU.add)
            mm.then_inc(s("bias_rows"), 1)
            link(dve.tensor_scalar(center[:, 0:64], ident[0:64, 0:64], 1.0 / IDX_DIM, None, ALU.subtract))
            dve.sem_inc(s("center"), 1)
            dve.tensor_scalar(center[:, 64:128], ident[0:64, 0:64], 1.0 / IDX_DIM, None, ALU.subtract).then_inc(s("center"), 1)

            stat_n = [0]

            def inverse_std(width, inv_d, eps, src=None):
                q = stat_n[0]
                stat_n[0] += 1
                if src is None:
                    dve.wait_ge(s("stats"), src_stats[0] + 1)
                    src_stats[0] += 1
                    src = aux[:, 0, 0:width]
                r = rstd[:, 0:width]
                dve.tensor_scalar(r, src, inv_d, eps, ALU.mult, ALU.add).then_inc(s("variance"), 1)
                dve.wait_ge(s("root"), q + 1)
                link(dve.reciprocal(r, r))
            src_stats = [0]

            def normalize(src, pair, width, gain, first):
                def low(r):
                    dve.wait_ge(s("pair_high"), first + r + 1)
                    dve.tensor_tensor(pair[:, 2 * r:2 * r + 2, 1, :], tmp[:, r % 2, 0:2 * width].rearrange("p (a t) -> p a t", a=2),
                                      pair[:, 2 * r:2 * r + 2, 0, :].bitcast(F32), ALU.subtract).then_inc(s("pair_ready"), 1)
                for r in range(8):
                    dve.wait_ge(s("pair_ready"), first + max(r - 1, 0))
                    for a in range(2):
                        k = 2 * r + a
                        ins = dve.scalar_tensor_tensor(out=tmp[:, r % 2, a * width:(a + 1) * width], in0=src(k), scalar=column(gain, k),
                                                       in1=rstd[:, 0:width], op0=ALU.mult, op1=ALU.mult)
                        if a == 0:
                            ins.then_inc(s("scaled_half"), 1)
                        else:
                            dve.wait_ge(s("scaled_half"), first + r + 1)
                            ins.then_inc(s("scaled"), 1)
                    if r >= 1:
                        low(r - 1)
                low(7)

            inverse_std(T, 1.0 / D, EPS)
            normalize(lambda k: turned[:, k, :], mem_pair, T, "mem_norm_g", 0)
            inverse_std(T, 1.0 / D, EPS)
            dve.wait_ge(s("bias_out"), 16)
            normalize(lambda k: turned[:, k, :], hT, T, "norm_g", 8)

            def splitting(name, body, links=0, beside=None):
                stream(dve, subtract_low, name, body, link, links, beside)

            def fold_into(name, dst, tile0=0, done=None):
                job = jobs[name]

                def body(i, u, part):
                    banks, _ = group_done(dve, job, i, u)
                    g = i * job.unroll + u
                    ins = fold(dve, dst[:, bass.ds(tile0 + g * 2, 2), :], banks)
                    ins.then_inc(acc_free, 1)
                return body

            for n in range(PAIRS):
                subtract_low(dve, jobs["mem_kv"], 0, 0, n)
            splitting("mem_kv", fold_into("mem_kv", mkv))
            def ikw_body(i, u, part):
                banks, _ = group_done(dve, jobs["ikw"], i, u)
                dve.tensor_reduce(ikw[:], banks[:, 0, :].rearrange("p (h t) -> p t h", h=2), AX, ALU.add).then_inc(acc_free, 1)
            splitting("ikw", ikw_body)

            def norm_steps(name, n):
                q = stages(NORM_AT[name], n, 1)
                if q is not None:
                    _, width, _, inv, both, _, _ = HEAD_NORMS[q]
                    w = T if both else width
                    dve.wait_ge(s("head_stats"), q + 1)
                    if q:
                        dve.wait_ge(s("head_normed"), q)
                    dve.tensor_scalar(rstd[:, 0:w], aux[:, 1, 0:w], inv, EPS, ALU.mult, ALU.add).then_inc(s("head_var"), 1)
                q = stages(NORM_AT[name], n, 2)
                if q is None:
                    return
                src, width, _, _, both, _, gain = HEAD_NORMS[q]
                w = T if both else width
                dve.wait_ge(s("head_root"), q + 1)
                link(dve.reciprocal(rstd[:, 0:w], rstd[:, 0:w]))
                if both:
                    dve.wait_ge(s("x_out"), 16)
                    for a in range(2):
                        link(dve.scalar_tensor_tensor(out=tmp[:, 0, a * T:(a + 1) * T], in0=src[:, a * T:(a + 1) * T], scalar=params[:, gain + a:gain + a + 1],
                                                      in1=rstd[:, 0:T], op0=ALU.mult, op1=ALU.mult))
                    v = tmp[:, 0, 0:2 * T].rearrange("p (a t) -> p a t", a=2)
                    link(dve.tensor_copy(ckv_pair[:, :, 0, :], v))
                    link(dve.tensor_tensor(ckv_pair[:, :, 1, :], v, ckv_pair[:, :, 0, :].bitcast(F32), ALU.subtract))
                    dve.sem_inc(s("ckv_ready"), 1)
                    dve.sem_inc(s("head_normed"), 1)
                    return
                ins = dve.scalar_tensor_tensor(out=src, in0=src, scalar=params[:, gain:gain + 1], in1=rstd[:, 0:w], op0=ALU.mult, op1=ALU.mult)
                if q == 0:
                    link(ins)
                    ins = dve.tensor_scalar(ikn[:], ikn[:], column("idx_k_ln_b"), None, ALU.add)
                    ins.then_inc(s("ik_ready"), 1)
                    dve.wait_ge(s("ik_ready"), 1)
                    dve.sem_inc(s("head_normed"), 1)
                    return
                ins.then_inc(s("head_normed"), 1)

            def index_steps(name, n):
                first = stages(INDEX_AT[name], n, 0)
                if first == 0:
                    dve.memset(score[:], 0.0).then_inc(s("score_zero"), 1)
                    dve.wait_ge(s("score_zero"), 1)
                for h in () if first is None else (first, first + 1):
                    dve.wait_ge(s("idx_relu"), h + 1)
                    if h:
                        dve.wait_ge(s("idx_added"), 2 * h)
                    for t in range(2):
                        lo, hi = head_cols("A", t)
                        dve.scalar_tensor_tensor(out=score[:, lo:hi], in0=lg[:, h % 2, lo:hi], scalar=iw[:, t, h:h + 1], in1=score[:, lo:hi],
                                                 op0=ALU.mult, op1=ALU.add).then_inc(s("idx_added"), 1)
                if first == IDX_HEADS - 2:
                    dve.wait_ge(s("idx_added"), 2 * IDX_HEADS)
                    dve.sem_inc(s("scored"), 1)

            def topk_steps(n):
                r = n - TOPK_AT
                if not 0 <= r < TOPK // 8:
                    return
                if r == 0:
                    dve.wait_ge(s("score_masked"), 2)
                for t in range(2):
                    lo, hi = head_cols("A", t)
                    src = score if r == 0 else work
                    link(dve.max(top8[:, t, :], src[:, lo:hi]))
                    link(dve.match_replace(work[:, lo:hi], top8[:, t, :], src[:, lo:hi], TAKEN))
                if r == TOPK // 8 - 1:
                    dve.tensor_scalar(work[:], work[:], TAKEN / 2, NEG, ALU.is_gt, ALU.mult).then_inc(s("topk"), 1)

            def value_steps(n):
                v = VALUES_AT.get(n)
                if v is None:
                    return
                dst, c = (v_a, v) if v < 6 else (v_b, 0) if v == 6 else (v_c, v - 7)
                dve.wait_ge(s("values_turned"), v + 1)
                dve.tensor_copy(dst[:, :, c * P:(c + 1) * P], aux[:, 3, 0:T].rearrange("p (t c) -> p t c", t=2)).then_inc(s("values_copied"), 1)

            def head_logits(h):
                kind, c = HEADS[h]
                l, _, w = logits_of(h)
                b = h % 2
                dve.wait_ge(s("qk"), h + 1)
                if h >= 2:
                    dve.wait_ge(s("probs_turned"), h - 1)
                scale = (B_DIM if kind == "B" else P) ** -0.5
                if kind == "A":
                    dve.wait_ge(s("masked"), 2 * h + 2)
                    link(dve.scalar_tensor_tensor(out=l, in0=aux[:, 0, 0:w], scalar=scale, in1=bias_mask[b][:], op0=ALU.mult, op1=ALU.add))
                elif kind == "B":
                    for t in range(2):
                        lo, hi = head_cols(kind, t)
                        link(dve.scalar_tensor_tensor(out=l[:, lo:hi], in0=aux[:, 0, lo:hi], scalar=scale,
                                                      in1=toep[:, A_HEADS + c, T - (hi - lo):T], op0=ALU.mult, op1=ALU.add))
                else:
                    link(dve.tensor_scalar(l, aux[:, 0, 0:w], scale, None, ALU.mult))
                for t in range(2):
                    lo, hi = head_cols(kind, t)
                    link(dve.tensor_reduce(negmax[:, b, t:t + 1], l[:, lo:hi], AX, ALU.max))
                if kind == "B":
                    if c == 0:
                        dve.wait_ge(s("sinks_in"), 16)
                    link(dve.tensor_scalar(negmax[:, b, :], negmax[:, b, :], sinks[:, c:c + 1], None, ALU.max))
                link(dve.tensor_scalar(negmax[:, b, :], negmax[:, b, :], -1.0, None, ALU.mult))
                dve.sem_inc(s("logits"), 1)

            def scale_probs(h):
                kind, c = HEADS[h]
                l, _, _ = logits_of(h)
                b = h % 2
                dve.wait_ge(s("exps"), 2 * h + 2)
                if kind == "B":
                    dve.wait_ge(s("sink_exps"), 2 * c + 2)
                    link(dve.tensor_tensor(denom[:, b, :], denom[:, b, :], esink[:, b, :], ALU.add))
                link(dve.reciprocal(denom[:, b, :], denom[:, b, :]))
                for t in range(2):
                    lo, hi = head_cols(kind, t)
                    link(dve.tensor_scalar(l[:, lo:hi], l[:, lo:hi], denom[:, b, t:t + 1], None, ALU.mult))
                dve.sem_inc(s("probs"), 1)

            def copy_out(h):
                kind, c = HEADS[h]
                dve.wait_ge(s("pv"), h + 1)
                if kind == "A":
                    dst, src = early[:, E_AQ + c, :], aux[:, 3, 0:T]
                elif kind == "C":
                    dst, src = late[:, L_CQ + c, :], aux[:, 3, 0:T]
                else:
                    r = (c % 2) * 64
                    dst, src = late[r:r + 64, L_BQ + c // 2, :], aux[r:r + 64, 3, 0:T]
                dve.tensor_copy(dst, src).then_inc(s("pv_copied"), 1)

            def head_steps(name, n):
                for lag, stage in ((5, copy_out), (2, scale_probs), (0, head_logits)):
                    h = stages(HEAD_AT[name], n, lag)
                    if h is not None:
                        stage(h)

            def split_step(q, r):
                dve.wait_ge(s("gated"), q + 1)
                v = gate[:, q % 2, 0:2 * T].rearrange("p (a t) -> p a t", a=2)
                link(dve.tensor_copy(o_pair[:, 2 * r:2 * r + 2, 0, :], v))
                dve.tensor_tensor(o_pair[:, 2 * r:2 * r + 2, 1, :], v, o_pair[:, 2 * r:2 * r + 2, 0, :].bitcast(F32), ALU.subtract).then_inc(s("o_split"), 1)

            def beside_early(n):
                if n == 0:
                    dve.wait_ge(s("ik_centered"), 1)
                    link(dve.tensor_copy(ikn[:], aux[:, 1, 0:T]))
                    dve.sem_inc(s("ik_copied"), 1)
                    dve.wait_ge(s("iw_turned"), 1)
                    dve.tensor_scalar(iw, aux[:, 2, 0:T].rearrange("p (t c) -> p t c", t=2)[:, :, 64:80],
                                      IDX_HEADS ** -0.5 * IDX_DIM ** -0.5, None, ALU.mult).then_inc(s("iw_ready"), 1)
                    dve.wait_ge(s("iw_ready"), 1)
                norm_steps("early", n)
                index_steps("early", n)

            def beside_late(n):
                index_steps("late", n)
                norm_steps("late", n)
                topk_steps(n)
                value_steps(n)
                head_steps("late", n)
                if 0 <= n - SILU_AT - 1 < 3:
                    split_step(n - SILU_AT - 1, n - SILU_AT - 1)

            splitting("early", fold_into("early", early), beside=beside_early)
            splitting("kv_up", fold_into("kv_up", akv))
            splitting("late", fold_into("late", late), beside=beside_late)

            def gated_product(name, steps0, dst=None, pair=None, ready=None, beside=None):
                job = jobs[name]

                def body(i, u, part):
                    banks, _ = group_done(dve, job, i, u, part)
                    i = i * job.unroll + u
                    n = steps0 + i
                    if part == 0:
                        dve.wait_ge(s("merged_step"), n)
                    done = s("gate_in") if part == 0 else s("up_ready")
                    fold(dve, tmp[:, part, 0:2 * T].rearrange("p (a t) -> p a t", a=2), banks).then_inc(done, 1)
                    dve.wait_ge(done, n + 1)
                    dve.sem_inc(acc_free, 1)
                    if part == 1 and pair is not None:
                        dve.wait_ge(s("merged_step"), n + 1)
                        hi, lo = pair[:, bass.ds(i * 2, 2), 0, :], pair[:, bass.ds(i * 2, 2), 1, :]
                        v = dst[:, bass.ds(i * 2, 2), :]
                        dve.tensor_copy(hi, v).then_inc(s("pair_step"), 1)
                        dve.wait_ge(s("pair_step"), i + 1 + (0 if ready == "merged_ready" else 8))
                        dve.tensor_tensor(lo, v, hi.bitcast(F32), ALU.subtract).then_inc(s(ready), 1)
                splitting(name, body, beside=beside)

            gated_product("w_up_a", 0, beside=lambda n: head_steps("w_up_a", n))
            for r in range(2):
                split_step(3 + r, r)
            gated_product("w_up_c", 8, beside=lambda n: head_steps("w_up_c", n))
            for r in range(3):
                split_step(5 + r, r)
            gated_product("w_up_b", 16, merged, merged_pair, "merged_ready")

            dve.sem_inc(s("residual"), 2)

            def wo_body(i, u, part):
                banks, _ = group_done(dve, jobs["w_o"], i, u)
                g = 2 * i + u
                dve.wait_ge(s("residual"), g + 1)
                fold(dve, tmp[:, u, 0:2 * T].rearrange("p (a t) -> p a t", a=2), banks).then_inc(s("folded"), 1)
                dve.wait_ge(s("folded"), g + 1)
                dve.sem_inc(acc_free, 1)
            splitting("w_o", wo_body)
            dve.wait_ge(s("meta_turned"), 1)
            link(dve.tensor_copy(h1[:, :, 0:META], aux[:, 1, 0:KT * META].rearrange("p (k t) -> p k t", k=KT)))
            sqm = tmp[:, 0, 0:KT * META]
            dve.wait_ge(s("residual"), 2 + 8)
            link(dve.tensor_tensor(sqm.rearrange("p (k t) -> p k t", k=KT), h1[:, :, 0:META], h1[:, :, 0:META], ALU.mult))
            link(dve.memset(sumsq[:, 1, 0:META], 0.0))
            dve.tensor_reduce(sumsq[:, 0, 0:META], sqm.rearrange("p (k t) -> p t k", k=KT), AX, ALU.add).then_inc(s("meta_sums"), 1)
            inverse_std(TM, 1.0 / D, EPS)
            normalize(lambda k: h1[:, k, :], uT, TM, "g_pre_mix_2", 16)

            link(dve.memset(glu[:, :, 0:TAPS - 1 - META], 0.0))

            def values_body(i, u, part):
                banks, _ = group_done(dve, jobs["values"], i, u)
                g = 2 * i + u
                link(dve.tensor_copy(glu[:, 2 * g:2 * g + 2, TAPS - 1 - META:], banks[:, :, 0:TM]))
                dve.sem_inc(s("values_moved"), 1)
                dve.sem_inc(acc_free, 1)

            def gates_body(i, u, part):
                dve.wait_ge(s("glu_sig"), 2 * i + u + 1)
                dve.sem_inc(acc_free, 1)

            def pools_body(i, u, part):
                banks, _ = group_done(dve, jobs["pools"], i, u)
                g = POOL_ORDER[2 * i + u]
                link(dve.tensor_copy(z_pool[:, 2 * g:2 * g + 2, :], banks[:, :, 0:TM]))
                dve.sem_inc(s("pooled"), 1)
                dve.sem_inc(acc_free, 1)

            taps_done = [0]

            def conv_taps(count):
                for _ in range(count):
                    n = taps_done[0]
                    if n == DVE_TILES * TAPS:
                        return
                    taps_done[0] += 1
                    tap, k = n // DVE_TILES, n % DVE_TILES
                    w = column("w_dw_2", 8 * tap + k)
                    if tap == 0:
                        ins = dve.tensor_scalar(conv[:, k, :], glu[:, k, 0:T], w, column("b_dw_2", k), ALU.mult, ALU.add)
                    else:
                        dve.wait_ge(s("conv_taps"), n - DVE_TILES + 1)
                        ins = dve.scalar_tensor_tensor(out=conv[:, k, :], in0=glu[:, k, tap:tap + T], scalar=w, in1=conv[:, k, :],
                                                       op0=ALU.mult, op1=ALU.add)
                    ins.then_inc(s("conv_taps"), 1)
                    if n == DVE_TILES * TAPS - 1:
                        dve.wait_ge(s("conv_taps"), DVE_TILES * TAPS)
                        dve.sem_inc(s("conv_done"), 1)

            def taps_beside_pools(n):
                if n == 0:
                    dve.wait_ge(s("glu_done"), 4)
                conv_taps(4)

            def grp_body(i, u, part):
                banks, _ = group_done(dve, jobs["pool_grp"], i, u)
                g = POOL_ORDER[8 * i + u]
                v = tmp[:, 0, 0:2 * T].rearrange("p (a t) -> p a t", a=2)
                link(fold(dve, v, banks))
                dve.sem_inc(acc_free, 1)
                for a in range(2):
                    link(dve.tensor_scalar(v[:, a, :], v[:, a, :], column("pool_scale_2", 2 * g + a), None, ALU.mult))
                link(dve.tensor_copy(y_pair[:, 2 * g:2 * g + 2, 0, :], v))
                dve.tensor_tensor(y_pair[:, 2 * g:2 * g + 2, 1, :], v, y_pair[:, 2 * g:2 * g + 2, 0, :].bitcast(F32), ALU.subtract).then_inc(s("y_split"), 1)
                dve.wait_ge(s("y_split"), 8 * i + u + 1)
                if 8 * i + u == 3:
                    dve.sem_inc(s("y_pair_ready"), 4)

            def layer_norm_steps(n):
                if n < LN_SLAB:
                    conv_taps(3 if n < LN_SLAB - 1 else DVE_TILES * TAPS)
                if n == LN_SLAB + 1:
                    dve.wait_ge(s("conv_sum"), 1)
                    link(dve.tensor_scalar(rstd[:, T:2 * T], aux[:, 1, 0:T], 1.0 / CONV_W, None, ALU.mult))
                    for k in range(8):
                        ins = dve.tensor_tensor(conv[:, k, :], conv[:, k, :], rstd[:, T:2 * T], ALU.subtract)
                        if k % 2 == 0:
                            ins.then_inc(s("center_half"), 1)
                        else:
                            dve.wait_ge(s("center_half"), k // 2 + 1)
                            ins.then_inc(s("conv_centered"), 1)
                if n == LN_SLAB + 6:
                    dve.wait_ge(s("conv_squares"), 4)
                    inverse_std(T, 1.0 / CONV_W, LN_EPS, src=aux[:, 0, 0:T])
                    for k in range(8):
                        ins = dve.tensor_tensor(conv[:, k, :], conv[:, k, :], rstd[:, 0:T], ALU.mult)
                        if k % 2 == 0:
                            ins.then_inc(s("scale_half"), 1)
                        else:
                            dve.wait_ge(s("scale_half"), k // 2 + 1)
                            ins.then_inc(s("conv_scaled"), 1)
                if n == LN_SLAB + 7:
                    for q in range(4):
                        dve.wait_ge(s("conv_sig"), 2 * q + 2)
                        dve.wait_ge(s("conv_affine"), 2 * q + 2)
                        v = conv[:, 2 * q:2 * q + 2, :]
                        dve.tensor_tensor(v, v, square[:, q % 2, 0:2 * T].rearrange("p (a t) -> p a t", a=2), ALU.mult).then_inc(s("conv_used"), 1)
                        if q >= 1:
                            conv_low(q - 1)
                    conv_low(3)

            def conv_low(q):
                dve.wait_ge(s("conv_high"), q + 1)
                dve.tensor_tensor(conv_pair[:, 2 * q:2 * q + 2, 1, :], conv[:, 2 * q:2 * q + 2, :], conv_pair[:, 2 * q:2 * q + 2, 0, :].bitcast(F32),
                                  ALU.subtract).then_inc(s("conv_ready"), 1)

            splitting("values", values_body)
            splitting("gates", gates_body)
            splitting("pools", pools_body, beside=taps_beside_pools)
            splitting("pool_grp", grp_body, beside=lambda n: conv_taps(2))
            gated_product("pool_out", 24, beside=layer_norm_steps)
            gated_product("conv_out", 32, m, m_pair, "m_ready")

            def mixed_body(i, u, part):
                banks, _ = group_done(dve, jobs["w_o_2"], i, u)
                g = 2 * i + u
                fold(dve, mixed[:, bass.ds(2 * g, 2), :], banks).then_inc(s("mixed"), 1)
                dve.wait_ge(s("mixed"), g + 1)
                dve.sem_inc(acc_free, 1)
            splitting("w_o_2", mixed_body)
            inverse_std(T, 1.0 / D, EPS)
            for k in range(KT):
                v = tmp[:, k % 2, 0:T]
                link(dve.scalar_tensor_tensor(out=v, in0=mixed[:, k, :], scalar=column("g_post_mix_2", k), in1=rstd[:, 0:T], op0=ALU.mult, op1=ALU.mult))
                dve.tensor_tensor(h1[:, k, META:TM], h1[:, k, META:TM], v, ALU.add).then_inc(s("h2"), 1)
            inverse_std(T, 1.0 / D, EPS)
            dve.wait_ge(s("h2"), 16)
            normalize(lambda k: h1[:, k, META:TM], u2, T, "g_pre_mlp_2", 24)

            def up_body(q):
                job = jobs[f"w_up{q}"]

                def body(i, u, part):
                    banks, _ = group_done(dve, job, i, u)
                    g = i * job.unroll + u
                    v = tmp[:, u, 0:2 * T].rearrange("p (a t) -> p a t", a=2)
                    link(fold(dve, v, banks))
                    dve.sem_inc(acc_free, 1)
                    f = tmp[:, u, 0:2 * T]
                    link(dve.scalar_tensor_tensor(out=f, in0=f, scalar=0.0, in1=f, op0=ALU.max, op1=ALU.mult))
                    hi, lo = f_pair[:, bass.ds(g * 2, 2), 0, :], f_pair[:, bass.ds(g * 2, 2), 1, :]
                    link(dve.tensor_copy(hi, v))
                    dve.tensor_tensor(lo, v, hi.bitcast(F32), ALU.subtract).then_inc(s("f_ready"), 1)
                return body

            def down_body(q):
                job = jobs[f"w_down{q}"]

                def body(i, u, part):
                    banks, _ = group_done(dve, job, i, u)
                    g = i * job.unroll + u
                    dve.wait_ge(s("down_added"), 8 * q + g)
                    fold(dve, tmp[:, u, 0:2 * T].rearrange("p (a t) -> p a t", a=2), banks).then_inc(s("down"), 1)
                    dve.wait_ge(s("down"), 8 * q + g + 1)
                    dve.sem_inc(acc_free, 1)
                return body
            for q in range(4):
                splitting(f"w_up{q}", up_body(q), 3)
                splitting(f"w_down{q}", down_body(q))
                dve.wait_ge(s("down_added"), 1 + 8 * q + 8)
            inverse_std(T, 1.0 / D, EPS)
            for k in range(KT):
                v = tmp[:, k % 2, 0:T]
                link(dve.scalar_tensor_tensor(out=v, in0=y[:, k, :], scalar=column("g_post_mlp_2", k), in1=rstd[:, 0:T], op0=ALU.mult, op1=ALU.mult))
                dve.tensor_tensor(y[:, k, :], h1[:, k, META:TM], v, ALU.add).then_inc(s("final"), 1)


_NAMES = ["x", "mem", "norm_g", "w_in", "kv_norm_g", "w_kv_up", "idx_k_ln_g", "idx_k_ln_b", "q_norm_a", "k_norm_a",
          "q_norm_b", "k_norm_b", "sinks_b", "mem_norm_g", "w_mem_kv", "q_norm_c", "k_norm_c", "w_up_a", "w_up_b",
          "w_up_c", "gate_bias", "w_o", "rel_bias", "meta_2", "g_pre_mix_2", "w_in_2", "w_pool_grp_2", "pool_scale_2",
          "w_pool_out_2", "w_dw_2", "b_dw_2", "conv_ln_g_2", "conv_ln_b_2", "w_conv_out_2", "w_o_2", "g_post_mix_2",
          "g_pre_mlp_2", "w_up_2", "w_down_2", "g_post_mlp_2"]


def kernel(**inputs):
    import concourse.bacc as bacc
    from concourse.bass_utils import run_bass_kernel_spmd

    nc = bacc.Bacc("TRN2", target_bir_lowering=False, num_devices=1)
    arrays, views = {}, {}
    for name in _NAMES:
        a = np.ascontiguousarray(inputs[name])
        arrays[f"in_{name}"] = a
        views[name] = nc.dram_tensor(f"in_{name}", a.shape, mybir.dt.from_np(a.dtype), kind="ExternalInput").ap()
    out = nc.dram_tensor("out", (1, T, D), F32, kind="ExternalOutput").ap()
    build(nc, views, out)
    return run_bass_kernel_spmd(nc, [arrays], core_ids=[0]).results[0]["out"]
```

```python
import math
from contextlib import ExitStack

import numpy as np
import concourse.bass as bass
from concourse import mybir

F32 = mybir.dt.float32
F32R = mybir.dt.float32r
ALU = mybir.AluOpType
ACT = mybir.ActivationFunctionType
AX = mybir.AxisListType.X

P = 128
D = 2048
KT = D // P
T = 256
META = 16
TM = T + META
A_HEADS, B_HEADS, C_HEADS = 6, 12, 4
IDX_HEADS, IDX_DIM, B_DIM = 16, 64, 64
TOPK = min(256, T // 4)
WINDOW = 128
BUCKETS, MAX_DISTANCE = 32, 128
KV_RANK = 256
A_W, B_W, C_W = 768, 768, 512
POOL_W = CONV_W = 1024
TAPS = 31
D_FF = 4 * D
EPS, LN_EPS = 1e-6, 1e-5
NEG = -1.0e30
TAKEN = -3.0e38

GROUP = 256
SLAB = 4
STAGES = 8
PAIRS = 4

A_CKV, I_Q, I_K = 768, 1024, 2048
A_GATE = 2128
MIX = 5712
E_AQ, E_CKV, E_IQ = 0, 6, 8
L_AGATE, L_BQ, L_BK, L_BV, L_BGATE, L_CQ, L_CGATE = 0, 6, 12, 13, 14, 20, 24

ROWS0 = [("gate_bias", 48), ("norm_g", 16), ("mem_norm_g", 16), ("g_pre_mix_2", 16), ("g_post_mix_2", 16), ("g_pre_mlp_2", 16)]
ROWS1 = [("g_post_mlp_2", 16), ("pool_scale_2", 8), ("b_dw_2", 8), ("conv_ln_g_2", 8), ("conv_ln_b_2", 8), ("kv_norm_g", 2),
         ("q_norm_a", 1), ("k_norm_a", 1), ("q_norm_c", 1), ("k_norm_c", 1)]
HALF_ROWS = ["q_norm_b", "k_norm_b", "idx_k_ln_g", "idx_k_ln_b"]
DW_ROWS = TAPS * (CONV_W // P)
COL, _at = {}, 0
for _name, _n in ROWS0 + ROWS1 + [(n, 1) for n in HALF_ROWS] + [("w_dw_2", DW_ROWS)]:
    COL[_name] = _at
    _at += _n
N0 = sum(n for _, n in ROWS0)
N1 = sum(n for _, n in ROWS1) + len(HALF_ROWS)
PARAM_GROUPS = [(0, N0), (N0, N1), (N0 + N1, DW_ROWS // 2), (N0 + N1 + DW_ROWS // 2, DW_ROWS // 2)]
PARAMS = _at

DVE_TILES = 6
POOL_ORDER = (3, 2, 1, 0)

KB = 1024


def bucket_starts():
    n = np.arange(T, dtype=np.int32)
    exact = BUCKETS // 2
    nf = np.maximum(n, 1).astype(np.float32)
    large = exact + (np.log(nf / np.float32(exact)) / np.float32(math.log(MAX_DISTANCE / exact))
                     * np.float32(BUCKETS - exact)).astype(np.int32)
    b = np.where(n < exact, n, np.minimum(large, BUCKETS - 1))
    return [int(np.argmax(b == k)) for k in range(BUCKETS)] + [T]


class Chain:

    def __init__(self, eng, sem):
        self.eng, self.sem, self.n, self.term = eng, sem, 0, 0

    def __call__(self, ins):
        ins.then_inc(self.sem, 1)
        self.n += 1
        self.eng.wait_ge(self.sem, self.n + self.term)


def repeat(eng, count, unroll, body, chain=None, links=0):
    whole = count // unroll
    start = 0
    if whole >= 2:
        n0 = chain.n if chain else 0
        with eng.Fori(0, whole) as i:
            if chain:
                chain.term = i * links
            for u in range(unroll):
                body(i, u)
        if chain:
            assert chain.n - n0 == links, (chain.n - n0, links)
            chain.n, chain.term = n0 + whole * links, 0
        start = whole * unroll
    for s in range(start, count):
        body(s // unroll, s % unroll)


class Part:

    def __init__(self, w, col0, slabs, rhs, ready=None, wide=False, cols=GROUP, stride=GROUP, row0=0):
        self.w, self.col0, self.slabs, self.rhs, self.wide, self.cols, self.stride, self.row0 = w, col0, slabs, rhs, wide, cols, stride, row0
        self.ready = ready


class Job:

    def __init__(self, steps, parts, unroll):
        self.steps, self.parts, self.unroll = steps, parts, unroll
        self.pieces = [(p, pn, sum(p.slabs[:q]), kt, q == len(p.slabs) - 1) for pn, p in enumerate(parts) for q, kt in enumerate(p.slabs)]
        self.S = len(self.pieces)

    def place(self, slab0, group0):
        self.slab0, self.group0 = slab0, group0
        return slab0 + self.steps * self.S, group0 + self.steps * len(self.parts)

    def slab(self, i, u, idx):
        n = self.slab0 + u * self.S + idx
        return n + i * (self.unroll * self.S), n

    def group(self, i, u, part):
        g = self.group0 + u * len(self.parts) + part
        last = self.slab0 + u * self.S + sum(len(p.slabs) for p in self.parts[:part + 1]) - 1
        return g + i * (self.unroll * len(self.parts)), g % 2, last + i * (self.unroll * self.S)


def build(nc, A, out):
    ctx = ExitStack()
    with ctx:
        ctx.enter_context(nc.sbuf_tensor("arena", [P, 53200], F32))
        BASE = 16512

        def at(name, kb, shape, dt=F32):
            return nc.alloc_sbuf_tensor_at(name, shape, dt, offset=BASE + int(kb * KB))

        def sem(name):
            return ctx.enter_context(nc.semaphore(name))

        stage = at("stage", 0, [P, STAGES, SLAB, GROUP])
        w_high = at("w_high", 32, [P, PAIRS, SLAB, GROUP], F32R)
        w_low = at("w_low", 48, [P, PAIRS, SLAB, GROUP], F32R)
        params = at("params", 64, [P, PARAMS])
        ident = at("ident", 66, [P, P])
        ones = at("ones", 66.5, [P, P])
        blocks = at("blocks", 67, [P, P])
        center = at("center", 67.5, [IDX_DIM, P])
        square = at("square", 68, [P, 2, 2 * TM])
        sumsq = at("sumsq", 72.25, [P, 2, TM])
        rstd = at("rstd", 74.5, [P, 2 * T])
        tmp = at("tmp", 76.5, [P, 2, 2 * TM])
        gate = at("gate", 80.75, [P, 2, 2 * TM])
        Z = 85
        hT = at("hT", Z, [P, KT, 2, T], F32R)
        late = at("late", Z + 32, [P, 28, T])
        mem_pair = at("mem_pair", Z + 32, [P, KT, 2, T], F32R)
        mkv = at("mkv", Z + 114, [P, 8, T])
        mem_in = at("mem_in", Z + 64, [P, 2, D])
        x_in = at("x_in", Z + 80, [P, 2, D])
        turned = at("turned", Z + 96, [P, KT, T])
        toep = at("toep", Z + 60, [P, A_HEADS + B_HEADS, T])
        early = at("early", Z + 78, [P, 16, T])
        flip = at("flip", Z + 113, [P, P])
        ikw = at("ikw", Z + 94, [P, T])
        akv = at("akv", Z + 95, [P, 12, T])
        ckv_pair = at("ckv_pair", Z + 107, [P, 2, 2, T], F32R)
        v_a = at("v_a", Z + 86, [P, 2, A_W])
        v_b = at("v_b", Z + 111, [P, 2, P])
        v_c = at("v_c", Z + 107, [P, 2, C_W])
        ptb = at("ptb", 76.5, [P, 2, 2 * T])
        lg = at("lg", 80.75, [P, 2, 2 * T])
        ptb_bc = at("ptb_bc", Z + 60, [P, 2, 2 * T])
        lg_bc = at("lg_bc", Z + 118, [P, 2, 2 * T])
        bias_mask = [at("bias_mask0", Z + 84, [P, 3 * P]), at("bias_mask1", Z + 92, [P, 3 * P])]
        score = at("score", Z + 111, [P, 3 * P])
        work = at("work", Z + 112.5, [P, 3 * P])
        ikn = at("ikn", 72.25, [P, T])
        bk_swap = at("bk_swap", 73.25, [P, T])
        small = at("small", 65.71875, [P, 72])
        merged = at("merged", Z + 78, [P, KT, T])
        o_pair = at("o_pair", Z + 94, [P, 6, 2, T], F32R)
        merged_pair = at("merged_pair", Z + 32, [P, KT, 2, T], F32R)
        xT = at("xT", Z + 106, [P, KT, T])
        h1 = at("h1", Z, [P, KT, TM])
        uT = at("uT", Z + 17, [P, KT, 2, TM], F32R)
        m = at("m", Z + 52, [P, KT, T])
        d_pair = at("d_pair", Z + 68, [P, 8, 2, T], F32R)
        y_pair = at("y_pair", Z + 68, [P, 8, 2, T], F32R)
        glu = at("glu", Z + 84, [P, 8, TAPS - 1 - META + TM])
        conv = at("conv", Z + 94, [P, 8, T])
        z_pool = at("z_pool", Z + 102.25, [P, 8, TM])
        window = at("window", Z + 110.75, [P, 2, 2 * TM])
        product = at("product", Z + 118.5, [P, 2, T])
        conv_pair = at("conv_pair", Z + 84, [P, 8, 2, T], F32R)
        gate_b = at("gate_b", Z + 102.25, [P, KT, T])
        m_pair = at("m_pair", Z + 17, [P, KT, 2, T], F32R)
        mixed = at("mixed", Z + 52, [P, KT, T])
        u2 = at("u2", Z + 17, [P, KT, 2, T], F32R)
        f_pair = at("f_pair", Z + 84, [P, KT, 2, T], F32R)
        y = at("y", Z + 52, [P, KT, T])
        rows_out = at("rows_out", Z + 68, [P, 2, D])
        rows_h = at("rows_h", Z + 17, [P, 2, D])
        prow = at("prow", Z, [P, 4, P])
        meta_in = at("meta_in", Z + 17, [META, D])
        relb = at("relb", Z + 2, [BUCKETS, A_HEADS + B_HEADS])
        relT = at("relT", Z + 2.5, [A_HEADS + B_HEADS, BUCKETS])
        brow = at("brow", Z + 3, [A_HEADS + B_HEADS, 2 * T])
        zrow = at("zrow", Z + 5, [A_HEADS + B_HEADS, 2 * T])

        acc = ctx.enter_context(nc.psum_tensor("acc", [P, 4, 512], F32))
        aux = ctx.enter_context(nc.psum_tensor("aux", [P, 4, 512], F32))
        spill_x = nc.dram_tensor("spill_x", [P, KT, T], F32, kind="Internal").ap()
        NB = A_HEADS + B_HEADS
        bias_dram = nc.dram_tensor("bias_rows", [NB, 2 * T], F32, kind="Internal")

        iw = small[:, 0:32].rearrange("p (t h) -> p t h", t=2)
        negmax = small[:, 32:36].rearrange("p (b t) -> p b t", b=2)
        denom = small[:, 36:40].rearrange("p (b t) -> p b t", b=2)
        top8 = small[:, 40:56].rearrange("p (t e) -> p t e", t=2)
        sinks = small[:, 56:68]
        esink = small[:, 68:72].rearrange("p (b t) -> p b t", b=2)
        inv_ms, out_ms, out_scale = small[:, 0:2], small[:, 2:4], small[:, 4:6]

        landed = [sem(f"landed{s}") for s in range(STAGES)]
        issued, high_done, split_done, used, acc_free = sem("issued"), sem("high_done"), sem("split_done"), sem("used"), sem("acc_free")
        act_link, dve_link, pool_link = sem("act_link"), sem("dve_link"), sem("pool_link")
        S = {}

        def s(name):
            if name not in S:
                S[name] = sem(name)
            return S[name]

        starts = bucket_starts()

        A = {n: (v[0] if v.shape[0] == 1 else v) for n, v in A.items()}

        def column(name, k=0):
            return params[:, COL[name] + k:COL[name] + k + 1]
        def tiles_of(src, first, n):
            return src[:, first:first + n, :].rearrange("p a t -> p (a t)")

        def norm(src, first, n, mat, inv, group, gain, both=False):
            return (tiles_of(src, first, n), n * T, mat, inv, both, group, COL[gain])

        HEAD_NORMS = [(ikn[:], T, blocks, 1.0 / IDX_DIM, False, ("ikw", 0), COL["idx_k_ln_g"])]
        HEAD_NORMS += [norm(mkv, r, 2, ones, 1.0 / P, ("mem_kv", 3), "k_norm_c") for r in (0, 2)]
        HEAD_NORMS += [norm(early, E_AQ + r, 2, ones, 1.0 / P, ("early", r // 2), "q_norm_a") for r in (0, 2, 4)]
        HEAD_NORMS += [norm(early, E_CKV, 2, ones, 1.0 / KV_RANK, ("early", 3), "kv_norm_g", True)]
        HEAD_NORMS += [norm(akv, r, 2, ones, 1.0 / P, ("kv_up", r // 2), "k_norm_a") for r in (0, 2, 4)]
        HEAD_NORMS += [norm(late, L_BQ + r, 2, blocks, 1.0 / B_DIM, ("late", (L_BQ + r) // 2), "q_norm_b") for r in (0, 2, 4)]
        HEAD_NORMS += [norm(late, L_BK, 1, blocks, 1.0 / B_DIM, ("late", L_BK // 2), "k_norm_b")]
        HEAD_NORMS += [norm(late, L_CQ + r, 2, ones, 1.0 / P, ("late", (L_CQ + r) // 2), "q_norm_c") for r in (0, 2)]
        NORM_AT = {"early": {1: 0, 3: 1, 5: 2, 8: 3, 10: 4, 12: 5, 16: 6},
                   "late": {4: 7, 7: 8, 10: 9, 43: 10, 45: 11, 47: 12, 49: 13, 51: 14, 53: 15}}
        NORMS_A, NORMS_ALL = 10, 16
        FLIP_AT = 7
        INDEX_AT = {"early": {21: 0, 22: 2, 25: 4, 26: 6, 29: 8, 30: 10}, "late": {0: 12, 1: 14}}
        TOPK_AT = {n: r for r, n in enumerate((3, 5, 6, 8, 9, 11, 12, 14))}
        VALUES_AT = {n: v for v, n in enumerate((10, 12, 15, 17, 19, 21, 45, 47, 49, 51, 53))}
        HEADS = [("A", h) for h in range(A_HEADS)] + [("C", h) for h in range(C_HEADS)] + [("B", h) for h in range(B_HEADS)]
        HEAD_AT = {"late": {17 + 4 * h: h for h in range(6)},
                   "w_up_a": {5 + 5 * h: 6 + h for h in range(8)},
                   "w_up_c": {3 + 4 * h: 14 + h for h in range(8)}}
        META_AT = 8
        SILU_AT = 52

        def stages(table, n, lag):
            return table.get(n - lag)

        RSTD = [rstd[:, T:2 * T], rstd[:, 0:T], rstd[:, 0:TM], rstd[:, 0:T], rstd[:, 0:T]]
        X_AT = 0
        X_NORM_AT = 9

        def head_cols(kind, t):
            if kind == "C":
                return t * T, (t + 1) * T
            return (0, P) if t == 0 else (P, 3 * P)

        def logits_of(n):
            a, b = (lg, ptb) if HEADS[n][0] == "A" else (lg_bc, ptb_bc)
            width = 4 * P if HEADS[n][0] == "C" else 3 * P
            return a[:, n % 2, 0:width], b[:, n % 2, 0:width], width

        LN_SLAB = 26

        full = [4, 4, 4, 4]

        def rhs_of(pair):
            return lambda k: (pair[:, k, :, :], pair[:, k, 0, :])

        def u_tokens(k):
            return uT[:, k, :, META:TM], uT[:, k, 0, META:TM]

        jobs = {}
        order = [
            ("mem_kv", Job(4, [Part(A["w_mem_kv"], 0, full, rhs_of(mem_pair), ("pair_ready", 0))], 2)),
            ("ikw", Job(1, [Part(A["w_in"], I_K, full, rhs_of(hT), ("pair_ready", 8), cols=P)], 2)),
            ("early", Job(8, [Part(A["w_in"], 0, full, rhs_of(hT))], 2)),
            ("kv_up", Job(6, [Part(A["w_kv_up"], 0, [2], rhs_of(ckv_pair), ("ckv_ready", 0))], 8)),
            ("late", Job(14, [Part(A["w_in"], A_GATE, full, rhs_of(hT))], 2)),
        ]
        for w, b, slabs, before in (("w_up_a", 0, [3, 3], 0), ("w_up_c", 2, [2, 2], 3), ("w_up_b", 1, [3, 3], 5)):
            order.append((w, Job(8, [Part(A["w_in"], MIX + b * D, full, rhs_of(hT)),
                                     Part(A[w], 0, slabs, rhs_of(o_pair), ("o_split", before))], 4)))
        order += [
            ("w_o", Job(8, [Part(A["w_o"], 0, full, rhs_of(merged_pair), ("merged_ready", 0))], 2)),
        ]
        for name, col0, stride in (("values", POOL_W, GROUP), ("gates", POOL_W + CONV_W, GROUP), ("pools", POOL_W - GROUP, -GROUP)):
            order.append((name, Job(4, [Part(A["w_in_2"], col0, full, lambda k: (uT[:, k, 0, :], uT[:, k, 1, :]), ("pair_ready", 16),
                                             wide=True, stride=stride)], 2)))
        order += [
            ("conv_gates", Job(8, [Part(A["w_in_2"], POOL_W + 2 * CONV_W + D, full, u_tokens)], 2)),
            ("pool_grp", Job(4, [Part(A["w_pool_grp_2"], 0, [2], rhs_of(d_pair), ("d_ready", 0), stride=0)], 8)),
            ("pool_out", Job(8, [Part(A["w_in_2"], POOL_W + 2 * CONV_W, full, u_tokens),
                                 Part(A["w_pool_out_2"], 0, [4, 4], rhs_of(y_pair), ("y_pair_ready", 0))], 4)),
            ("conv_out", Job(8, [Part(A["w_conv_out_2"], 0, [4, 4], rhs_of(conv_pair), ("conv_ready", 0))], 4)),
            ("w_o_2", Job(8, [Part(A["w_o_2"], 0, full, rhs_of(m_pair), ("m_ready", 0))], 2)),
        ]
        for q in range(4):
            order.append((f"w_up{q}", Job(8, [Part(A["w_up_2"], q * D, full, rhs_of(u2), ("pair_ready", 24))], 2)))
            order.append((f"w_down{q}", Job(8, [Part(A["w_down_2"], 0, full, rhs_of(f_pair), ("f_ready", 8 * q), row0=q * KT)], 2)))
        slab0 = group0 = 0
        for name, job in order:
            slab0, group0 = job.place(slab0, group0)
            jobs[name] = job
        names = [name for name, _ in order]

        stream_of_slabs = [(job, step, idx) for _, job in order for step in range(job.steps) for idx in range(job.S)]

        def load_slab(sp, job, i, u, idx):
            step = i * job.unroll + u
            n, n_static = job.slab(i, u, idx)
            p, _, k, kt, _ = job.pieces[idx]
            slot = n_static % STAGES
            sp.wait_ge(split_done, n + 1)
            sp.sem_inc(issued, 1)
            rows = slice((p.row0 + k) * P, (p.row0 + k + kt) * P)
            src = p.w[rows, bass.ds(p.col0 + step * p.stride, p.cols)] if p.stride else p.w[POOL_ORDER[step], :, :]
            sp.dma_start(stage[:, slot, 0:kt, 0:p.cols], src.rearrange("(k p) n -> p k n", p=P)).then_inc(landed[slot], 16)

        def round_high(act, job, i, u, idx):
            n, n_static = job.slab(i, u, idx)
            p, _, k, kt, _ = job.pieces[idx]
            slot, pr = n_static % STAGES, n_static % PAIRS
            act.wait_ge(landed[slot], 16 * (n_static // STAGES + 1) + i * (16 * (job.unroll * job.S // STAGES)))
            act.wait_ge(used, n + 1)
            act.activation(w_high[:, pr, 0:kt, 0:p.cols], stage[:, slot, 0:kt, 0:p.cols], ACT.Copy).then_inc(high_done, 1)

        def subtract_low(dve, job, i, u, idx):
            n, n_static = job.slab(i, u, idx)
            p, _, k, kt, _ = job.pieces[idx]
            slot, pr = n_static % STAGES, n_static % PAIRS
            dve.wait_ge(high_done, n + 1)
            dve.tensor_tensor(w_low[:, pr, 0:kt, 0:p.cols], stage[:, slot, 0:kt, 0:p.cols],
                              w_high[:, pr, 0:kt, 0:p.cols].bitcast(F32), ALU.subtract).then_inc(split_done, 1)

        def stream(eng, split, name, body=None, chain=None, links=0, beside=None):
            job = jobs[name]
            tail = -(-PAIRS // job.S)

            def step(i, u, known):
                for idx, (_, part, _, _, last) in enumerate(job.pieces):
                    ahead = u * job.S + idx + PAIRS
                    if known:
                        n = job.slab0 + i * job.unroll * job.S + ahead
                        if n < len(stream_of_slabs):
                            j2, s2, idx2 = stream_of_slabs[n]
                            split(eng, j2, s2 // j2.unroll, s2 % j2.unroll, idx2)
                    else:
                        split(eng, job, i, ahead // job.S, ahead % job.S)
                    if last and body:
                        body(i, u, part)
                    if beside:
                        beside((i * job.unroll + u) * job.S + idx)

            count = job.steps - tail
            looped = 0 if beside or count // job.unroll < 2 else count // job.unroll * job.unroll
            if looped:
                repeat(eng, looped, job.unroll, lambda i, u: step(i, u, False), chain, links * job.unroll)
            for n in range(looped, job.steps):
                step(n // job.unroll, n % job.unroll, True)

        def multiply(pe, job, i, u, beside=None):
            for idx, (p, part, k0, kt, last) in enumerate(job.pieces):
                n, n_static = job.slab(i, u, idx)
                if k0 == 0:
                    g, bank, _ = job.group(i, u, part)
                    pe.wait_ge(acc_free, g + 1)
                pr = n_static % PAIRS
                if p.ready:
                    name, before = p.ready
                    pe.wait_ge(s(name), before + ((0 if p.stride else 2 * u) + k0 + kt + 1) // 2)
                pe.wait_ge(split_done, STAGES + n + 1)
                for j in range(p.cols // P):
                    bk = acc[:, 2 * bank + j, :]
                    for k in range(kt):
                        first, final = k0 + k == 0, last and k == kt - 1
                        high, low = (w[:, pr, k, j * P:(j + 1) * P] for w in (w_high, w_low))
                        if p.wide:
                            a, b = p.rhs(k0 + k)
                            pe.matmul(bk[:, 0:TM], high, b, start=first, stop=False)
                            pe.matmul(bk[:, 0:TM], low, a, start=False, stop=False)
                            mm = pe.matmul(bk[:, 0:TM], high, a, start=False, stop=final)
                            continue
                        both, a = p.rhs(k0 + k if p.stride else 2 * POOL_ORDER[u] + k)
                        if first:
                            pe.matmul(bk, high, both, start=True, stop=False, skip_group_check=True)
                            pe.matmul(bk[:, 0:T], low, a, start=False, stop=False, skip_group_check=True)
                        else:
                            pe.matmul(bk[:, 0:T], low, a, start=False, stop=False, skip_group_check=True)
                            mm = pe.matmul(bk, high, both, start=False, stop=final, skip_group_check=True)
                mm.then_inc(used, 1)
                if beside:
                    beside((i * job.unroll + u) * job.S + idx)

        def group_done(eng, job, i, u, part=0):
            g, bank, last = job.group(i, u, part)
            eng.wait_ge(used, PAIRS + last + 1)
            return acc[:, 2 * bank:2 * bank + 2, :], g

        def folded(name, group):
            return 2 + jobs[name].group0 + group + 1

        def fold(dve, dst, banks):
            return dve.tensor_reduce(dst, banks.rearrange("p j (h t) -> p j t h", h=2), AX, ALU.add)

        block = ctx.enter_context(nc.Block())

        @block.sync
        def _(sp):
            def rows(name):
                v = A[name]
                return v.rearrange("(a n) -> a n", n=P)
            def load_rows(group, members, name_of_sem):
                at_row = 0
                for name, n in members:
                    sp.dma_start(prow[at_row:at_row + n, group, :], rows(name)).then_inc(s(name_of_sem), 16)
                    at_row += n
                return at_row

            def other_params():
                at_row = load_rows(1, ROWS1, "params_in")
                for name in HALF_ROWS:
                    for half in range(2):
                        sp.dma_start(prow[at_row:at_row + 1, 1, half * 64:half * 64 + 64], A[name].rearrange("(a n) -> a n", a=1)).then_inc(s("params_in"), 16)
                    at_row += 1
                taps = A["w_dw_2"].rearrange("t (c n) -> (t c) n", n=P)
                for half in range(2):
                    sp.dma_start(prow[0:DW_ROWS // 2, 2 + half, :], taps[half * DW_ROWS // 2:(half + 1) * DW_ROWS // 2, :]).then_inc(s("params_in"), 16)
                sp.dma_start(relb[:], A["rel_bias"]).then_inc(s("params_in"), 16)
                sp.dma_start(sinks, A["sinks_b"].partition_broadcast(P)).then_inc(s("sinks_in"), 16)

            load_rows(0, ROWS0, "params0_in")
            for name in names:
                job = jobs[name]
                if name == "mem_kv":
                    for step in range(job.steps):
                        for idx in range(job.S):
                            load_slab(sp, job, step // job.unroll, step % job.unroll, idx)
                        if step == 0:
                            other_params()
                    continue
                repeat(sp, job.steps, job.unroll, lambda i, u: [load_slab(sp, job, i, u, idx) for idx in range(job.S)])
            for e in range(8):
                r, t = e // 2, e % 2
                sp.wait_ge(s("rows_ready"), e + 1)
                sp.dma_start(out[0, t * P:(t + 1) * P, r * 512:(r + 1) * 512], rows_out[:, t, r * 512:(r + 1) * 512]).then_inc(s("stored"), 16)
            sp.wait_ge(s("stored"), 16 * 8)

        @block.gpsimd
        def _(pool):
            link = Chain(pool, pool_link)
            link(pool.memset(ones[:], 1.0))
            link(pool.memset(ident[:], 0.0))
            link(pool.affine_select(out=ident[:], in_=ident[:], compare_op=ALU.not_equal, fill=1.0, base=0,
                                    pattern=[[-1, P]], channel_multiplier=1))
            link(pool.memset(blocks[:], 0.0))
            link(pool.memset(blocks[0:64, 0:64], 1.0))
            link(pool.memset(blocks[64:128, 64:128], 1.0))
            link(pool.memset(zrow[:], 0.0))
            pool.sem_inc(s("consts"), 1)

            def gather_squares(count, first, width=2 * T, done=0):
                view = sumsq.rearrange("p a t -> p (a t)")[:, 0:width]
                for r in range(count):
                    q = first + r
                    pool.wait_ge(s("squared"), q + 1)
                    if r == 0:
                        pool.tensor_copy(view, square[:, q % 2, 0:width]).then_inc(s("gathered"), 1)
                    else:
                        pool.wait_ge(s("gathered"), q)
                        pool.tensor_tensor(view, view, square[:, q % 2, 0:width], ALU.add).then_inc(s("gathered"), 1)

            gather_squares(8, 0)
            pool.wait_ge(s("stats"), 1)
            gather_squares(8, 8)
            pool.wait_ge(s("turned_pe"), 16)
            link(pool.memset(flip[:], 0.0))
            pool.affine_select(out=flip[:], in_=flip[:], compare_op=ALU.not_equal, fill=1.0, base=1 - P,
                               pattern=[[1, P]], channel_multiplier=1).then_inc(s("flip_made"), 1)
            pool.wait_ge(s("turned_done"), 8)
            pool.dma_start(spill_x, turned[:]).then_inc(s("x_out"), 16)
            pool.wait_ge(s("bias_out"), 16)
            pool.wait_ge(used, PAIRS + jobs["ikw"].slab0)
            pool.dma_start(toep[:], bass.AP(bias_dram, 0, [[1, P], [2 * T, NB], [1, T]])).then_inc(s("toep_in"), 16)
            pool.wait_ge(s("flip_copied"), NB // 2)
            pool.affine_select(out=toep[:], in_=toep[:], compare_op=ALU.is_ge, fill=NEG, base=P,
                               pattern=[[0, NB], [-1, T]], channel_multiplier=1).then_inc(s("toep_masked"), 1)
            pool.wait_ge(s("toep_masked"), 1)
            tb = toep[:, A_HEADS:NB, :]
            pool.affine_select(out=tb, in_=tb, compare_op=ALU.is_ge, fill=NEG, base=WINDOW - 1 - P,
                               pattern=[[0, B_HEADS], [1, T]], channel_multiplier=-1).then_inc(s("toep_masked"), 1)
            pool.wait_ge(s("scored"), 1)
            for t in range(2):
                v = score[:, t * P:t * P + P * (t + 1)]
                pool.affine_select(out=v, in_=v, compare_op=ALU.is_ge, fill=NEG, base=t * P,
                                   pattern=[[-1, P * (t + 1)]], channel_multiplier=1).then_inc(s("score_masked"), 1)
            pool.wait_ge(s("topk"), 1)
            pool.wait_ge(s("toep_masked"), 2)
            for h in range(A_HEADS):
                if h >= 2:
                    pool.wait_ge(s("logits"), h - 1)
                mk = bias_mask[h % 2]
                pool.tensor_tensor(mk[:, 0:P], toep[:, h, P:T], work[:, 0:P], ALU.add).then_inc(s("masked"), 1)
                pool.tensor_tensor(mk[:, P:3 * P], toep[:, h, :], work[:, P:3 * P], ALU.add).then_inc(s("masked"), 1)

            pool.wait_ge(s("head_normed"), 14)
            pool.dma_start(bk_swap[0:64, :], late[64:128, L_BK, :]).then_inc(s("swapped"), 16)
            pool.dma_start(bk_swap[64:128, :], late[0:64, L_BK, :]).then_inc(s("swapped"), 16)

            def gated(first, src, gates, tiles):
                for r in range(tiles // 2):
                    q = first + r
                    pool.wait_ge(s("gate_sig"), q + 1)
                    v = gate[:, q % 2, 0:2 * T]
                    g2 = late[:, gates + 2 * r:gates + 2 * r + 2, :].rearrange("p a t -> p (a t)")
                    o2 = src[:, 2 * r:2 * r + 2, :].rearrange("p a t -> p (a t)")
                    link(pool.tensor_tensor(v, v, g2, ALU.mult))
                    pool.tensor_tensor(v, v, o2, ALU.mult).then_inc(s("gated"), 1)

            def merge(name, dst, steps0, add, beside=None):
                job = jobs[name]

                def body(i, u):
                    n = steps0 + i
                    pool.wait_ge(s("sig_ready"), n + 1)
                    pool.wait_ge(s("up_ready"), n + 1)
                    d2 = dst[:, bass.ds(i * 2, 2), :].rearrange("p a t -> p (a t)")
                    if add:
                        link(pool.tensor_tensor(gate[:, 1, 0:2 * T], gate[:, 0, 0:2 * T], tmp[:, 1, 0:2 * T], ALU.mult))
                        pool.tensor_tensor(d2, d2, gate[:, 1, 0:2 * T], ALU.add).then_inc(s("merged_step"), 1)
                    else:
                        pool.tensor_tensor(d2, gate[:, 0, 0:2 * T], tmp[:, 1, 0:2 * T], ALU.mult).then_inc(s("merged_step"), 1)
                    if beside:
                        beside(i)
                if beside:
                    for i in range(job.steps):
                        body(i, 0)
                else:
                    repeat(pool, job.steps, 1, body, link, 1 if add else 0)

            gated(0, early[:, E_AQ:E_AQ + 6, :], L_AGATE, 6)
            merge("w_up_a", merged, 0, False)
            gated(3, late[:, L_CQ:L_CQ + 4, :], L_CGATE, 4)
            merge("w_up_c", merged, 8, True)
            pool.wait_ge(s("x_out"), 16)
            pool.wait_ge(s("pv_copied"), len(HEADS))
            pool.dma_start(xT[:], spill_x).then_inc(s("x_back"), 16)
            gated(5, late[:, L_BQ:L_BQ + 6, :], L_BGATE, 6)
            merge("w_up_b", merged, 16, True)

            def add_square(q, parity, first=False):
                pool.wait_ge(s("squared"), q + 1)
                sq = square[:, parity, 0:2 * T].rearrange("p (a t) -> p a t", a=2)
                if first:
                    pool.tensor_copy(sumsq[:, :, META:TM], sq).then_inc(s("gathered"), 1)
                else:
                    pool.wait_ge(s("gathered"), q)
                    pool.tensor_tensor(sumsq[:, :, META:TM], sumsq[:, :, META:TM], sq, ALU.add).then_inc(s("gathered"), 1)

            pool.wait_ge(s("merged_ready"), 8)
            pool.dma_start(meta_in[:], A["meta_2"]).then_inc(s("meta_in"), 16)
            pool.wait_ge(s("x_back"), 16)
            for g in range(8):
                pool.wait_ge(s("folded"), g + 1)
                pool.tensor_tensor(h1[:, 2 * g:2 * g + 2, META:TM], tmp[:, g % 2, 0:2 * T].rearrange("p (a t) -> p a t", a=2),
                                   xT[:, 2 * g:2 * g + 2, :], ALU.add).then_inc(s("residual"), 1)
                if g >= 1:
                    add_square(16 + g - 1, (g - 1) % 2, g == 1)
            add_square(23, 1)
            pool.wait_ge(s("values_moved"), 4)
            for g in range(4):
                pool.wait_ge(s("glu_sig"), g + 1)
                v = glu[:, 2 * g:2 * g + 2, TAPS - 1 - META:]
                pool.tensor_tensor(v, v, gate[:, g % 2, :].rearrange("p (a t) -> p a t", a=2), ALU.mult).then_inc(s("glu_done"), 1)
            pool.wait_ge(s("glu_done"), 4)

            taps_done = [0]
            mine = range(DVE_TILES, 8)

            def conv_taps(count):
                for _ in range(count):
                    n = taps_done[0]
                    if n == len(mine) * TAPS:
                        return
                    taps_done[0] += 1
                    tap, k = n // len(mine), mine[n % len(mine)]
                    w = column("w_dw_2", 8 * tap + k)
                    if tap == 0:
                        ins = pool.tensor_scalar(conv[:, k, :], glu[:, k, 0:T], w, column("b_dw_2", k), ALU.mult, ALU.add)
                    else:
                        link(pool.tensor_scalar(product[:, n % 2, :], glu[:, k, tap:tap + T], w, None, ALU.mult))
                        pool.wait_ge(s("pool_taps"), n - len(mine) + 1)
                        ins = pool.tensor_tensor(conv[:, k, :], conv[:, k, :], product[:, n % 2, :], ALU.add)
                    ins.then_inc(s("pool_taps"), 1)

            for q, g in enumerate(POOL_ORDER):
                pool.wait_ge(s("pooled"), q + 1)
                src = z_pool[:, 2 * g:2 * g + 2, :]
                reach = 1
                for r in range(g + 1):
                    dst = window[:, r % 2, :].rearrange("p (a t) -> p a t", a=2)
                    link(pool.tensor_tensor(dst[:, :, 2 * reach - 1:TM], src[:, :, 2 * reach - 1:TM], src[:, :, reach - 1:TM - reach], ALU.add))
                    src = dst
                    reach *= 2
                v = window[:, (g + 1) % 2, 0:2 * T].rearrange("p (a t) -> p a t", a=2)
                link(pool.tensor_scalar(v, src[:, :, META:TM], 1.0 / reach, None, ALU.mult))
                link(pool.tensor_tensor(v, v, z_pool[:, 2 * g:2 * g + 2, META:TM], ALU.subtract))
                link(pool.tensor_copy(d_pair[:, 2 * g:2 * g + 2, 0, :], v))
                link(pool.tensor_tensor(d_pair[:, 2 * g:2 * g + 2, 1, :], v, d_pair[:, 2 * g:2 * g + 2, 0, :].bitcast(F32), ALU.subtract))
                pool.sem_inc(s("d_ready"), 1)
            conv_taps(8 * TAPS)
            merge("pool_out", m, 24, False)
            for g in range(8):
                pool.wait_ge(s("up_ready"), 32 + g + 1)
                pool.wait_ge(s("gate_b_sig"), g + 1)
                v = tmp[:, g % 2, 0:2 * T]
                link(pool.tensor_tensor(v, v, gate_b[:, 2 * g:2 * g + 2, :].rearrange("p a t -> p (a t)"), ALU.mult))
                d2 = m[:, 2 * g:2 * g + 2, :].rearrange("p a t -> p (a t)")
                pool.tensor_tensor(d2, d2, v, ALU.add).then_inc(s("merged_step"), 1)
            for g in range(8):
                add_square(24 + g, g % 2, g == 0)
            for r in range(8):
                pool.wait_ge(s("h2_part"), r + 1)
                v = h1[:, 2 * r:2 * r + 2, META:TM]
                pool.tensor_tensor(v, v, gate[:, r % 2, 0:2 * T].rearrange("p (a t) -> p a t", a=2), ALU.add).then_inc(s("h2"), 1)
            pool.wait_ge(s("stats"), 4)
            for g in range(8):
                add_square(32 + g, g % 2, g == 0)

            def add_down(q):
                job = jobs[f"w_down{q}"]

                def body(i, u):
                    g = i * job.unroll + u
                    pool.wait_ge(s("down"), q * 8 + g + 1)
                    d2 = y[:, bass.ds(g * 2, 2), :].rearrange("p a t -> p (a t)")
                    pool.tensor_tensor(d2, d2, tmp[:, u, 0:2 * T], ALU.add).then_inc(s("down_added"), 1)
                    if q == 3 and g >= 1:
                        add_square(40 + g - 1, (g - 1) % 2, g == 1)
                if q < 3:
                    repeat(pool, job.steps, job.unroll, body)
                    return
                pool.wait_ge(s("h2_sums"), 1)
                for g in range(job.steps):
                    body(g // 2, g % 2)
                add_square(47, 1)

            pool.wait_ge(s("h2"), 8)
            pool.wait_ge(s("h2_part"), 8)
            pool.memset(y[:], 0.0).then_inc(s("y_zero"), 1)
            pool.wait_ge(s("y_zero"), 1)
            pool.sem_inc(s("down_added"), 2)
            for q in range(4):
                add_down(q)

        @block.scalar
        def _(act):
            def rounding(name, body=None, beside=None):
                stream(act, round_high, name, body, beside=beside)

            std = [0]

            def load_rows(v, dst, name, c):
                cols = slice(c * 512, (c + 1) * 512)
                act.dma_start(dst[:, :, cols], v[:, cols].rearrange("(t p) d -> p t d", p=P)).then_inc(s(f"{name}{c}"), 16)
            for c in range(4):
                load_rows(A["mem"], mem_in, "mem_in", c)

            def root():
                r = RSTD[std[0]]
                std[0] += 1
                act.wait_ge(s("variance"), std[0])
                act.activation(r, r, ACT.Sqrt).then_inc(s("root"), 1)

            def high_part(pair, width, first, r):
                act.wait_ge(s("scaled"), first + r + 1)
                act.activation(pair[:, 2 * r:2 * r + 2, 0, :], tmp[:, r % 2, 0:2 * width].rearrange("p (a t) -> p a t", a=2),
                               ACT.Copy).then_inc(s("pair_high"), 1)

            def high_parts(pair, width, first):
                for r in range(8):
                    high_part(pair, width, first, r)

            def square_turned(e):
                if e >= 2:
                    act.wait_ge(s("gathered"), e - 1)
                act.activation(square[:, e % 2, 0:2 * T], aux[:, 1 + e % 3, :], ACT.Square).then_inc(s("squared"), 1)

            for e in range(8):
                act.wait_ge(s("turned_pe"), e + 1)
                square_turned(e)
                high_part(mem_pair, T, 0, e)
                if e >= 4:
                    load_rows(A["x"], x_in, "x_in", e - 4)
                if e % 2:
                    round_high(act, jobs["mem_kv"], 0, 0, e // 2)

            def beside_mem(n):
                if n == 2:
                    root()
                if 0 <= n - X_AT < 8:
                    e = n - X_AT
                    act.wait_ge(s("turned_pe"), 8 + e + 1)
                    act.activation(turned[:, 2 * e:2 * e + 2, :], aux[:, 1 + (8 + e) % 3, :].rearrange("p (a t) -> p a t", a=2),
                                   ACT.Copy).then_inc(s("turned_done"), 1)
                    square_turned(8 + e)
                if n == X_NORM_AT:
                    act.wait_ge(s("bias_rows"), 1)
                    act.dma_start(bias_dram.ap(), brow[:]).then_inc(s("bias_out"), 16)
                    root()
                if 0 <= n - X_NORM_AT - 1 < 4:
                    for r in (2 * (n - X_NORM_AT - 1), 2 * (n - X_NORM_AT - 1) + 1):
                        high_part(hT, T, 8, r)
            rounding("mem_kv", beside=beside_mem)
            rounding("ikw")

            def norm_steps(name, n):
                q = stages(NORM_AT[name], n, 0)
                if q is not None:
                    src, width, _, _, _, (job, group), _ = HEAD_NORMS[q]
                    if q == 0:
                        act.wait_ge(s("ik_copied"), 1)
                    act.wait_ge(acc_free, folded(job, group))
                    if q >= 1:
                        act.wait_ge(s("head_stats"), q)
                    act.activation(square[:, 0, 0:width], src, ACT.Square).then_inc(s("head_squared"), 1)
                q = stages(NORM_AT[name], n, 2)
                if q is not None:
                    w = T if HEAD_NORMS[q][4] else HEAD_NORMS[q][1]
                    act.wait_ge(s("head_var"), q + 1)
                    act.activation(rstd[:, 0:w], rstd[:, 0:w], ACT.Sqrt).then_inc(s("head_root"), 1)

            def index_steps(name, n):
                first = stages(INDEX_AT[name], n, 0)
                for h in () if first is None else (first, first + 1):
                    act.wait_ge(s("idx_products"), h + 1)
                    if h >= 2:
                        act.wait_ge(s("idx_added"), 2 * (h - 1))
                    act.activation(lg[:, h % 2, 0:3 * P], aux[:, 2 + h % 2, 0:3 * P], ACT.Relu).then_inc(s("idx_relu"), 1)

            def head_steps(name, n):
                h = stages(HEAD_AT[name], n, 5)
                if h is not None:
                    _, turned_p, w = logits_of(h)
                    act.wait_ge(s("probs_turned"), h + 1)
                    if h >= 2:
                        act.wait_ge(s("pv"), h - 1)
                    act.activation(turned_p, aux[:, 2, 0:w], ACT.Copy).then_inc(s("probs_copied"), 1)
                h = stages(HEAD_AT[name], n, 1)
                if h is not None:
                    kind, c = HEADS[h]
                    l, _, _ = logits_of(h)
                    b = h % 2
                    act.wait_ge(s("logits"), h + 1)
                    for t in range(2):
                        lo, hi = head_cols(kind, t)
                        act.activation(l[:, lo:hi], l[:, lo:hi], ACT.Exp, bias=negmax[:, b, t:t + 1],
                                       accum_out=denom[:, b, t:t + 1]).then_inc(s("exps"), 1)
                    if kind == "B":
                        for t in range(2):
                            act.activation(esink[:, b, t:t + 1], sinks[:, c:c + 1], ACT.Exp, bias=negmax[:, b, t:t + 1]).then_inc(s("sink_exps"), 1)

            def beside_early(n):
                norm_steps("early", n)
                if 0 <= n - FLIP_AT < NB // 2:
                    r = n - FLIP_AT
                    act.wait_ge(s("flipped"), r + 1)
                    act.activation(toep[:, 2 * r:2 * r + 2, :], aux[:, 2 + r % 2, :].rearrange("p (a t) -> p a t", a=2), ACT.Copy).then_inc(s("flip_copied"), 1)
                index_steps("early", n)

            def silu_step(q, gates, r):
                if q >= 2:
                    act.wait_ge(s("o_split"), q - 1)
                g2 = late[:, gates + 2 * r:gates + 2 * r + 2, :]
                act.activation(gate[:, q % 2, 0:2 * T].rearrange("p (a t) -> p a t", a=2), g2, ACT.Sigmoid).then_inc(s("gate_sig"), 1)

            def beside_late(n):
                index_steps("late", n)
                norm_steps("late", n)
                head_steps("late", n)
                if 0 <= n - SILU_AT < 3:
                    if n == SILU_AT:
                        act.wait_ge(s("probs_turned"), A_HEADS)
                    silu_step(n - SILU_AT, L_AGATE, n - SILU_AT)

            rounding("early", beside=beside_early)
            rounding("kv_up")
            rounding("late", beside=beside_late)

            def silu(name, first, steps, gates, rounds, n):
                if n < rounds:
                    if n == 0:
                        act.wait_ge(s("merged_step"), steps)
                    silu_step(first + n, gates, n)

            def gate_groups(name, steps0, bias, beside=None, split_before=3):
                def body(i, u, part):
                    if part == 1:
                        return
                    i = i * jobs[name].unroll + u
                    n = steps0 + i
                    act.wait_ge(s("gate_in"), n + 1)
                    if n:
                        act.wait_ge(s("merged_step"), n)
                    if i == 0:
                        act.wait_ge(s("o_split"), split_before)
                    for j in range(2):
                        b = params[:, bass.ds(COL["gate_bias"] + bias + i * 2 + j, 1)] if bias is not None else 0.0
                        act.activation(gate[:, 0, j * T:(j + 1) * T], tmp[:, 0, j * T:(j + 1) * T], ACT.Sigmoid,
                                       bias=b).then_inc(s("sig_half") if j == 0 else s("sig_ready"), 1)
                rounding(name, body, beside)

            def beside_up_c(n):
                silu("w_up_c", 3, 8, L_CGATE, 2, n)
                head_steps("w_up_c", n)

            gate_groups("w_up_a", 0, 0, lambda n: head_steps("w_up_a", n))
            gate_groups("w_up_c", 8, 32, beside_up_c, 5)
            gate_groups("w_up_b", 16, 16, lambda n: silu("w_up_b", 5, 16, L_BGATE, 3, n), 8)

            def square_of(v, parity, q):
                act.wait_ge(s("gathered"), q - 1)
                act.activation(square[:, parity, 0:2 * T].rearrange("p (a t) -> p a t", a=2), v, ACT.Square).then_inc(s("squared"), 1)

            def sq_residual(i, u, part):
                g = 2 * i + u
                act.wait_ge(s("residual"), 2 + g + 1)
                square_of(h1[:, bass.ds(2 * g, 2), META:TM], u, 16 + g)
            rounding("w_o", sq_residual)
            root()
            high_parts(uT, TM, 16)

            rounding("values")

            def glu_body(i, u, part):
                g = 2 * i + u
                banks, _ = group_done(act, jobs["gates"], i, u)
                if g >= 2:
                    act.wait_ge(s("glu_done"), g - 1)
                act.activation(gate[:, g % 2, :].rearrange("p (a t) -> p a t", a=2), banks[:, :, 0:TM], ACT.Sigmoid).then_inc(s("glu_sig"), 1)
            rounding("gates", glu_body)
            rounding("pools")

            def layer_norm_steps(n):
                r = n - LN_SLAB - 2
                if 0 <= r < 4:
                    act.wait_ge(s("conv_centered"), r + 1)
                    if r >= 2:
                        act.wait_ge(s("conv_squares"), r - 1)
                    act.activation(square[:, r % 2, 0:2 * T], conv[:, 2 * r:2 * r + 2, :].rearrange("p a t -> p (a t)"), ACT.Square).then_inc(s("conv_sq"), 1)
                if r == 4:
                    root()
                q = r - 5
                if 1 <= q < 5:
                    conv_high(q - 1)
                if 0 <= q < 4:
                    act.wait_ge(s("conv_scaled"), q + 1)
                    for k in (2 * q, 2 * q + 1):
                        act.activation(square[:, q % 2, (k % 2) * T:(k % 2 + 1) * T], conv[:, k, :], ACT.Sigmoid,
                                       bias=column("conv_ln_b_2", k), scale=column("conv_ln_g_2", k)).then_inc(s("conv_sig"), 1)
                        act.wait_ge(s("conv_sig"), k + 1)
                        act.activation(conv[:, k, :], conv[:, k, :], ACT.Identity,
                                       bias=column("conv_ln_b_2", k), scale=column("conv_ln_g_2", k)).then_inc(s("conv_affine"), 1)

            def conv_high(q):
                act.wait_ge(s("conv_used"), q + 1)
                if q >= 2:
                    act.wait_ge(s("conv_ready"), q)
                act.activation(conv_pair[:, 2 * q:2 * q + 2, 0, :], conv[:, 2 * q:2 * q + 2, :], ACT.Copy).then_inc(s("conv_high"), 1)

            def gate_b_body(i, u, part):
                g = 2 * i + u
                act.wait_ge(acc_free, folded("conv_gates", g))
                v = gate_b[:, bass.ds(2 * g, 2), :]
                act.activation(v, v, ACT.Sigmoid).then_inc(s("gate_b_sig"), 1)

            def m_high(g):
                act.wait_ge(s("merged_step"), 32 + g + 1)
                act.activation(m_pair[:, 2 * g:2 * g + 2, 0, :], m[:, 2 * g:2 * g + 2, :], ACT.Copy).then_inc(s("m_high"), 1)

            def conv_out_body(i, u, part):
                if 4 * i + u >= 1:
                    m_high(4 * i + u - 1)

            rounding("conv_gates", gate_b_body)
            rounding("pool_grp")
            gate_groups("pool_out", 24, None, layer_norm_steps)
            rounding("conv_out", conv_out_body)
            m_high(7)

            def sq_mixed(i, u, part):
                g = 2 * i + u
                act.wait_ge(s("mixed"), g + 1)
                square_of(mixed[:, bass.ds(2 * g, 2), :], u, 24 + g)
            rounding("w_o_2", sq_mixed)
            root()
            for r in range(8):
                act.wait_ge(s("h2"), r + 1)
                act.wait_ge(s("pair_ready"), 24 + max(r - 1, 0))
                for a in range(2):
                    k = 2 * r + a
                    act.activation(tmp[:, r % 2, a * T:(a + 1) * T], h1[:, k, META:TM], ACT.Copy, scale=column("g_pre_mlp_2", k)).then_inc(s("mlp_scaled"), 1)
                act.wait_ge(s("mlp_scaled"), 2 * r + 2)
                act.activation(u2[:, 2 * r:2 * r + 2, 0, :], tmp[:, r % 2, 0:2 * T].rearrange("p (a t) -> p a t", a=2), ACT.Copy).then_inc(s("pair_high"), 1)

            def square_residual(n):
                if n < 8:
                    square_of(h1[:, 2 * n:2 * n + 2, META:TM], n % 2, 32 + n)

            def finish_down(g):
                act.wait_ge(s("down_added"), 2 + 24 + g + 1)
                square_of(y[:, 2 * g:2 * g + 2, :], g % 2, 40 + g)
                act.wait_ge(s("squared"), 41 + g)
                for k in (2 * g, 2 * g + 1):
                    act.activation(y[:, k, :], y[:, k, :], ACT.Copy, scale=column("g_post_mlp_2", k)).then_inc(s("y_scaled"), 1)

            def last_down(i, u, part):
                if 2 * i + u >= 1:
                    finish_down(2 * i + u - 1)

            def residual_rows(n):
                if n % 3 == 0 and n < 24:
                    e = n // 3
                    r, t = e // 2, e % 2
                    act.wait_ge(s("h_turned"), e + 1)
                    act.activation(rows_h[:, t, r * 512:(r + 1) * 512], aux[:, e % 4, :], ACT.Copy).then_inc(s("h_rows"), 1)

            for q in range(4):
                rounding(f"w_up{q}", beside=square_residual if q == 0 else None)
                rounding(f"w_down{q}", last_down if q == 3 else None, residual_rows if q == 3 else None)
            finish_down(7)
            act.wait_ge(s("out_var"), 1)
            act.activation(out_ms, out_ms, ACT.Sqrt).then_inc(s("out_root"), 1)

        @block.tensor
        def _(pe):
            def products(name, beside=None):
                job = jobs[name]
                if beside:
                    for step in range(job.steps):
                        multiply(pe, job, step // job.unroll, step % job.unroll, beside)
                    return
                repeat(pe, job.steps, job.unroll, lambda i, u: multiply(pe, job, i, u))

            def stat(width, gathered):
                pe.wait_ge(s("gathered"), gathered)
                v = sumsq.rearrange("p a t -> p (a t)")
                for a in range(2):
                    mm = pe.matmul(aux[:, 0, 0:width], ones[:], v[:, a * width:(a + 1) * width], start=(a == 0), stop=(a == 1))
                mm.then_inc(s("stats"), 1)

            def stat_wide(width, gathered, lo):
                pe.wait_ge(s("gathered"), gathered)
                for a in range(2):
                    mm = pe.matmul(aux[:, 0, 0:width], ones[:], sumsq[:, a, lo:TM], start=(a == 0), stop=(a == 1))
                mm.then_inc(s("stats"), 1)

            pe.sem_inc(used, PAIRS)
            pe.wait_ge(s("consts"), 1)
            pe.wait_ge(s("params0_in"), 16 * len(ROWS0))
            pe.transpose(aux[:, 0, 0:N0], prow[0:N0, 0, :], ident[0:N0, 0:N0]).then_inc(s("params_turned"), 1)

            def turn(src, name, e):
                pe.wait_ge(s(f"{name}{e % 8 // 2}"), 16)
                if e >= 3:
                    pe.wait_ge(s("squared"), e - 2)
                    pe.wait_ge(s("scaled"), min(e - 2, 8))
                for k in range(2):
                    for t in range(2):
                        kt = 2 * (e % 8) + k
                        mm = pe.transpose(aux[:, 1 + e % 3, (2 * k + t) * P:(2 * k + t + 1) * P], src[:, t, kt * P:(kt + 1) * P], ident[:])
                mm.then_inc(s("turned_pe"), 1)

            for e in range(8):
                turn(mem_in, "mem_in", e)

            def beside_mem(n):
                if n == 0:
                    pe.wait_ge(s("params_copied"), 1)
                    stat(T, 8)
                if n == 1:
                    pe.wait_ge(s("variance"), 1)
                    pe.wait_ge(s("params_in"), 16 * (len(ROWS1) + 2 * len(HALF_ROWS) + 3))
                    for q, (c0, w) in enumerate(PARAM_GROUPS[1:]):
                        pe.transpose(aux[:, 0, q * P:q * P + w], prow[0:w, 1 + q, :], ident[0:w, 0:w])
                    pe.transpose(aux[0:NB, 0, 3 * P:3 * P + BUCKETS], relb[:], ident[0:BUCKETS, 0:BUCKETS]).then_inc(s("params_turned"), 1)
                if 0 <= n - X_AT < 8:
                    turn(x_in, "x_in", 8 + n - X_AT)
                if n == X_NORM_AT:
                    pe.wait_ge(s("params_copied"), 5)
                    stat(T, 16)
            products("mem_kv", beside_mem)
            products("ikw")

            def norm_steps(name, n):
                q = stages(NORM_AT[name], n, 1)
                if q is None:
                    return
                _, width, mat, _, both, _, _ = HEAD_NORMS[q]
                pe.wait_ge(s("head_squared"), q + 1)
                if q >= 1:
                    pe.wait_ge(s("head_var"), q)
                if both:
                    for a in range(2):
                        mm = pe.matmul(aux[:, 1, 0:T], mat[:], square[:, 0, a * T:(a + 1) * T], start=(a == 0), stop=(a == 1))
                else:
                    mm = pe.matmul(aux[:, 1, 0:width], mat[:], square[:, 0, 0:width], start=True, stop=True)
                mm.then_inc(s("head_stats"), 1)

            def index_steps(name, n):
                first = stages(INDEX_AT[name], n, 0)
                for h in () if first is None else (first, first + 1):
                    pe.wait_ge(s("ik_ready"), 1)
                    pe.wait_ge(acc_free, folded("early", E_IQ // 2 + h // 4))
                    if h >= 2:
                        pe.wait_ge(s("idx_relu"), h - 1)
                    r = (h % 2) * 64
                    q = early[r:r + 64, E_IQ + h // 2, :]
                    pe.matmul(aux[:, 2 + h % 2, 0:P], q[:, 0:P], ikn[r:r + 64, 0:P], start=True, stop=True)
                    pe.matmul(aux[:, 2 + h % 2, P:3 * P], q[:, P:T], ikn[r:r + 64, :], start=True, stop=True).then_inc(s("idx_products"), 1)

            def beside_early(n):
                if n == 0:
                    pe.wait_ge(acc_free, folded("ikw", 0))
                    pe.wait_ge(s("center"), 2)
                    pe.matmul(aux[:, 1, 0:T], center[:], ikw[0:IDX_DIM, :], start=True, stop=True).then_inc(s("ik_centered"), 1)
                    for t in range(2):
                        mm = pe.transpose(aux[:, 2, t * P:(t + 1) * P], ikw[:, t * P:(t + 1) * P], ident[:])
                    mm.then_inc(s("iw_turned"), 1)
                norm_steps("early", n)
                if 0 <= n - FLIP_AT < NB // 2:
                    r = n - FLIP_AT
                    if r == 0:
                        pe.wait_ge(s("toep_in"), 16)
                        pe.wait_ge(s("flip_made"), 1)
                        pe.wait_ge(s("iw_ready"), 1)
                    if r >= 2:
                        pe.wait_ge(s("flip_copied"), r - 1)
                    pe.matmul(aux[:, 2 + r % 2, :], flip[:], toep[:, 2 * r:2 * r + 2, :], start=True, stop=True).then_inc(s("flipped"), 1)
                if n == FLIP_AT + NB // 2:
                    pe.wait_ge(s("flip_copied"), NB // 2)
                index_steps("early", n)

            def value_steps(n):
                v = VALUES_AT.get(n)
                if v is None:
                    return
                if v < 6:
                    src = akv[:, 6 + v, :]
                    pe.wait_ge(acc_free, folded("kv_up", 3 + v // 2))
                    pe.wait_ge(s("idx_relu"), IDX_HEADS)
                elif v == 6:
                    src = late[:, L_BV, :]
                    pe.wait_ge(acc_free, folded("late", L_BV // 2))
                    pe.wait_ge(s("pv_copied"), A_HEADS)
                else:
                    src = mkv[:, 4 + v - 7, :]
                if v >= 1:
                    pe.wait_ge(s("values_copied"), v)
                for t in range(2):
                    mm = pe.transpose(aux[:, 3, t * P:(t + 1) * P], src[:, t * P:(t + 1) * P], ident[:])
                mm.then_inc(s("values_turned"), 1)

            def head_logits(h):
                kind, c = HEADS[h]
                pe.wait_ge(s("head_normed"), NORMS_A if kind == "A" else NORMS_ALL)
                if h >= 1:
                    pe.wait_ge(s("logits"), h)
                if kind == "A":
                    q, k = early[:, E_AQ + c, :], akv[:, c, :]
                elif kind == "C":
                    q, k = late[:, L_CQ + c, :], mkv[:, c, :]
                else:
                    pe.wait_ge(s("swapped"), 32)
                    r = (c % 2) * 64
                    q = late[r:r + 64, L_BQ + c // 2, :]
                    k = late[r:r + 64, L_BK, :] if c // (B_HEADS // 2) == c % 2 else bk_swap[r:r + 64, :]
                for t in range(2):
                    lo, hi = head_cols(kind, t)
                    mm = pe.matmul(aux[:, 0, lo:hi], q[:, t * P:(t + 1) * P], k[:, 0:hi - lo], start=True, stop=True)
                mm.then_inc(s("qk"), 1)

            def turn_probs(h):
                l, _, w = logits_of(h)
                pe.wait_ge(s("probs"), h + 1)
                if h >= 1:
                    pe.wait_ge(s("probs_copied"), h)
                for c in range(w // P):
                    mm = pe.transpose(aux[:, 2, c * P:(c + 1) * P], l[:, c * P:(c + 1) * P], ident[:])
                mm.then_inc(s("probs_turned"), 1)

            def weigh_values(h):
                kind, c = HEADS[h]
                _, p, _ = logits_of(h)
                pe.wait_ge(s("probs_copied"), h + 1)
                pe.wait_ge(s("values_copied"), 6 if kind == "A" else 11)
                if h >= 1:
                    pe.wait_ge(s("pv_copied"), h)
                dst = aux[:, 3, 0:T]
                if kind == "A":
                    v, lo, hi = v_a, c * P, (c + 1) * P
                elif kind == "C":
                    v, lo, hi = v_c, c * P, (c + 1) * P
                else:
                    v, lo, r = v_b, c // (B_HEADS // 2) * 64, (c % 2) * 64
                    hi = lo + 64
                    dst = aux[r:r + 64, 3, 0:T]
                if kind == "C":
                    for t in range(2):
                        for st in range(2):
                            at = (2 * t + st) * P
                            mm = pe.matmul(dst[:, t * P:(t + 1) * P], v[:, st, lo:hi], p[:, at:at + P], start=(st == 0), stop=(st == 1))
                else:
                    pe.matmul(dst[:, 0:P], v[:, 0, lo:hi], p[:, 0:P], start=True, stop=True)
                    pe.matmul(dst[:, P:T], v[:, 0, lo:hi], p[:, P:2 * P], start=True, stop=False)
                    mm = pe.matmul(dst[:, P:T], v[:, 1, lo:hi], p[:, 2 * P:3 * P], start=False, stop=True)
                mm.then_inc(s("pv"), 1)

            def head_steps(name, n):
                for lag, stage in ((7, weigh_values), (5, turn_probs), (0, head_logits)):
                    h = stages(HEAD_AT[name], n, lag)
                    if h is not None:
                        stage(h)

            def beside_late(n):
                index_steps("late", n)
                norm_steps("late", n)
                value_steps(n)
                head_steps("late", n)

            products("early", beside_early)
            products("kv_up")
            products("late", beside_late)
            products("w_up_a", lambda n: head_steps("w_up_a", n))
            products("w_up_c", lambda n: head_steps("w_up_c", n))
            def meta_step(n):
                if n == META_AT:
                    pe.wait_ge(s("meta_in"), 16)
                    pe.wait_ge(s("pv_copied"), len(HEADS))
                    for k in range(KT):
                        mm = pe.transpose(aux[:, 1, k * META:(k + 1) * META], meta_in[:, k * P:(k + 1) * P], ident[0:META, 0:META])
                    mm.then_inc(s("meta_turned"), 1)
            products("w_up_b")
            products("w_o", meta_step)
            pe.wait_ge(s("meta_sums"), 1)
            stat_wide(TM, 24, 0)
            for name in ("values", "gates", "pools", "conv_gates", "pool_grp"):
                products(name)

            def layer_norm_sums(n):
                if n == LN_SLAB:
                    pe.wait_ge(s("conv_done"), 1)
                    pe.wait_ge(s("pool_taps"), (8 - DVE_TILES) * TAPS)
                    for k in range(8):
                        mm = pe.matmul(aux[:, 1, 0:T], ones[:], conv[:, k, :], start=(k == 0), stop=(k == 7))
                    mm.then_inc(s("conv_sum"), 1)
                r = n - LN_SLAB - 3
                if 0 <= r < 4:
                    pe.wait_ge(s("conv_sq"), r + 1)
                    for a in range(2):
                        mm = pe.matmul(aux[:, 0, 0:T], ones[:], square[:, r % 2, a * T:(a + 1) * T], start=(r == 0 and a == 0), stop=(r == 3 and a == 1))
                    mm.then_inc(s("conv_squares"), 1)
            products("pool_out", layer_norm_sums)
            for name in ("conv_out", "w_o_2"):
                products(name)
            stat_wide(T, 32, META)

            def token_sums(bank, gathered):
                pe.wait_ge(s("gathered"), gathered)
                for t in range(2):
                    for a in range(2):
                        mm = pe.matmul(bank[:, t:t + 1], sumsq[:, a, META + t * P:META + (t + 1) * P], ones[:, 0:1], start=(a == 0), stop=(a == 1))
                return mm

            def residual_rows(n):
                if n % 3 == 0 and n < 24:
                    e = n // 3
                    r, t = e // 2, e % 2
                    if e >= 4:
                        pe.wait_ge(s("h_rows"), e - 3)
                    for k in range(4):
                        mm = pe.transpose(aux[:, e % 4, k * P:(k + 1) * P], h1[:, 4 * r + k, META + t * P:META + (t + 1) * P], ident[:])
                    mm.then_inc(s("h_turned"), 1)

            for q in range(4):
                products(f"w_up{q}")
                if q == 0:
                    pe.wait_ge(s("variance"), 5)
                    token_sums(aux[:, 0, :], 40).then_inc(s("h2_sums"), 1)
                products(f"w_down{q}", residual_rows if q == 3 else None)

            def turn_result(e):
                r, t = e // 2, e % 2
                pe.wait_ge(s("y_scaled"), 4 * r + 4)
                if e >= 4:
                    pe.wait_ge(s("rows_ready"), e - 3)
                for k in range(4):
                    mm = pe.transpose(aux[:, e % 4, k * P:(k + 1) * P], y[:, 4 * r + k, t * P:(t + 1) * P], ident[:])
                mm.then_inc(s("out_turned"), 1)
            pe.wait_ge(s("h_rows"), 8)
            for e in range(4):
                turn_result(e)
            pe.wait_ge(acc_free, folded("w_down3", 7))
            token_sums(acc[:, 0, :], 48).then_inc(s("out_sums"), 1)
            for e in range(4, 8):
                turn_result(e)

        @block.vector
        def _(dve):
            link = Chain(dve, dve_link)

            dve.sem_inc(split_done, STAGES)
            dve.sem_inc(acc_free, 2)
            dve.wait_ge(s("params_turned"), 1)
            dve.tensor_copy(params[:, 0:N0], aux[:, 0, 0:N0]).then_inc(s("params_copied"), 1)
            dve.wait_ge(s("params_copied"), 1)

            def other_params():
                dve.wait_ge(s("params_turned"), 2)
                for q, (c0, n) in enumerate(PARAM_GROUPS[1:]):
                    dve.tensor_copy(params[:, c0:c0 + n], aux[:, 0, q * P:q * P + n]).then_inc(s("params_copied"), 1)
                dve.tensor_copy(relT[:], aux[0:NB, 0, 3 * P:3 * P + BUCKETS]).then_inc(s("params_copied"), 1)
                dve.wait_ge(s("params_copied"), 5)

            def bias_rows(eighth):
                dve.wait_ge(s("consts"), 1)
                for b in range(eighth * BUCKETS // 8, (eighth + 1) * BUCKETS // 8):
                    lo = T - starts[b + 1]
                    hi = T - starts[b] if b else 2 * T
                    mm = dve.tensor_scalar(brow[:, lo:hi], zrow[:, lo:hi], relT[:, b:b + 1], None, ALU.add)
                if eighth < 7:
                    return
                mm.then_inc(s("bias_rows"), 1)
                for half in range(2):
                    dve.tensor_scalar(center[:, half * 64:half * 64 + 64], ident[0:64, 0:64], 1.0 / IDX_DIM, None, ALU.subtract).then_inc(s("center"), 1)

            stat_n = [0]

            def variance(width, inv_d, eps, src=None):
                r = RSTD[stat_n[0]]
                stat_n[0] += 1
                if src is None:
                    dve.wait_ge(s("stats"), src_stats[0] + 1)
                    src_stats[0] += 1
                    src = aux[:, 0, 0:width]
                dve.tensor_scalar(r, src, inv_d, eps, ALU.mult, ALU.add).then_inc(s("variance"), 1)

            def inverse_root():
                r = RSTD[stat_n[0] - 1]
                dve.wait_ge(s("root"), stat_n[0])
                link(dve.reciprocal(r, r))

            def inverse_std(width, inv_d, eps, src=None):
                variance(width, inv_d, eps, src)
                inverse_root()
            src_stats = [0]

            def low_part(pair, width, first, r):
                dve.wait_ge(s("pair_high"), first + r + 1)
                dve.tensor_tensor(pair[:, 2 * r:2 * r + 2, 1, :], tmp[:, r % 2, 0:2 * width].rearrange("p (a t) -> p a t", a=2),
                                  pair[:, 2 * r:2 * r + 2, 0, :].bitcast(F32), ALU.subtract).then_inc(s("pair_ready"), 1)

            def scale_tiles(src, width, gain, first, r, by=None):
                dve.wait_ge(s("pair_ready"), first + max(r - 1, 0))
                for a in range(2):
                    k = 2 * r + a
                    dst = tmp[:, r % 2, a * width:(a + 1) * width]
                    if by is None:
                        ins = dve.tensor_scalar(dst, src(k), column(gain, k), None, ALU.mult)
                    else:
                        ins = dve.scalar_tensor_tensor(out=dst, in0=src(k), scalar=column(gain, k), in1=by, op0=ALU.mult, op1=ALU.mult)
                    if a == 0:
                        ins.then_inc(s("scaled_half"), 1)
                    else:
                        dve.wait_ge(s("scaled_half"), first + r + 1)
                        ins.then_inc(s("scaled"), 1)

            def normalize(src, pair, width, gain, first, by):
                for r in range(8):
                    scale_tiles(src, width, gain, first, r, by)
                    if r >= 1:
                        low_part(pair, width, first, r - 1)
                low_part(pair, width, first, 7)

            for e in range(8):
                dve.wait_ge(s("squared"), e + 1)
                if e >= 2:
                    dve.wait_ge(s("pair_ready"), e - 1)
                for a in range(2):
                    ins = dve.tensor_scalar(tmp[:, e % 2, a * T:(a + 1) * T], aux[:, 1 + e % 3, a * T:(a + 1) * T],
                                            column("mem_norm_g", 2 * e + a), None, ALU.mult)
                    if a == 0:
                        ins.then_inc(s("scaled_half"), 1)
                    else:
                        dve.wait_ge(s("scaled_half"), e + 1)
                        ins.then_inc(s("scaled"), 1)
                if e >= 1:
                    low_part(mem_pair, T, 0, e - 1)
                if e % 2:
                    subtract_low(dve, jobs["mem_kv"], 0, 0, e // 2)
            low_part(mem_pair, T, 0, 7)

            def splitting(name, body, links=0, beside=None):
                stream(dve, subtract_low, name, body, link, links, beside)

            def fold_into(name, dst, tile0=0, done=None):
                job = jobs[name]

                def body(i, u, part):
                    banks, _ = group_done(dve, job, i, u)
                    g = i * job.unroll + u
                    ins = fold(dve, dst[:, bass.ds(tile0 + g * 2, 2), :], banks)
                    ins.then_inc(acc_free, 1)
                return body


            def mem_kv_body(i, u, part):
                banks, _ = group_done(dve, jobs["mem_kv"], i, u)
                g = 2 * i + u
                link(fold(dve, mkv[:, 2 * g:2 * g + 2, :], banks))
                for k in (2 * g, 2 * g + 1):
                    link(dve.tensor_tensor(mkv[:, k, :], mkv[:, k, :], rstd[:, T:2 * T], ALU.mult))
                dve.sem_inc(acc_free, 1)

            def beside_mem(n):
                if n == 0:
                    variance(T, 1.0 / D, EPS)
                if n == 1:
                    other_params()
                if 0 <= n - 2 < 8:
                    bias_rows(n - 2)
                if n == 2:
                    inverse_root()
                if n == X_NORM_AT:
                    inverse_std(T, 1.0 / D, EPS)
                    dve.wait_ge(s("bias_out"), 16)
                if 0 <= n - X_NORM_AT - 1 < 4:
                    for r in (2 * (n - X_NORM_AT - 1), 2 * (n - X_NORM_AT - 1) + 1):
                        scale_tiles(lambda k: turned[:, k, :], T, "norm_g", 8, r, rstd[:, 0:T])
                        if r >= 1:
                            low_part(hT, T, 8, r - 1)
                if n == X_NORM_AT + 5:
                    low_part(hT, T, 8, 7)
            splitting("mem_kv", mem_kv_body, beside=beside_mem)
            def ikw_body(i, u, part):
                banks, _ = group_done(dve, jobs["ikw"], i, u)
                dve.tensor_reduce(ikw[:], banks[:, 0, :].rearrange("p (h t) -> p t h", h=2), AX, ALU.add).then_inc(acc_free, 1)
            splitting("ikw", ikw_body)

            def norm_steps(name, n):
                q = stages(NORM_AT[name], n, 1)
                if q is not None:
                    _, width, _, inv, both, _, _ = HEAD_NORMS[q]
                    w = T if both else width
                    dve.wait_ge(s("head_stats"), q + 1)
                    if q:
                        dve.wait_ge(s("head_normed"), q)
                    dve.tensor_scalar(rstd[:, 0:w], aux[:, 1, 0:w], inv, EPS, ALU.mult, ALU.add).then_inc(s("head_var"), 1)
                q = stages(NORM_AT[name], n, 2)
                if q is None:
                    return
                src, width, _, _, both, _, gain = HEAD_NORMS[q]
                w = T if both else width
                dve.wait_ge(s("head_root"), q + 1)
                link(dve.reciprocal(rstd[:, 0:w], rstd[:, 0:w]))
                if both:
                    dve.wait_ge(s("x_out"), 16)
                    for a in range(2):
                        link(dve.scalar_tensor_tensor(out=tmp[:, 0, a * T:(a + 1) * T], in0=src[:, a * T:(a + 1) * T], scalar=params[:, gain + a:gain + a + 1],
                                                      in1=rstd[:, 0:T], op0=ALU.mult, op1=ALU.mult))
                    v = tmp[:, 0, 0:2 * T].rearrange("p (a t) -> p a t", a=2)
                    link(dve.tensor_copy(ckv_pair[:, :, 0, :], v))
                    link(dve.tensor_tensor(ckv_pair[:, :, 1, :], v, ckv_pair[:, :, 0, :].bitcast(F32), ALU.subtract))
                    dve.sem_inc(s("ckv_ready"), 1)
                    dve.sem_inc(s("head_normed"), 1)
                    return
                ins = dve.scalar_tensor_tensor(out=src, in0=src, scalar=params[:, gain:gain + 1], in1=rstd[:, 0:w], op0=ALU.mult, op1=ALU.mult)
                if q == 0:
                    link(ins)
                    ins = dve.tensor_scalar(ikn[:], ikn[:], column("idx_k_ln_b"), None, ALU.add)
                    ins.then_inc(s("ik_ready"), 1)
                    dve.wait_ge(s("ik_ready"), 1)
                    dve.sem_inc(s("head_normed"), 1)
                    return
                ins.then_inc(s("head_normed"), 1)

            def index_steps(name, n):
                first = stages(INDEX_AT[name], n, 0)
                if first == 0:
                    dve.memset(score[:], 0.0).then_inc(s("score_zero"), 1)
                    dve.wait_ge(s("score_zero"), 1)
                for h in () if first is None else (first, first + 1):
                    dve.wait_ge(s("idx_relu"), h + 1)
                    if h:
                        dve.wait_ge(s("idx_added"), 2 * h)
                    for t in range(2):
                        lo, hi = head_cols("A", t)
                        dve.scalar_tensor_tensor(out=score[:, lo:hi], in0=lg[:, h % 2, lo:hi], scalar=iw[:, t, h:h + 1], in1=score[:, lo:hi],
                                                 op0=ALU.mult, op1=ALU.add).then_inc(s("idx_added"), 1)
                if first == IDX_HEADS - 2:
                    dve.wait_ge(s("idx_added"), 2 * IDX_HEADS)
                    dve.sem_inc(s("scored"), 1)

            def topk_steps(n):
                r = TOPK_AT.get(n)
                if r is None:
                    return
                if r == 0:
                    dve.wait_ge(s("score_masked"), 2)
                for t in range(2):
                    lo, hi = head_cols("A", t)
                    src = score if r == 0 else work
                    link(dve.max(top8[:, t, :], src[:, lo:hi]))
                    link(dve.match_replace(work[:, lo:hi], top8[:, t, :], src[:, lo:hi], TAKEN))
                if r == TOPK // 8 - 1:
                    dve.tensor_scalar(work[:], work[:], TAKEN / 2, NEG, ALU.is_gt, ALU.mult).then_inc(s("topk"), 1)

            def value_steps(n):
                v = VALUES_AT.get(n)
                if v is None:
                    return
                dst, c = (v_a, v) if v < 6 else (v_b, 0) if v == 6 else (v_c, v - 7)
                dve.wait_ge(s("values_turned"), v + 1)
                dve.tensor_copy(dst[:, :, c * P:(c + 1) * P], aux[:, 3, 0:T].rearrange("p (t c) -> p t c", t=2)).then_inc(s("values_copied"), 1)

            def head_logits(h):
                kind, c = HEADS[h]
                l, _, w = logits_of(h)
                b = h % 2
                dve.wait_ge(s("qk"), h + 1)
                if h >= 2:
                    dve.wait_ge(s("probs_turned"), h - 1)
                scale = (B_DIM if kind == "B" else P) ** -0.5
                if kind == "A":
                    dve.wait_ge(s("masked"), 2 * h + 2)
                    link(dve.scalar_tensor_tensor(out=l, in0=aux[:, 0, 0:w], scalar=scale, in1=bias_mask[b][:], op0=ALU.mult, op1=ALU.add))
                elif kind == "B":
                    for t in range(2):
                        lo, hi = head_cols(kind, t)
                        link(dve.scalar_tensor_tensor(out=l[:, lo:hi], in0=aux[:, 0, lo:hi], scalar=scale,
                                                      in1=toep[:, A_HEADS + c, T - (hi - lo):T], op0=ALU.mult, op1=ALU.add))
                else:
                    link(dve.tensor_scalar(l, aux[:, 0, 0:w], scale, None, ALU.mult))
                for t in range(2):
                    lo, hi = head_cols(kind, t)
                    link(dve.tensor_reduce(negmax[:, b, t:t + 1], l[:, lo:hi], AX, ALU.max))
                if kind == "B":
                    if c == 0:
                        dve.wait_ge(s("sinks_in"), 16)
                    link(dve.tensor_scalar(negmax[:, b, :], negmax[:, b, :], sinks[:, c:c + 1], None, ALU.max))
                link(dve.tensor_scalar(negmax[:, b, :], negmax[:, b, :], -1.0, None, ALU.mult))
                dve.sem_inc(s("logits"), 1)

            def scale_probs(h):
                kind, c = HEADS[h]
                l, _, _ = logits_of(h)
                b = h % 2
                dve.wait_ge(s("exps"), 2 * h + 2)
                if kind == "B":
                    dve.wait_ge(s("sink_exps"), 2 * c + 2)
                    link(dve.tensor_tensor(denom[:, b, :], denom[:, b, :], esink[:, b, :], ALU.add))
                link(dve.reciprocal(denom[:, b, :], denom[:, b, :]))
                for t in range(2):
                    lo, hi = head_cols(kind, t)
                    link(dve.tensor_scalar(l[:, lo:hi], l[:, lo:hi], denom[:, b, t:t + 1], None, ALU.mult))
                dve.sem_inc(s("probs"), 1)

            def copy_out(h):
                kind, c = HEADS[h]
                dve.wait_ge(s("pv"), h + 1)
                if kind == "A":
                    dst, src = early[:, E_AQ + c, :], aux[:, 3, 0:T]
                elif kind == "C":
                    dst, src = late[:, L_CQ + c, :], aux[:, 3, 0:T]
                else:
                    r = (c % 2) * 64
                    dst, src = late[r:r + 64, L_BQ + c // 2, :], aux[r:r + 64, 3, 0:T]
                dve.tensor_copy(dst, src).then_inc(s("pv_copied"), 1)

            def head_steps(name, n):
                for lag, stage in ((7, copy_out), (2, scale_probs), (0, head_logits)):
                    h = stages(HEAD_AT[name], n, lag)
                    if h is not None:
                        stage(h)

            def split_step(q, r):
                dve.wait_ge(s("gated"), q + 1)
                v = gate[:, q % 2, 0:2 * T].rearrange("p (a t) -> p a t", a=2)
                link(dve.tensor_copy(o_pair[:, 2 * r:2 * r + 2, 0, :], v))
                dve.tensor_tensor(o_pair[:, 2 * r:2 * r + 2, 1, :], v, o_pair[:, 2 * r:2 * r + 2, 0, :].bitcast(F32), ALU.subtract).then_inc(s("o_split"), 1)

            def beside_early(n):
                if n == 0:
                    dve.wait_ge(s("ik_centered"), 1)
                    link(dve.tensor_copy(ikn[:], aux[:, 1, 0:T]))
                    dve.sem_inc(s("ik_copied"), 1)
                    dve.wait_ge(s("iw_turned"), 1)
                    dve.tensor_scalar(iw, aux[:, 2, 0:T].rearrange("p (t c) -> p t c", t=2)[:, :, 64:80],
                                      IDX_HEADS ** -0.5 * IDX_DIM ** -0.5, None, ALU.mult).then_inc(s("iw_ready"), 1)
                    dve.wait_ge(s("iw_ready"), 1)
                norm_steps("early", n)
                index_steps("early", n)

            def beside_late(n):
                index_steps("late", n)
                norm_steps("late", n)
                topk_steps(n)
                value_steps(n)
                head_steps("late", n)
                if 0 <= n - SILU_AT - 1 < 3:
                    split_step(n - SILU_AT - 1, n - SILU_AT - 1)

            splitting("early", fold_into("early", early), beside=beside_early)
            splitting("kv_up", fold_into("kv_up", akv))
            splitting("late", fold_into("late", late), beside=beside_late)

            def gated_product(name, steps0, dst=None, pair=None, ready=None, beside=None):
                job = jobs[name]

                def body(i, u, part):
                    banks, _ = group_done(dve, job, i, u, part)
                    i = i * job.unroll + u
                    n = steps0 + i
                    if part == 0 and n:
                        dve.wait_ge(s("merged_step"), n)
                    done = s("gate_in") if part == 0 else s("up_ready")
                    fold(dve, tmp[:, part, 0:2 * T].rearrange("p (a t) -> p a t", a=2), banks).then_inc(done, 1)
                    dve.wait_ge(done, n + 1)
                    dve.sem_inc(acc_free, 1)
                    if part == 1 and pair is not None:
                        dve.wait_ge(s("merged_step"), n + 1)
                        hi, lo = pair[:, bass.ds(i * 2, 2), 0, :], pair[:, bass.ds(i * 2, 2), 1, :]
                        v = dst[:, bass.ds(i * 2, 2), :]
                        dve.tensor_copy(hi, v).then_inc(s("pair_step"), 1)
                        dve.wait_ge(s("pair_step"), i + 1)
                        dve.tensor_tensor(lo, v, hi.bitcast(F32), ALU.subtract).then_inc(s(ready), 1)
                splitting(name, body, beside=beside)

            def beside_up_c(n):
                if n in (1, 2):
                    split_step(3 + n - 1, n - 1)
                head_steps("w_up_c", n)

            def beside_up_b(n):
                if n in (1, 2, 3):
                    split_step(5 + n - 1, n - 1)

            gated_product("w_up_a", 0, beside=lambda n: head_steps("w_up_a", n))
            gated_product("w_up_c", 8, beside=beside_up_c)
            gated_product("w_up_b", 16, merged, merged_pair, "merged_ready", beside=beside_up_b)

            dve.sem_inc(s("residual"), 2)

            def wo_body(i, u, part):
                banks, _ = group_done(dve, jobs["w_o"], i, u)
                g = 2 * i + u
                dve.wait_ge(s("residual"), g + 1)
                fold(dve, tmp[:, u, 0:2 * T].rearrange("p (a t) -> p a t", a=2), banks).then_inc(s("folded"), 1)
                dve.wait_ge(s("folded"), g + 1)
                dve.sem_inc(acc_free, 1)

            def meta_step(n):
                if n != META_AT:
                    return
                dve.wait_ge(s("meta_turned"), 1)
                link(dve.tensor_copy(h1[:, :, 0:META], aux[:, 1, 0:KT * META].rearrange("p (k t) -> p k t", k=KT)))
                sqm = gate[:, 0, 0:KT * META]
                link(dve.tensor_tensor(sqm.rearrange("p (k t) -> p k t", k=KT), h1[:, :, 0:META], h1[:, :, 0:META], ALU.mult))
                link(dve.memset(sumsq[:, 1, 0:META], 0.0))
                dve.tensor_reduce(sumsq[:, 0, 0:META], sqm.rearrange("p (k t) -> p t k", k=KT), AX, ALU.add).then_inc(s("meta_sums"), 1)
            splitting("w_o", wo_body, beside=meta_step)
            dve.wait_ge(s("residual"), 2 + 8)
            inverse_std(TM, 1.0 / D, EPS)
            normalize(lambda k: h1[:, k, :], uT, TM, "g_pre_mix_2", 16, rstd[:, 0:TM])

            link(dve.memset(glu[:, :, 0:TAPS - 1 - META], 0.0))

            def values_body(i, u, part):
                banks, _ = group_done(dve, jobs["values"], i, u)
                g = 2 * i + u
                link(dve.tensor_copy(glu[:, 2 * g:2 * g + 2, TAPS - 1 - META:], banks[:, :, 0:TM]))
                dve.sem_inc(s("values_moved"), 1)
                dve.sem_inc(acc_free, 1)

            def gates_body(i, u, part):
                dve.wait_ge(s("glu_sig"), 2 * i + u + 1)
                dve.sem_inc(acc_free, 1)

            def pools_body(i, u, part):
                banks, _ = group_done(dve, jobs["pools"], i, u)
                g = POOL_ORDER[2 * i + u]
                link(dve.tensor_copy(z_pool[:, 2 * g:2 * g + 2, :], banks[:, :, 0:TM]))
                dve.sem_inc(s("pooled"), 1)
                dve.sem_inc(acc_free, 1)

            taps_done = [0]

            def conv_taps(count):
                for _ in range(count):
                    n = taps_done[0]
                    if n == DVE_TILES * TAPS:
                        return
                    taps_done[0] += 1
                    tap, k = n // DVE_TILES, n % DVE_TILES
                    w = column("w_dw_2", 8 * tap + k)
                    if tap == 0:
                        ins = dve.tensor_scalar(conv[:, k, :], glu[:, k, 0:T], w, column("b_dw_2", k), ALU.mult, ALU.add)
                    else:
                        dve.wait_ge(s("conv_taps"), n - DVE_TILES + 1)
                        ins = dve.scalar_tensor_tensor(out=conv[:, k, :], in0=glu[:, k, tap:tap + T], scalar=w, in1=conv[:, k, :],
                                                       op0=ALU.mult, op1=ALU.add)
                    ins.then_inc(s("conv_taps"), 1)
                    if n == DVE_TILES * TAPS - 1:
                        dve.wait_ge(s("conv_taps"), DVE_TILES * TAPS)
                        dve.sem_inc(s("conv_done"), 1)

            def taps_beside_pools(n):
                if n == 0:
                    dve.wait_ge(s("glu_done"), 4)
                conv_taps(3)

            def grp_body(i, u, part):
                banks, _ = group_done(dve, jobs["pool_grp"], i, u)
                g = POOL_ORDER[8 * i + u]
                v = tmp[:, 0, 0:2 * T].rearrange("p (a t) -> p a t", a=2)
                link(fold(dve, v, banks))
                dve.sem_inc(acc_free, 1)
                for a in range(2):
                    link(dve.tensor_scalar(v[:, a, :], v[:, a, :], column("pool_scale_2", 2 * g + a), None, ALU.mult))
                link(dve.tensor_copy(y_pair[:, 2 * g:2 * g + 2, 0, :], v))
                dve.tensor_tensor(y_pair[:, 2 * g:2 * g + 2, 1, :], v, y_pair[:, 2 * g:2 * g + 2, 0, :].bitcast(F32), ALU.subtract).then_inc(s("y_split"), 1)
                dve.wait_ge(s("y_split"), 8 * i + u + 1)
                if 8 * i + u == 3:
                    dve.sem_inc(s("y_pair_ready"), 4)

            def layer_norm_steps(n):
                if n < LN_SLAB:
                    conv_taps(2 if n < LN_SLAB - 1 else DVE_TILES * TAPS)
                if n == LN_SLAB + 1:
                    dve.wait_ge(s("conv_sum"), 1)
                    link(dve.tensor_scalar(rstd[:, T:2 * T], aux[:, 1, 0:T], 1.0 / CONV_W, None, ALU.mult))
                    for k in range(8):
                        ins = dve.tensor_tensor(conv[:, k, :], conv[:, k, :], rstd[:, T:2 * T], ALU.subtract)
                        if k % 2 == 0:
                            ins.then_inc(s("center_half"), 1)
                        else:
                            dve.wait_ge(s("center_half"), k // 2 + 1)
                            ins.then_inc(s("conv_centered"), 1)
                if n == LN_SLAB + 6:
                    dve.wait_ge(s("conv_squares"), 4)
                    inverse_std(T, 1.0 / CONV_W, LN_EPS, src=aux[:, 0, 0:T])
                    for k in range(8):
                        ins = dve.tensor_tensor(conv[:, k, :], conv[:, k, :], rstd[:, 0:T], ALU.mult)
                        if k % 2 == 0:
                            ins.then_inc(s("scale_half"), 1)
                        else:
                            dve.wait_ge(s("scale_half"), k // 2 + 1)
                            ins.then_inc(s("conv_scaled"), 1)
                q = n - LN_SLAB - 7
                if 0 <= q < 4:
                    dve.wait_ge(s("conv_sig"), 2 * q + 2)
                    dve.wait_ge(s("conv_affine"), 2 * q + 2)
                    v = conv[:, 2 * q:2 * q + 2, :]
                    dve.tensor_tensor(v, v, square[:, q % 2, 0:2 * T].rearrange("p (a t) -> p a t", a=2), ALU.mult).then_inc(s("conv_used"), 1)
                if 1 <= q < 5:
                    conv_low(q - 1)

            def conv_low(q):
                dve.wait_ge(s("conv_high"), q + 1)
                dve.tensor_tensor(conv_pair[:, 2 * q:2 * q + 2, 1, :], conv[:, 2 * q:2 * q + 2, :], conv_pair[:, 2 * q:2 * q + 2, 0, :].bitcast(F32),
                                  ALU.subtract).then_inc(s("conv_ready"), 1)

            splitting("values", values_body)
            splitting("gates", gates_body)
            splitting("pools", pools_body, beside=taps_beside_pools)
            def gate_b_body(i, u, part):
                banks, _ = group_done(dve, jobs["conv_gates"], i, u)
                g = 2 * i + u
                fold(dve, gate_b[:, bass.ds(2 * g, 2), :], banks).then_inc(acc_free, 1)

            def m_low(g):
                dve.wait_ge(s("m_high"), g + 1)
                dve.tensor_tensor(m_pair[:, 2 * g:2 * g + 2, 1, :], m[:, 2 * g:2 * g + 2, :], m_pair[:, 2 * g:2 * g + 2, 0, :].bitcast(F32),
                                  ALU.subtract).then_inc(s("m_ready"), 1)

            def conv_out_body(i, u, part):
                banks, _ = group_done(dve, jobs["conv_out"], i, u)
                g = 4 * i + u
                if g >= 2:
                    dve.wait_ge(s("merged_step"), 32 + g - 1)
                else:
                    dve.wait_ge(s("merged_step"), 32)
                fold(dve, tmp[:, g % 2, 0:2 * T].rearrange("p (a t) -> p a t", a=2), banks).then_inc(s("up_ready"), 1)
                dve.wait_ge(s("up_ready"), 32 + g + 1)
                dve.sem_inc(acc_free, 1)
                if g >= 1:
                    m_low(g - 1)

            dve.wait_ge(s("d_ready"), 4)
            splitting("conv_gates", gate_b_body, beside=lambda n: conv_taps(3))
            splitting("pool_grp", grp_body)
            gated_product("pool_out", 24, beside=layer_norm_steps)
            splitting("conv_out", conv_out_body)
            m_low(7)

            def mixed_body(i, u, part):
                banks, _ = group_done(dve, jobs["w_o_2"], i, u)
                g = 2 * i + u
                fold(dve, mixed[:, bass.ds(2 * g, 2), :], banks).then_inc(s("mixed"), 1)
                dve.wait_ge(s("mixed"), g + 1)
                dve.sem_inc(acc_free, 1)
            splitting("w_o_2", mixed_body)
            inverse_std(T, 1.0 / D, EPS)
            for r in range(8):
                if r >= 2:
                    dve.wait_ge(s("h2"), r - 1)
                for a in range(2):
                    k = 2 * r + a
                    ins = dve.scalar_tensor_tensor(out=gate[:, r % 2, a * T:(a + 1) * T], in0=mixed[:, k, :], scalar=column("g_post_mix_2", k),
                                                   in1=rstd[:, 0:T], op0=ALU.mult, op1=ALU.mult)
                    if a == 0:
                        ins.then_inc(s("h2_half"), 1)
                    else:
                        dve.wait_ge(s("h2_half"), r + 1)
                        ins.then_inc(s("h2_part"), 1)
                if r >= 2:
                    low_part(u2, T, 24, r - 2)
            low_part(u2, T, 24, 6)
            low_part(u2, T, 24, 7)

            def up_body(q):
                job = jobs[f"w_up{q}"]

                def body(i, u, part):
                    banks, _ = group_done(dve, job, i, u)
                    g = i * job.unroll + u
                    v = tmp[:, u, 0:2 * T].rearrange("p (a t) -> p a t", a=2)
                    link(fold(dve, v, banks))
                    dve.sem_inc(acc_free, 1)
                    f = tmp[:, u, 0:2 * T]
                    link(dve.scalar_tensor_tensor(out=f, in0=f, scalar=0.0, in1=f, op0=ALU.max, op1=ALU.mult))
                    hi, lo = f_pair[:, bass.ds(g * 2, 2), 0, :], f_pair[:, bass.ds(g * 2, 2), 1, :]
                    link(dve.tensor_copy(hi, v))
                    dve.tensor_tensor(lo, v, hi.bitcast(F32), ALU.subtract).then_inc(s("f_ready"), 1)
                return body

            def down_body(q):
                job = jobs[f"w_down{q}"]

                def body(i, u, part):
                    banks, _ = group_done(dve, job, i, u)
                    g = i * job.unroll + u
                    dve.wait_ge(s("down_added"), 8 * q + g + 1)
                    fold(dve, tmp[:, u, 0:2 * T].rearrange("p (a t) -> p a t", a=2), banks).then_inc(s("down"), 1)
                    dve.wait_ge(s("down"), 8 * q + g + 1)
                    dve.sem_inc(acc_free, 1)
                return body
            for q in range(4):
                splitting(f"w_up{q}", up_body(q), 3)
                splitting(f"w_down{q}", down_body(q))
                dve.wait_ge(s("down_added"), 2 + 8 * q + 8)
                if q == 0:
                    dve.wait_ge(s("h2_sums"), 1)
                    link(dve.tensor_scalar(inv_ms, aux[:, 0, 0:2], 1.0 / D, EPS, ALU.mult, ALU.add))
                    link(dve.reciprocal(inv_ms, inv_ms))

            dve.wait_ge(s("out_sums"), 1)
            link(dve.tensor_scalar(out_ms, acc[:, 0, 0:2], 1.0 / D, None, ALU.mult))
            link(dve.tensor_tensor(out_ms, out_ms, inv_ms, ALU.mult))
            link(dve.tensor_tensor(out_ms, out_ms, inv_ms, ALU.mult))
            dve.tensor_scalar(out_ms, out_ms, EPS, None, ALU.add).then_inc(s("out_var"), 1)
            dve.wait_ge(s("out_root"), 1)
            link(dve.reciprocal(out_ms, out_ms))
            link(dve.tensor_tensor(out_scale, out_ms, inv_ms, ALU.mult))
            for e in range(8):
                r, t = e // 2, e % 2
                cols = slice(r * 512, (r + 1) * 512)
                dve.wait_ge(s("out_turned"), e + 1)
                dve.scalar_tensor_tensor(out=rows_out[:, t, cols], in0=aux[:, e % 4, :], scalar=out_scale[:, t:t + 1], in1=rows_h[:, t, cols],
                                         op0=ALU.mult, op1=ALU.add).then_inc(s("rows_ready"), 1)


_NAMES = ["x", "mem", "norm_g", "w_in", "kv_norm_g", "w_kv_up", "idx_k_ln_g", "idx_k_ln_b", "q_norm_a", "k_norm_a",
          "q_norm_b", "k_norm_b", "sinks_b", "mem_norm_g", "w_mem_kv", "q_norm_c", "k_norm_c", "w_up_a", "w_up_b",
          "w_up_c", "gate_bias", "w_o", "rel_bias", "meta_2", "g_pre_mix_2", "w_in_2", "w_pool_grp_2", "pool_scale_2",
          "w_pool_out_2", "w_dw_2", "b_dw_2", "conv_ln_g_2", "conv_ln_b_2", "w_conv_out_2", "w_o_2", "g_post_mix_2",
          "g_pre_mlp_2", "w_up_2", "w_down_2", "g_post_mlp_2"]


def kernel(**inputs):
    import concourse.bacc as bacc
    from concourse.bass_utils import run_bass_kernel_spmd

    nc = bacc.Bacc("TRN2", target_bir_lowering=False, num_devices=1)
    arrays, views = {}, {}
    for name in _NAMES:
        a = np.ascontiguousarray(inputs[name])
        arrays[f"in_{name}"] = a
        views[name] = nc.dram_tensor(f"in_{name}", a.shape, mybir.dt.from_np(a.dtype), kind="ExternalInput").ap()
    out = nc.dram_tensor("out", (1, T, D), F32, kind="ExternalOutput").ap()
    build(nc, views, out)
    return run_bass_kernel_spmd(nc, [arrays], core_ids=[0]).results[0]["out"]
```
